# Optimizing a Trainium2 kernel written in Bass

```python
import jax
import jax.numpy as jnp
from jax import lax
import numpy as np
import jax, jax.numpy as jnp

D_MODEL = 1024
BATCH = 1
SEQ = 512
DEPTH = 1

GRID_W = 64
CTX_LEN = 256
N_MIXERS = 4
EPS = 1e-6
N_MOD = 6

FNET_GROUPS = 4
FNET_GROUP_DIM = D_MODEL // FNET_GROUPS

NA_HEADS = 16
NA_HEAD_DIM = D_MODEL // NA_HEADS
NA_WIN_ROWS = 8
NA_WIN_COLS = 16

SG_CHUNK = 128
SG_GROUPS = 4
SG_DIM = D_MODEL
SG_GROUP_DIM = SG_DIM // SG_GROUPS

ATT_HEADS = 16
ATT_KV_HEADS = 4
ATT_GROUP = ATT_HEADS // ATT_KV_HEADS
ATT_HEAD_DIM = D_MODEL // ATT_HEADS
ATT_Q_BLOCK = 128
ROPE_THETA = 10000.0

FFN_DIM = 2816
FFN_CONV = 3


def _layers_using(m):
    return (DEPTH - m + N_MIXERS - 1) // N_MIXERS

def rms_norm(x, g):
    xf = x.astype(jnp.float32)
    y = xf * lax.rsqrt(jnp.mean(xf * xf, axis=-1, keepdims=True) + EPS)
    return (y * g.astype(jnp.float32)).astype(x.dtype)

def modulate(h, g, shift, scale):
    return rms_norm(h, g) * (1 + scale) + shift

def ada_params(cond, w_mod, b_mod):
    m = jax.nn.silu(cond) @ w_mod + b_mod
    return jnp.split(m[:, None, :], N_MOD, axis=-1)

def depthwise_conv_seq(h, w, b):
    pad = FFN_CONV // 2
    y = lax.conv_general_dilated(h, w[:, None, :].astype(h.dtype), window_strides=(1,),
                                 padding=((pad, FFN_CONV - 1 - pad),),
                                 dimension_numbers=("NWC", "WIO", "NWC"),
                                 feature_group_count=h.shape[-1])
    return y + b

def conv_ffn(h, w_up, w_conv, b_conv, w_down):
    g, v = jnp.split(h @ w_up, 2, axis=-1)
    g = depthwise_conv_seq(g, w_conv, b_conv)
    return (jax.nn.silu(g) * v) @ w_down

def fourier_mix(a, w_out):
    B, L, D = a.shape
    ag = a.reshape(B, L, FNET_GROUPS, FNET_GROUP_DIM).astype(jnp.float32)
    f = jnp.fft.fft2(ag, axes=(1, 3), norm="ortho").real
    return f.astype(a.dtype).reshape(B, L, D) @ w_out

def spatial_gating_mix(a, w_in, g_v, w_s, b_s, w_out):
    B, L, _ = a.shape
    z = jax.nn.gelu(a @ w_in)
    u, v = jnp.split(z, 2, axis=-1)
    v = rms_norm(v, g_v)
    n = L // SG_CHUNK
    vg = v.reshape(B, n, SG_CHUNK, SG_GROUPS, SG_GROUP_DIM)
    mixed = jnp.einsum("gpq,bnqgc->bnpgc", w_s, vg) + b_s.T[None, None, :, :, None]
    return (u * mixed.reshape(B, L, SG_DIM)) @ w_out

def axial_rope(L):
    t = jnp.arange(L)
    row = (t // GRID_W).astype(jnp.float32)
    col = (t % GRID_W).astype(jnp.float32)
    n_freq = ATT_HEAD_DIM // 4
    inv_freq = ROPE_THETA ** (-jnp.arange(n_freq, dtype=jnp.float32) / n_freq)
    ang = jnp.concatenate([row[:, None] * inv_freq, col[:, None] * inv_freq], axis=-1)
    return jnp.cos(ang), jnp.sin(ang)

def apply_rope(x, cos, sin):
    xf = x.astype(jnp.float32)
    x1, x2 = jnp.split(xf, 2, axis=-1)
    c = cos[None, :, None, :]
    s = sin[None, :, None, :]
    return jnp.concatenate([x1 * c - x2 * s, x1 * s + x2 * c], axis=-1).astype(x.dtype)

def _gqa_attend(q, k, v):
    s = jnp.einsum("bqkgd,bskd->bkgqs", q, k).astype(jnp.float32) * (ATT_HEAD_DIM ** -0.5)
    p = jax.nn.softmax(s, axis=-1).astype(v.dtype)
    return jnp.einsum("bkgqs,bskd->bqkgd", p, v)

def gqa_mix(a_lat, a_ctx, w_qkv, g_q, g_k, w_out, need_ctx_out):
    B, L, _ = a_lat.shape
    H, KV, G, Dh = ATT_HEADS, ATT_KV_HEADS, ATT_GROUP, ATT_HEAD_DIM
    q, k, v = jnp.split(a_lat @ w_qkv, [H * Dh, (H + KV) * Dh], axis=-1)
    q = rms_norm(q.reshape(B, L, H, Dh), g_q)
    k = rms_norm(k.reshape(B, L, KV, Dh), g_k)
    v = v.reshape(B, L, KV, Dh)
    cos, sin = axial_rope(L)
    q = apply_rope(q, cos, sin)
    k = apply_rope(k, cos, sin)
    n_ctx = a_ctx.shape[1]
    kc, vc = jnp.split(a_ctx @ w_qkv[:, H * Dh:], 2, axis=-1)
    kc = rms_norm(kc.reshape(B, n_ctx, KV, Dh), g_k)
    vc = vc.reshape(B, n_ctx, KV, Dh)
    k_all = jnp.concatenate([k, kc], axis=1)
    v_all = jnp.concatenate([v, vc], axis=1)
    nblk = L // ATT_Q_BLOCK
    q_blocks = q.reshape(B, nblk, ATT_Q_BLOCK, KV, G, Dh).swapaxes(0, 1)
    o = lax.map(lambda qb: _gqa_attend(qb, k_all, v_all), q_blocks)
    y_lat = o.swapaxes(0, 1).reshape(B, L, H * Dh) @ w_out
    y_ctx = None
    if need_ctx_out:
        qc = rms_norm((a_ctx @ w_qkv[:, :H * Dh]).reshape(B, n_ctx, H, Dh), g_q)
        oc = _gqa_attend(qc.reshape(B, n_ctx, KV, G, Dh), kc, vc)
        y_ctx = oc.reshape(B, n_ctx, H * Dh) @ w_out
    return y_lat, y_ctx

def neighbourhood_mix(a_lat, a_ctx, w_qkv, rpb, w_out, need_ctx_out):
    B, L, D = a_lat.shape
    H, Dh = NA_HEADS, NA_HEAD_DIM
    rows = L // GRID_W
    kh = min(NA_WIN_ROWS, rows)
    kw = NA_WIN_COLS
    scale = Dh ** -0.5
    q, k, v = jnp.split(a_lat @ w_qkv, 3, axis=-1)
    n_ctx = a_ctx.shape[1]
    kc, vc = jnp.split(a_ctx @ w_qkv[:, D:], 2, axis=-1)
    kc = kc.reshape(B, n_ctx, H, Dh)
    vc = vc.reshape(B, n_ctx, H, Dh)
    k_grid = k.reshape(B, rows, GRID_W, H, Dh)
    v_grid = v.reshape(B, rows, GRID_W, H, Dh)
    col = jnp.arange(GRID_W)
    col_start = jnp.clip(col - kw // 2, 0, GRID_W - kw)
    col_idx = col_start[:, None] + jnp.arange(kw)[None, :]
    col_off = col_idx - col[:, None] + (NA_WIN_COLS - 1)
    q_rows = q.reshape(B, rows, GRID_W, H, Dh).swapaxes(0, 1)

    def row_block(args):
        r, q_r = args
        r_start = jnp.clip(r - kh // 2, 0, rows - kh)
        k_r = lax.dynamic_slice_in_dim(k_grid, r_start, kh, axis=1)[:, :, col_idx]
        v_r = lax.dynamic_slice_in_dim(v_grid, r_start, kh, axis=1)[:, :, col_idx]
        row_off = r_start + jnp.arange(kh) - r + (NA_WIN_ROWS - 1)
        bias = rpb[:, row_off[:, None, None], col_off[None, :, :]].astype(jnp.float32)
        s_nb = jnp.einsum("bwhd,bawjhd->bhwaj", q_r, k_r).astype(jnp.float32) * scale
        s_nb = (s_nb + bias.transpose(0, 2, 1, 3)[None]).reshape(B, H, GRID_W, kh * kw)
        s_ctx = jnp.einsum("bwhd,bchd->bhwc", q_r, kc).astype(jnp.float32) * scale
        p = jax.nn.softmax(jnp.concatenate([s_nb, s_ctx], axis=-1), axis=-1).astype(q_r.dtype)
        p_nb = p[..., :kh * kw].reshape(B, H, GRID_W, kh, kw)
        p_ctx = p[..., kh * kw:]
        return (jnp.einsum("bhwaj,bawjhd->bwhd", p_nb, v_r)
                + jnp.einsum("bhwc,bchd->bwhd", p_ctx, vc))

    o = lax.map(row_block, (jnp.arange(rows), q_rows))
    y_lat = o.swapaxes(0, 1).reshape(B, L, D) @ w_out
    y_ctx = None
    if need_ctx_out:
        qc = (a_ctx @ w_qkv[:, :D]).reshape(B, n_ctx, H, Dh)
        s = jnp.einsum("bqhd,bkhd->bhqk", qc, kc).astype(jnp.float32) * scale
        p = jax.nn.softmax(s, axis=-1).astype(vc.dtype)
        y_ctx = jnp.einsum("bhqk,bkhd->bqhd", p, vc).reshape(B, n_ctx, D) @ w_out
    return y_lat, y_ctx

def _normal(k, shape, scale):
    return jax.random.normal(k, shape, jnp.float32) * scale

def first_inputs(seed: int = 0) -> dict:
    key = jax.random.key(seed)
    ks = iter(jax.random.split(key, 32))
    D = D_MODEL
    inv = D ** -0.5
    n_a, n_b, n_c, n_d = (_layers_using(m) for m in range(N_MIXERS))
    qkv_dim = (ATT_HEADS + 2 * ATT_KV_HEADS) * ATT_HEAD_DIM
    return {
        "x": _normal(next(ks), (BATCH, SEQ, D), 1.0),
        "c": _normal(next(ks), (BATCH, D), 1.0),
        "ctx": _normal(next(ks), (BATCH, CTX_LEN, D), 1.0),
        "c_ctx": _normal(next(ks), (D,), 1.0),
        "w_mod": _normal(next(ks), (DEPTH, D, N_MOD * D), 0.5 * inv),
        "b_mod": _normal(next(ks), (DEPTH, N_MOD * D), 0.01),
        "g_norm_mix": 1.0 + _normal(next(ks), (DEPTH, D), 0.02),
        "g_norm_ffn": 1.0 + _normal(next(ks), (DEPTH, D), 0.02),
        "w_ffn_up": _normal(next(ks), (DEPTH, D, 2 * FFN_DIM), inv),
        "w_ffn_conv": _normal(next(ks), (DEPTH, FFN_CONV, FFN_DIM), FFN_CONV ** -0.5),
        "b_ffn_conv": _normal(next(ks), (DEPTH, FFN_DIM), 0.01),
        "w_ffn_down": _normal(next(ks), (DEPTH, FFN_DIM, D), FFN_DIM ** -0.5),
        "w_fnet_out": _normal(next(ks), (n_a, D, D), inv),
        "w_na_qkv": _normal(next(ks), (n_b, D, 3 * D), inv),
        "na_rel_bias": _normal(next(ks), (n_b, NA_HEADS, 2 * NA_WIN_ROWS - 1, 2 * NA_WIN_COLS - 1), 0.1),
        "w_na_out": _normal(next(ks), (n_b, D, D), inv),
        "w_sg_in": _normal(next(ks), (n_c, D, 2 * SG_DIM), inv),
        "g_sg_v": 1.0 + _normal(next(ks), (n_c, SG_DIM), 0.02),
        "w_sg_spatial": _normal(next(ks), (n_c, SG_GROUPS, SG_CHUNK, SG_CHUNK), SG_CHUNK ** -0.5),
        "b_sg_spatial": 1.0 + _normal(next(ks), (n_c, SG_GROUPS, SG_CHUNK), 0.01),
        "w_sg_out": _normal(next(ks), (n_c, SG_DIM, D), SG_DIM ** -0.5),
        "w_att_qkv": _normal(next(ks), (n_d, D, qkv_dim), inv),
        "g_att_q": 1.0 + _normal(next(ks), (n_d, ATT_HEAD_DIM), 0.02),
        "g_att_k": 1.0 + _normal(next(ks), (n_d, ATT_HEAD_DIM), 0.02),
        "w_att_out": _normal(next(ks), (n_d, ATT_HEADS * ATT_HEAD_DIM, D), (ATT_HEADS * ATT_HEAD_DIM) ** -0.5),
        "g_final": 1.0 + _normal(next(ks), (D,), 0.02),
    }

def first_block(x, c, ctx, c_ctx, w_mod, b_mod, g_norm_mix, g_norm_ffn, w_ffn_up, w_ffn_conv, b_ffn_conv,
              w_ffn_down, w_fnet_out, w_na_qkv, na_rel_bias, w_na_out, w_sg_in, g_sg_v, w_sg_spatial,
              b_sg_spatial, w_sg_out, w_att_qkv, g_att_q, g_att_k, w_att_out, g_final):
    h_lat, h_ctx = x, ctx
    for i in range(DEPTH):
        m, j = i % N_MIXERS, i // N_MIXERS
        last = i == DEPTH - 1
        ctx_in_needed = (not last) or m in (1, 3)
        sh1, sc1, gt1, sh2, sc2, gt2 = ada_params(c, w_mod[i], b_mod[i])
        a_lat = modulate(h_lat, g_norm_mix[i], sh1, sc1)
        if ctx_in_needed:
            csh1, csc1, cgt1, csh2, csc2, cgt2 = ada_params(c_ctx[None, :], w_mod[i], b_mod[i])
            a_ctx = modulate(h_ctx, g_norm_mix[i], csh1, csc1)
        if m == 0:
            y_lat = fourier_mix(a_lat, w_fnet_out[j])
            y_ctx = None if last else fourier_mix(a_ctx, w_fnet_out[j])
        elif m == 1:
            y_lat, y_ctx = neighbourhood_mix(a_lat, a_ctx, w_na_qkv[j], na_rel_bias[j], w_na_out[j], not last)
        elif m == 2:
            y_lat = spatial_gating_mix(a_lat, w_sg_in[j], g_sg_v[j], w_sg_spatial[j], b_sg_spatial[j], w_sg_out[j])
            y_ctx = None if last else spatial_gating_mix(a_ctx, w_sg_in[j], g_sg_v[j], w_sg_spatial[j],
                                                         b_sg_spatial[j], w_sg_out[j])
        else:
            y_lat, y_ctx = gqa_mix(a_lat, a_ctx, w_att_qkv[j], g_att_q[j], g_att_k[j], w_att_out[j], not last)
        h_lat = h_lat + gt1 * y_lat
        h_lat = h_lat + gt2 * conv_ffn(modulate(h_lat, g_norm_ffn[i], sh2, sc2),
                                       w_ffn_up[i], w_ffn_conv[i], b_ffn_conv[i], w_ffn_down[i])
        if not last:
            h_ctx = h_ctx + cgt1 * y_ctx
            h_ctx = h_ctx + cgt2 * conv_ffn(modulate(h_ctx, g_norm_ffn[i], csh2, csc2),
                                           w_ffn_up[i], w_ffn_conv[i], b_ffn_conv[i], w_ffn_down[i])
    return rms_norm(h_lat, g_final)


MIX_WIDTH = D_MODEL
RWKV_WIDTH = MIX_WIDTH // 2
POOL_WIDTH = MIX_WIDTH - RWKV_WIDTH
HEAD_SIZE = 64
N_HEADS = RWKV_WIDTH // HEAD_SIZE
D_DECAY_LORA = max(32, int(round(1.8 * RWKV_WIDTH ** 0.5 / 32)) * 32)
D_AAA_LORA = max(32, int(round(1.8 * RWKV_WIDTH ** 0.5 / 32)) * 32)
D_GATE_LORA = max(32, int(round(0.6 * RWKV_WIDTH ** 0.8 / 32)) * 32)
POOL_WINDOWS = (2, 4, 8, 16)
N_POOL_GROUPS = len(POOL_WINDOWS)
POOL_GROUP = POOL_WIDTH // N_POOL_GROUPS
D_FF = 256 * ((8 * D_MODEL // 3 + 255) // 256)
SPLIT_SIZES = (RWKV_WIDTH, RWKV_WIDTH, RWKV_WIDTH, D_DECAY_LORA, D_AAA_LORA, D_GATE_LORA, POOL_WIDTH)
RWKV_COLS = sum(SPLIT_SIZES[:6])
IN_COLS = sum(SPLIT_SIZES)
RMS_EPS = 1e-6
GN_EPS = 64e-5
L2_EPS = 1e-12


def rms_norm_2(x, g):
    xf = x.astype(jnp.float32)
    y = xf * lax.rsqrt(jnp.mean(xf * xf, axis=-1, keepdims=True) + RMS_EPS)
    return (y * g).astype(x.dtype)

def swiglu(x, w_gate, w_up, w_down):
    return (jax.nn.silu(x @ w_gate) * (x @ w_up)) @ w_down

def token_shift(p):
    return jnp.pad(p, ((0, 0), (1, 0), (0, 0)))[:, :-1]

def rwkv7_time_mix(p_r, p_k, p_v, p_w, p_a, p_g, w0, w_lora_up, a0, a_lora_up, g_lora_up,
                   k_k, k_a, r_k, ln_w, ln_b):
    B, S, _ = p_r.shape
    f32 = jnp.float32
    log_w = -jax.nn.softplus(-(w0 + jnp.tanh(p_w) @ w_lora_up).astype(f32)) - 0.5
    decay = jnp.exp(-jnp.exp(log_w))
    a = jax.nn.sigmoid((a0 + p_a @ a_lora_up).astype(f32))
    g = jax.nn.sigmoid(p_g) @ g_lora_up

    def heads(t):
        return t.reshape(B, S, N_HEADS, HEAD_SIZE).astype(f32)

    kk = heads(p_k * k_k)
    kk = kk / jnp.maximum(jnp.sqrt(jnp.sum(kk * kk, axis=-1, keepdims=True)), L2_EPS)
    k = heads(p_k * (1.0 + (a - 1.0) * k_a))
    r, v = heads(p_r), heads(p_v)
    w_h, a_h = heads(decay), heads(a)

    def step(state, inp):
        r_t, w_t, k_t, v_t, kk_t, a_t = inp
        sa = jnp.einsum('bhvk,bhk->bhv', state, -kk_t)
        state = (state * w_t[:, :, None, :]
                 + sa[..., None] * (kk_t * a_t)[:, :, None, :]
                 + v_t[..., None] * k_t[:, :, None, :])
        return state, jnp.einsum('bhvk,bhk->bhv', state, r_t)

    seq_major = lambda t: jnp.moveaxis(t, 1, 0)
    state0 = jnp.zeros((B, N_HEADS, HEAD_SIZE, HEAD_SIZE), f32)
    _, y = lax.scan(step, state0, (seq_major(r), seq_major(w_h), seq_major(k),
                                   seq_major(v), seq_major(kk), seq_major(a_h)))
    y = jnp.moveaxis(y, 0, 1)
    mean = jnp.mean(y, axis=-1, keepdims=True)
    var = jnp.mean(jnp.square(y - mean), axis=-1, keepdims=True)
    y = ((y - mean) * lax.rsqrt(var + GN_EPS)).reshape(B, S, RWKV_WIDTH) * ln_w + ln_b
    bonus = jnp.sum(r * k * r_k, axis=-1, keepdims=True) * v
    y = y + bonus.reshape(B, S, RWKV_WIDTH)
    return (y * g).astype(p_r.dtype)

def multiscale_pool_mix(p, w_pool, pool_scale):
    B, S, _ = p.shape
    f32 = jnp.float32
    pg = p.reshape(B, S, N_POOL_GROUPS, POOL_GROUP).astype(f32)
    cs = jnp.pad(jnp.cumsum(pg, axis=1), ((0, 0), (1, 0), (0, 0), (0, 0)))
    t1 = jnp.arange(1, S + 1)
    outs = []
    for gi, win in enumerate(POOL_WINDOWS):
        csg = cs[:, :, gi]
        lo = jnp.maximum(t1 - win, 0)
        window_sum = csg[:, 1:] - jnp.take(csg, lo, axis=1)
        count = jnp.minimum(t1, win).astype(f32)[None, :, None]
        outs.append(window_sum / count - pg[:, :, gi])
    pooled = jnp.stack(outs, axis=2)
    mixed = jnp.einsum('bsgc,gcd->bsgd', pooled, w_pool.astype(f32))
    return (mixed.reshape(B, S, POOL_WIDTH) * pool_scale).astype(p.dtype)

def second_inputs(seed: int = 0) -> dict:
    key = jax.random.key(seed)
    ks = jax.random.split(key, 32)
    L = DEPTH
    f32 = jnp.float32

    def nrm(k, shape, scale):
        return jax.random.normal(k, shape, f32) * scale

    return {
        "x": nrm(ks[0], (BATCH, SEQ, D_MODEL), 1.0),
        "ffn1_norm": 1.0 + nrm(ks[1], (L, D_MODEL), 0.1),
        "ffn1_w_gate": nrm(ks[2], (L, D_MODEL, D_FF), D_MODEL ** -0.5),
        "ffn1_w_up": nrm(ks[3], (L, D_MODEL, D_FF), D_MODEL ** -0.5),
        "ffn1_w_down": nrm(ks[4], (L, D_FF, D_MODEL), D_FF ** -0.5),
        "mix_norm": 1.0 + nrm(ks[5], (L, D_MODEL), 0.1),
        "w_in": nrm(ks[6], (L, D_MODEL, IN_COLS), D_MODEL ** -0.5),
        "mu_shift": jax.random.uniform(ks[7], (L, RWKV_COLS), f32),
        "w0": jax.random.uniform(ks[8], (L, RWKV_WIDTH), f32, -6.0, -1.0),
        "w_lora_up": nrm(ks[9], (L, D_DECAY_LORA, RWKV_WIDTH), 0.5 * D_DECAY_LORA ** -0.5),
        "a0": nrm(ks[10], (L, RWKV_WIDTH), 0.1),
        "a_lora_up": nrm(ks[11], (L, D_AAA_LORA, RWKV_WIDTH), D_AAA_LORA ** -0.5),
        "g_lora_up": nrm(ks[12], (L, D_GATE_LORA, RWKV_WIDTH), D_GATE_LORA ** -0.5),
        "k_k": 0.85 + nrm(ks[13], (L, RWKV_WIDTH), 0.1),
        "k_a": 1.0 + nrm(ks[14], (L, RWKV_WIDTH), 0.1),
        "r_k": nrm(ks[15], (L, N_HEADS, HEAD_SIZE), 0.1),
        "ln_w": 1.0 + nrm(ks[16], (L, RWKV_WIDTH), 0.1),
        "ln_b": nrm(ks[17], (L, RWKV_WIDTH), 0.02),
        "w_pool": nrm(ks[18], (L, N_POOL_GROUPS, POOL_GROUP, POOL_GROUP), POOL_GROUP ** -0.5),
        "pool_scale": 1.0 + nrm(ks[19], (L, POOL_WIDTH), 0.1),
        "w_out": nrm(ks[20], (L, MIX_WIDTH, D_MODEL), MIX_WIDTH ** -0.5),
        "ffn2_norm": 1.0 + nrm(ks[21], (L, D_MODEL), 0.1),
        "ffn2_w_gate": nrm(ks[22], (L, D_MODEL, D_FF), D_MODEL ** -0.5),
        "ffn2_w_up": nrm(ks[23], (L, D_MODEL, D_FF), D_MODEL ** -0.5),
        "ffn2_w_down": nrm(ks[24], (L, D_FF, D_MODEL), D_FF ** -0.5),
        "final_norm": 1.0 + nrm(ks[25], (D_MODEL,), 0.1),
    }

def second_block(x, ffn1_norm, ffn1_w_gate, ffn1_w_up, ffn1_w_down, mix_norm, w_in, mu_shift,
              w0, w_lora_up, a0, a_lora_up, g_lora_up, k_k, k_a, r_k, ln_w, ln_b,
              w_pool, pool_scale, w_out, ffn2_norm, ffn2_w_gate, ffn2_w_up, ffn2_w_down,
              final_norm):
    split_points = np.cumsum(SPLIT_SIZES[:5]).tolist()
    for l in range(DEPTH):
        x = x + 0.5 * swiglu(rms_norm_2(x, ffn1_norm[l]), ffn1_w_gate[l], ffn1_w_up[l], ffn1_w_down[l])

        h = rms_norm_2(x, mix_norm[l])
        p = h @ w_in[l]
        p_rw, p_pool = p[..., :RWKV_COLS], p[..., RWKV_COLS:]
        p_rw = p_rw + (token_shift(p_rw) - p_rw) * mu_shift[l]
        p_r, p_k, p_v, p_w, p_a, p_g = jnp.split(p_rw, split_points, axis=-1)
        y_rw = rwkv7_time_mix(p_r, p_k, p_v, p_w, p_a, p_g, w0[l], w_lora_up[l], a0[l],
                              a_lora_up[l], g_lora_up[l], k_k[l], k_a[l], r_k[l],
                              ln_w[l], ln_b[l])
        y_pool = multiscale_pool_mix(p_pool, w_pool[l], pool_scale[l])
        x = x + jnp.concatenate([y_rw, y_pool], axis=-1) @ w_out[l]

        x = x + 0.5 * swiglu(rms_norm_2(x, ffn2_norm[l]), ffn2_w_gate[l], ffn2_w_up[l], ffn2_w_down[l])
    return rms_norm_2(x, final_norm)


def setup_inputs(seed=0):
    out = dict(first_inputs(seed))
    for name, value in second_inputs(seed + 1).items():
        if name != "x":
            out[name + "_2"] = value
    return out


def reference(
    x, c, ctx, c_ctx, w_mod, b_mod, g_norm_mix, g_norm_ffn, w_ffn_up, w_ffn_conv, b_ffn_conv,
    w_ffn_down, w_fnet_out, w_na_qkv, na_rel_bias, w_na_out, w_sg_in, g_sg_v, w_sg_spatial,
    b_sg_spatial, w_sg_out, w_att_qkv, g_att_q, g_att_k, w_att_out, g_final, ffn1_norm_2,
    ffn1_w_gate_2, ffn1_w_up_2, ffn1_w_down_2, mix_norm_2, w_in_2, mu_shift_2, w0_2,
    w_lora_up_2, a0_2, a_lora_up_2, g_lora_up_2, k_k_2, k_a_2, r_k_2, ln_w_2, ln_b_2, w_pool_2,
    pool_scale_2, w_out_2, ffn2_norm_2, ffn2_w_gate_2, ffn2_w_up_2, ffn2_w_down_2, final_norm_2,
):
    x = first_block(
        x, c, ctx, c_ctx, w_mod, b_mod, g_norm_mix, g_norm_ffn, w_ffn_up, w_ffn_conv,
        b_ffn_conv, w_ffn_down, w_fnet_out, w_na_qkv, na_rel_bias, w_na_out, w_sg_in, g_sg_v,
        w_sg_spatial, b_sg_spatial, w_sg_out, w_att_qkv, g_att_q, g_att_k, w_att_out, g_final,
    )
    return second_block(
        x, ffn1_norm_2, ffn1_w_gate_2, ffn1_w_up_2, ffn1_w_down_2, mix_norm_2, w_in_2,
        mu_shift_2, w0_2, w_lora_up_2, a0_2, a_lora_up_2, g_lora_up_2, k_k_2, k_a_2, r_k_2,
        ln_w_2, ln_b_2, w_pool_2, pool_scale_2, w_out_2, ffn2_norm_2, ffn2_w_gate_2,
        ffn2_w_up_2, ffn2_w_down_2, final_norm_2,
    )


_drawn_inputs = setup_inputs


def setup_inputs(seed=0):
    import zlib

    import numpy as np

    out = dict(_drawn_inputs(seed))
    spreads = {}
    factors = {'b_mod': 4.217,
     'g_norm_mix': 8.0,
     'g_norm_ffn': 7.515,
     'b_ffn_conv': 38.191,
     'w_lora_up_2': 7.835,
     'a0_2': 4.908,
     'ln_b_2': 8.0,
     'k_k_2': 3.08}
    for name, (base, spread) in spreads.items():
        noise = np.random.default_rng([zlib.crc32(name.encode()), seed]).standard_normal(out[name].shape)
        drawn = base * np.exp(spread * noise) if base else spread * noise
        out[name] = jnp.asarray(drawn.astype(out[name].dtype))
    for name, factor in factors.items():
        out[name] = (out[name] * factor).astype(out[name].dtype)
    return out
```

```python
from contextlib import ExitStack

import numpy as np
import concourse.bass as bass
from concourse import mybir

P = 128
T = 512
D = 1024
KT = D // P
F = 2816
FT = F // P
TT_ = T // P
FG = 256
NCOS = T // 2 + 2
NSIN = T // 2
NF = NCOS + NSIN
RW = 512
HS = 64
PAIRS = RW // P
CH = 64
NCH = T // CH
NCP = NCH // 2
EPS = 1e-6
GN_EPS = 64e-5
L2_EPS = 1e-12
KAPPA = float(np.exp(-0.5))
WINDOWS = (2, 4, 8, 16)
PADW = 16
LEVELS = (1, 2, 4, 8, 16, 32)

IN_STARTS_RW = [1536, 1600] + [s + P * p for p in range(PAIRS) for s in (512, 0, 1024)]
IN_STARTS = IN_STARTS_RW + [1696 + P * g for g in range(len(WINDOWS))]
U_DFT = 0
U_FNET = 1
U_UP0 = U_FNET + KT
U_DN0 = U_UP0 + 2 * FT
U_UP1 = U_DN0 + FT
U_DN1 = U_UP1 + 2 * FT
U_IN = U_DN1 + FT
U_OUT = U_IN + len(IN_STARTS)
U_UP2 = U_OUT + KT
U_DN2 = U_UP2 + 2 * FT
NU = U_DN2 + FT
RING = 4
AHEAD = 3

VEC = {}
NVEC = 0
for _name, _n in (("c", KT), ("b_mod", 6 * KT), ("g_mix", KT), ("g_ffn", KT), ("conv", 3 * FT), ("b_conv", FT),
                  ("g_ffn1", KT), ("g_in", KT), ("mu", len(IN_STARTS_RW)), ("w0", PAIRS), ("a0", PAIRS),
                  ("k_k", PAIRS), ("k_a", PAIRS), ("r_k", PAIRS), ("ln_w", PAIRS), ("ln_b", PAIRS),
                  ("pool_scale", len(WINDOWS)), ("g_ffn2", KT), ("g_mid", KT), ("g_last", KT), ("eps", 1), ("gn_eps", 1)):
    VEC[_name] = NVEC
    NVEC += _n
NCONST = 3 * P + len(WINDOWS) * PADW
NMASK = 4 * P + len(LEVELS) * P + P

PE_STEPS = (["tA", "tB", "tK", "tV"] + [f"L{i}" for i in range(NCP)] + [f"K{i}" for i in range(NCP)] + ["t1a", "t1b"]
            + [s for n in range(2, 7) for s in ([f"U{n}a", f"U{n}b", f"D{n}a", f"D{n}b"] + ([f"t{n}a", f"t{n}b"] if n < 6 else []))]
            + ["AV", "GHa", "GHb", "RP", "OV", "MTa", "MTb", "Na", "Nb"] + [f"S{c}" for c in range(1, NCH - 1)]
            + ["Y", "mean", "var"])
VE_STEPS = (["zero", "tB", "tV"] + [f"L{i}" for i in range(NCP)] + [f"K{i}" for i in range(NCP)] + ["D1a", "D1b", "X2", "t1b"]
            + [s for n in range(2, 7) for s in ([f"D{n}a", f"D{n}b"] + ([f"X{n + 1}", f"t{n}b"] if n < 6 else []))]
            + ["GHb", "RP", "MTa", "MTb", "Na", "Nb"] + [f"S{c}" for c in range(1, NCH - 1)]
            + ["Y", "yc", "yn", "out"])
AC_STEPS = (["planes", "tA", "tK", "t1a"] + [s for n in range(2, 7) for s in ([f"U{n}a", f"U{n}b"] + ([f"t{n}a"] if n < 6 else []))]
            + ["AV", "GHa", "OV", "sq", "sd", "affine"])


def at(steps, pair, name):
    return pair * len(steps) + steps.index(name) + 1


def build(nc, a_vec, a_const, a_mask, a_x, a_xt, a_cs, a_wmod, a_w, a_lora, a_pool, out):
    f32, f32r = mybir.dt.float32, mybir.dt.float32r
    ACT = mybir.ActivationFunctionType
    ALU = mybir.AluOpType
    MUL, ADD, SUB, MAX = ALU.mult, ALU.add, ALU.subtract, ALU.max

    with ExitStack() as ctx:
        lo_edge = (nc.sbuf_base + 63) // 64 * 64
        place = [lo_edge]

        def reserve(n_floats):
            o = place[0]
            place[0] += (4 * n_floats + 31) // 32 * 32
            return o

        def view(name, shape, offset, dt=f32):
            return nc.alloc_sbuf_tensor_at(name, shape, dt, offset=offset)

        def fresh(name, shape, dt=f32):
            return view(name, shape, reserve(int(np.prod(shape[1:]))), dt)

        raw = fresh("raw", [P, RING, D])
        w_hi = fresh("w_hi", [P, RING, D], f32r)
        w_lo = fresh("w_lo", [P, RING, D], f32r)
        xT = fresh("xT", [P, KT, T])
        o_act = reserve(2 * KT * T)
        act_hi = view("act_hi", [P, KT, T], o_act, f32r)
        act_lo = view("act_lo", [P, KT, T], o_act + 4 * KT * T, f32r)
        o_hid = reserve(2 * FT * T)
        hid_hi = view("hid_hi", [P, FT * T], o_hid, f32r)
        hid_lo = view("hid_lo", [P, FT * T], o_hid + 4 * FT * T, f32r)
        o_misc = reserve(3 * D)
        o_acc = reserve(D)
        sumsq = fresh("sumsq", [P, T])
        rstd = fresh("rstd", [P, T])
        vec = fresh("vec", [P, NVEC])
        const = fresh("const", [P, NCONST])
        mods = fresh("mods", [P, 6 * KT])
        small = fresh("small", [P, 64])
        assert place[0] <= nc.sbuf_usable_end, (place[0], nc.sbuf_usable_end)

        ident, ones, bones = const[:, 0:P], const[:, P:2 * P], const[:, 2 * P:3 * P]
        inv_count = const[:, 3 * P:]
        c_silu, gain, sh_dc = small[:, 0:8], small[:, 8:16], small[:, 16:24]
        x_ss, gain2, one_minus_ka, g_both = small[:, 24:28], small[:, 28:36], small[:, 36:40], small[:, 40:48]

        def v(name, i=0, n=1):
            return vec[:, VEC[name] + i:VEC[name] + i + n]

        def mod(which, m):
            return mods[:, which * KT + m:which * KT + m + 1]

        SH1, SC1, GT1, SH2, SC2, GT2 = range(6)

        x_tok = view("x_tok", [P, TT_, D], o_act)
        cs_raw = view("cs_raw", [P, TT_, NF], o_act + 4 * TT_ * D)
        y_raw = view("y_raw", [P, KT, NF], o_act)
        xn_hi, xn_lo = hid_hi[:, 0:TT_ * D], hid_lo[:, 0:TT_ * D]
        cs_hi, cs_lo = (h[:, TT_ * D:TT_ * (D + NF)] for h in (hid_hi, hid_lo))
        y_hi, y_lo = (h[:, TT_ * (D + NF):TT_ * (D + NF) + KT * NF] for h in (hid_hi, hid_lo))
        f_buf = view("f_buf", [P, 2, T], o_hid)
        q_buf = view("q_buf", [P, 2, NSIN], o_hid + 4 * 2 * T)
        sq_buf = view("sq_buf", [P, KT, T], o_hid)
        sq_mid = view("sq_mid", [P, KT, T], o_hid + 4 * KT * T)
        wm_ring = view("wm_ring", [P, 3, D], o_misc)
        mod_acc = view("mod_acc", [P, D], o_acc)
        junk = view("junk", [P, D], o_hid + 4 * FT * T + 4 * TT_ * (D + NF))

        g_buf = view("g_buf", [P, 2, T], o_misc)
        u_buf = view("u_buf", [P, 2, T], o_misc + 4 * 2 * T)
        t_buf = view("t_buf", [P, 2, T], o_misc)
        a_buf = view("a_buf", [P, 2, T], o_misc + 4 * 2 * T)
        o_tb = o_misc + 4 * 4 * T

        def tiles(name, first, n=1):
            return view(name, [P, n, T], o_hid + 4 * T * first)

        rA, rR, rB, rK = (tiles(n, 4 * i, 4) for i, n in enumerate(("rA", "rR", "rB", "rK")))
        rV, rBonus, rG = tiles("rV", 16, 4), tiles("rBonus", 20, 4), tiles("rG", 24, 4)
        pooled = tiles("pooled", 28, 4)
        pk, sg, ag, cs, iv, nr, sq = (tiles(n, 32 + i) for i, n in enumerate(("pk", "sg", "ag", "cs", "iv", "nr", "sqk")))
        wa, gx, scan_mask = tiles("wa", 39), tiles("gx", 40), tiles("scan_mask", 41)
        pads = view("pads", [P, 2, T + 4], o_misc + 4 * T)
        diff = view("diff", [P, T], o_misc)
        lora = view("lora", [P, 2, RW], o_acc)
        g_lora = view("g_lora", [P, RW], o_tb)
        w_pool = view("w_pool", [P, len(WINDOWS), P], o_tb + 4 * T)
        pool_a = view("pool_a", [P, PADW + T], o_misc)
        pool_b = view("pool_b", [P, PADW + T], o_hid + 4 * T * 42)
        pool_c = view("pool_c", [P, PADW + T], o_hid + 4 * T * 32)
        pchunk = fresh("pchunk", [P, PAIRS, NCH])
        assert place[0] <= nc.sbuf_usable_end, (place[0], nc.sbuf_usable_end)

        act_out = view("act_out", [P, KT, T], o_act)
        planes = view("planes", [P, NCP, 4, P], o_act)
        MT = view("MT", [P, NCH, P], o_act)
        MB = view("MB", [P, NCP, 4, P], o_act + 4 * KT * T)
        MK = tiles("MK", 28, 4)[:, :, :].rearrange("p c (h t) -> p c h t", h=4)
        TTm = view("TTm", [P, NCP, 2, P], o_hid + 4 * T * 32)
        Tm = view("Tm", [P, NCP, 2, P], o_hid + 4 * T * 34)
        Um = view("Um", [P, NCP, 2, P], o_hid + 4 * T * 36)
        Xm = view("Xm", [P, NCP, 2, P], o_hid + 4 * T * 38)
        AA = view("AA", [P, NCP, 2, P], o_hid + 4 * T * 40)
        GH = view("GH", [P, 2, 2 * NCP, HS], o_hid + 4 * T * 42)
        S = view("S", [P, NCH, P], o_hid + 4 * T * 36)
        RP = view("RP", [P, T], o_hid + 4 * T * 38)
        BTt, KTt, VTt, yb, ysq, OVb = (view(n, [P, T], o_misc + 4 * T * i) for i, n in enumerate(("BTt", "KTt", "VTt", "yb", "ysq", "OVb")))
        mask4 = sumsq
        mask_lv = view("mask_lv", [P, len(LEVELS) + 1, P], o_acc)
        mask_bd = mask_lv[:, len(LEVELS), :]

        ps = ctx.enter_context(nc.psum_tensor("ps", [P, 8, T], f32))

        sems = {}

        def sem(name):
            if name not in sems:
                sems[name] = ctx.enter_context(nc.semaphore(name))
            return sems[name]

        raw_full = [sem(f"raw_full{i}") for i in range(RING)]
        wm_full = [sem(f"wm_full{i}") for i in range(3)]
        hi_done, lo_done = sem("hi_done"), sem("lo_done")
        unit_used = sem("unit_used")
        for n in ("loaded_vec", "loaded_x", "loaded_cs", "loaded_xt", "loaded_lora", "loaded_masks"):
            sem(n)
        tensor_step, vector_step, scalar_step = sem("tensor_step"), sem("vector_step"), sem("scalar_step")
        v_chain, a_chain = sem("v_chain"), sem("a_chain")
        block = ctx.enter_context(nc.Block())

        def ffn_sems(s):
            return {n: sem(f"f{s}_{n}") for n in ("gate_read", "act_in", "silu", "val_read", "hid", "hid_hi", "hid_lo", "c1", "c2",
                                                  "down_tile", "x_new", "nx_hi", "nx_sq", "nx_lo", "nx_sum", "stat", "sd", "rstd")}

        @block.sync
        def _(sp):
            sp.dma_start(vec[:, :], a_vec).then_inc(sem("loaded_vec"), 16)
            for t in range(TT_):
                sp.dma_start(x_tok[:, t, :], a_x[t * P:(t + 1) * P, :]).then_inc(sem("loaded_x"), 16)
            sp.dma_start(const[:, :], a_const).then_inc(sem("loaded_vec"), 16)
            sp.dma_start(cs_raw[:, :, :], a_cs).then_inc(sem("loaded_cs"), 16)

            def load_unit(u, slot, turn):
                sp.dma_start(raw[:, slot, :], a_w[u]).then_inc(raw_full[slot], 16)

            def load_wm(i):
                if i >= 3:
                    sp.wait_ge(sem("wm_used"), i - 2)
                sp.dma_start(wm_ring[:, i % 3, :], a_wmod[i]).then_inc(wm_full[i % 3], 16)

            u = 0
            for i in range(6 * KT):
                load_wm(i)
                if i == 3:
                    sp.dma_start(xT[:, :, :], a_xt).then_inc(sem("loaded_xt"), 16)
                if i in (6, 8, 10, 12) or (i > 18 and i % 3 == 0):
                    if u >= RING:
                        sp.wait_ge(lo_done, u - RING + 1)
                    load_unit(u, u % RING, 0)
                    u += 1

            def load_through(first, last):
                n = first
                while n % RING and n < last:
                    sp.wait_ge(lo_done, n - RING + 1)
                    load_unit(n, n % RING, 0)
                    n += 1
                turns = (last - n) // RING
                if turns > 1:
                    with sp.Fori(0, turns) as i:
                        for j in range(RING):
                            sp.wait_ge(lo_done, i * RING + (n + j - RING + 1))
                            sp.dma_start(raw[:, j, :], a_w[bass.ds(i * RING + (n + j), 1)].rearrange("a p n -> p (a n)")).then_inc(raw_full[j], 16)
                    n += turns * RING
                while n < last:
                    sp.wait_ge(lo_done, n - RING + 1)
                    load_unit(n, n % RING, 0)
                    n += 1

            load_through(u, U_UP0 + 8)
            sp.wait_ge(sem("mod_mm"), 6)
            sp.dma_start(lora[:, :, :], a_lora[:, 0:2, :]).then_inc(sem("loaded_lora"), 16)
            sp.dma_start(g_lora[:, :], a_lora[:, 2, :]).then_inc(sem("loaded_lora"), 16)
            sp.dma_start(w_pool[:, :, :], a_pool).then_inc(sem("loaded_lora"), 16)
            load_through(U_UP0 + 8, U_OUT + AHEAD)
            sp.wait_ge(sem("za_read"), PAIRS)
            sp.wait_ge(sem("in_read"), len(IN_STARTS))
            sp.dma_start(mask4[:, :], a_mask[:, 0:4 * P]).then_inc(sem("loaded_masks"), 16)
            sp.dma_start(mask_lv[:, :, :], a_mask[:, 4 * P:].rearrange("p (l t) -> p l t", t=P)).then_inc(sem("loaded_masks"), 16)
            load_through(U_OUT + AHEAD, NU)
            for m in range(KT):
                sp.wait_ge(sem("y_out"), m + 1)
                sp.dma_start(out[m * P:(m + 1) * P, :], act_out[:, m, :]).then_inc(sem("stored"), 16)
            sp.wait_ge(sem("stored"), 16 * KT)

        @block.gpsimd
        def _(pool):
            def low(u, slot):
                pool.wait_ge(hi_done, u + 1)
                nc.gpsimd.tensor_tensor(w_lo[:, slot, :], raw[:, slot, :], w_hi[:, slot, :].bitcast(f32), SUB).then_inc(lo_done, 1)

            turns = NU // RING
            with pool.Fori(0, turns) as i:
                for j in range(RING):
                    low(i * RING + j, j)
            for u in range(turns * RING, NU):
                low(u, u % RING)

        @block.scalar
        def _(act):
            def after(s, n):
                act.wait_ge(s, n)

            def high(u, slot, turn, first=False):
                act.wait_ge(raw_full[slot], 16 * (turn + 1))
                if not first:
                    act.wait_ge(unit_used, u - RING + 1)
                nc.scalar.activation(w_hi[:, slot, :], raw[:, slot, :], ACT.Copy).then_inc(hi_done, 1)

            def high_n(u):
                if u < NU:
                    high(u, u % RING, u // RING, u < RING)

            n_chain = [0]

            def chain(ins):
                n_chain[0] += 1
                ins.then_inc(a_chain, 1)
                act.wait_ge(a_chain, n_chain[0])

            after(sem("loaded_vec"), 32)
            nc.scalar.activation(c_silu, v("c", 0, KT), ACT.Silu).then_inc(sem("c_silu"), 1)
            after(sem("loaded_x"), 16 * TT_)
            for t in range(TT_):
                chain(nc.scalar.activation(junk[:, :], x_tok[:, t, :], ACT.Square, accum_out=x_ss[:, t:t + 1]))
            nc.scalar.activation(x_ss, x_ss, ACT.Sqrt, bias=v("eps"), scale=1.0 / D).then_inc(sem("x_sd"), 1)
            after(sem("x_rstd"), 1)
            for t in range(TT_):
                nc.scalar.activation(xn_hi[:, t * D:(t + 1) * D], x_tok[:, t, :], ACT.Copy, scale=x_ss[:, t:t + 1]).then_inc(sem("xn_hi"), 1)
            after(sem("loaded_cs"), 16)
            nc.scalar.activation(cs_hi, cs_raw[:, :, :].rearrange("p a b -> p (a b)"), ACT.Copy).then_inc(sem("cs_hi"), 1)
            after(sem("cs_lo"), 1)
            for m in range(KT):
                b = 2 * (m % 3)
                after(sem("seq_mm"), m + 1)
                nc.scalar.activation(y_raw[:, m, 0:NCOS], ps[:, b, 0:NCOS], ACT.Copy).then_inc(sem("y_raw"), 1)
                nc.scalar.activation(y_raw[:, m, NCOS:NF], ps[:, b + 1, 0:NSIN], ACT.Copy).then_inc(sem("y_raw"), 1)
            for u in range(AHEAD):
                high_n(u)
            for m in range(KT):
                after(sem("y_mod"), m + 1)
                nc.scalar.activation(y_hi[:, m * NF:(m + 1) * NF], y_raw[:, m, :], ACT.Copy).then_inc(sem("y_hi"), 1)
            high_n(AHEAD)
            for t in range(KT):
                after(sem("chan_mm"), t + 1)
                if t >= 2:
                    after(sem("f_new"), t - 1)
                nc.scalar.activation(q_buf[:, t % 2, :], ps[:, 2 * (t % 3) + 1, 0:NSIN], ACT.Copy).then_inc(sem("q_new"), 1)
                after(sem("f_new"), t + 1)
                nc.scalar.activation(act_hi[:, t, :], f_buf[:, t % 2, :], ACT.Copy).then_inc(sem("f_hi"), 1)

            def squares(s_new, s_sq, m, dst, ready=None):
                after(s_new, m + 1)
                if ready is not None:
                    after(*ready)
                nc.scalar.activation(dst, xT[:, m, :], ACT.Square).then_inc(s_sq, 1)

            for m in range(KT):
                high_n(U_FNET + m + AHEAD)
                squares(sem("x0_new"), sem("x0_sq"), m, sumsq[:, :] if m == 0 else sq_buf[:, m, :])

            def root(s_stat, s_sd):
                after(s_stat, 1)
                nc.scalar.activation(rstd[:, :], ps[:, 6, :], ACT.Sqrt, bias=v("eps"), scale=1.0 / D).then_inc(s_sd, 1)

            root(sem("x0_stat"), sem("x0_sd"))
            for m in range(KT):
                after(sem("t_new"), m + 1)
                if m >= 2:
                    after(sem("a_lo"), m - 1)
                nc.scalar.activation(a_buf[:, m % 2, :], t_buf[:, m % 2, :], ACT.Identity, bias=mod(SH2, m), scale=gain2[:, m:m + 1]).then_inc(sem("a_new"), 1)
                after(sem("a_new"), m + 1)
                nc.scalar.activation(act_hi[:, m, :], a_buf[:, m % 2, :], ACT.Copy).then_inc(sem("a_hi"), 1)

            def ffn(stage, u_up, u_dn):
                s = ffn_sems(stage)

                def up_pair(i, first):
                    for q in range(2):
                        j = 2 * i + q
                        for h in range(2):
                            off = u_up + 2 * q + h + AHEAD
                            high(4 * i + off, off % RING, i + off // RING)
                        if stage == 0:
                            act.wait_ge(unit_used, u_up + 2 * j + 1)
                            if not first:
                                act.wait_ge(s["hid_lo"], j - 1)
                            nc.scalar.activation(g_buf[:, q, :], ps[:, 2 * q, :], ACT.Identity, bias=b_conv(j), scale=tap(1, j)).then_inc(s["c1"], 1)
                        act.wait_ge(s["act_in"], j + 1)
                        nc.scalar.activation(g_buf[:, q, :], g_buf[:, q, :], ACT.Silu).then_inc(s["silu"], 1)
                        act.wait_ge(s["hid"], j + 1)
                        nc.scalar.activation(hid_hi[:, bass.ds(j * T, T)], g_buf[:, q, :], ACT.Copy).then_inc(s["hid_hi"], 1)

                up_pair(0, True)
                with act.Fori(1, FT // 2) as i:
                    up_pair(i, False)
                for kt in range(FT):
                    high_n(u_dn + kt + AHEAD)

            def b_conv(j):
                return vec[:, bass.ds(VEC["b_conv"] + j, 1)]

            def tap(k, j):
                return vec[:, bass.ds(VEC["conv"] + k * FT + j, 1)]

            def next_input(s, m, g):
                after(s["x_new"], m + 1)
                nc.scalar.activation(act_hi[:, m, :], xT[:, m, :], ACT.Copy, scale=v(g, m)).then_inc(s["nx_hi"], 1)
                nc.scalar.activation(sumsq[:, :] if m == 0 else sq_buf[:, m, :], xT[:, m, :], ACT.Square).then_inc(s["nx_sq"], 1)

            ffn(0, U_UP0, U_DN0)
            s0 = ffn_sems(0)
            after(sem("g_both"), 1)
            for m in range(KT):
                after(s0["x_new"], m + 1)
                nc.scalar.activation(act_hi[:, m, :], xT[:, m, :], ACT.Copy, scale=g_both[:, m:m + 1]).then_inc(s0["nx_hi"], 1)
                nc.scalar.activation(sumsq[:, :] if m == 0 else sq_buf[:, m, :], xT[:, m, :], ACT.Square).then_inc(s0["nx_sq"], 1)
                nc.scalar.activation(sq_mid[:, m, :], xT[:, m, :], ACT.Square, scale=v("g_mid", m)).then_inc(s0["nx_sq"], 1)
            after(s0["stat"], 1)
            nc.scalar.activation(sumsq[:, :], ps[:, 6, :], ACT.Sqrt, bias=v("eps"), scale=1.0 / D).then_inc(s0["sd"], 1)
            after(sem("mid_ms"), 1)
            nc.scalar.activation(rstd[:, :], rstd[:, :], ACT.Sqrt, bias=v("eps")).then_inc(sem("mid_sd"), 1)
            ffn(1, U_UP1, U_DN1)
            s1 = ffn_sems(1)
            for m in range(KT):
                next_input(s1, m, "g_in")
            root(s1["stat"], s1["sd"])

            for i in range(len(IN_STARTS)):
                high_n(U_IN + i + AHEAD)
                if i == 0:
                    after(sem("in_read"), 1)
                    nc.scalar.activation(wa[0:32, 0, :], wa[0:32, 0, :], ACT.Tanh).then_inc(sem("wa_ready"), 1)
                if i == 1:
                    after(sem("in_read"), 2)
                    nc.scalar.activation(gx[:, 0, :], gx[:, 0, :], ACT.Sigmoid).then_inc(sem("g_in"), 1)
                if 2 <= i < 2 + 3 * PAIRS and (i - 2) % 3 == 2:
                    p = (i - 2) // 3
                    after(sem("za_mm"), p + 1)
                    if p:
                        after(sem("prep"), p)
                    chain(nc.scalar.activation(sg[:, 0, :], ps[:, 4, :], ACT.Sigmoid, bias=v("w0", p)))
                    nc.scalar.activation(ag[:, 0, :], ps[:, 5, :], ACT.Sigmoid, bias=v("a0", p)).then_inc(sem("za_read"), 1)
                    after(sem("in_read"), 3 + 3 * p)
                    nc.scalar.activation(sq[:, 0, :], pk[:, 0, :], ACT.Square, scale=v("k_k", p)).then_inc(sem("sq_ready"), 1)
                    after(sem("ss_mm"), p + 1)
                    nc.scalar.activation(nr[:, 0, :], ps[:, 6, :], ACT.Sqrt).then_inc(sem("nr_ready"), 1)
                    after(sem("cs_ready"), p + 1)
                    chain(nc.scalar.activation(iv[:, 0, :], cs[:, 0, :], ACT.Exp, scale=KAPPA))
                    chain(nc.scalar.activation(sg[:, 0, :], sg[:, 0, :], ACT.Exp, scale=-KAPPA))
                    nc.scalar.activation(cs[:, 0, :], cs[:, 0, :], ACT.Exp, scale=-KAPPA).then_inc(sem("exps"), 1)
                    after(sem("g_mm"), p + 1)
                    nc.scalar.activation(rG[:, p, :], ps[:, 7, :], ACT.Copy).then_inc(sem("g_read"), 1)
            for g in range(len(WINDOWS)):
                after(sem("pool_mm"), g + 1)
                nc.scalar.activation(act_hi[:, PAIRS + g, :], ps[:, g, :], ACT.Copy, scale=v("pool_scale", g)).then_inc(sem("pool_hi"), 1)

            n_step = [0]

            def did(p, name, ins):
                n_step[0] += 1
                assert at(AC_STEPS, p, name) == n_step[0]
                ins.then_inc(scalar_step, 1)

            for p in range(PAIRS):
                def pe_did(name):
                    act.wait_ge(tensor_step, at(PE_STEPS, p, name))

                def ve_did(name, p=p):
                    act.wait_ge(vector_step, at(VE_STEPS, p, name))

                ve_did("zero")
                for k, src in ((0, rA), (2, rR)):
                    for h in range(2):
                        r = slice(h * HS, (h + 1) * HS)
                        ins = nc.scalar.activation(planes[r, :, k + h, :], src[r, p, :].rearrange("q (c t) -> q c t", t=P), ACT.Copy)
                        if (k, h) != (2, 1):
                            chain(ins)
                did(p, "planes", ins)
                pe_did("tA")
                did(p, "tA", nc.scalar.activation(AA[:, :, :, 0:HS], ps[:, 0, :].rearrange("q (c h k) -> q c h k", c=NCP, h=2), ACT.Copy))
                pe_did("tK")
                did(p, "tK", nc.scalar.activation(KTt[:, :], ps[:, 2, :], ACT.Copy))
                halves = {"a": slice(0, 2), "b": slice(2, 4)}

                def square(dst, half, bank):
                    return nc.scalar.activation(dst[:, halves[half], :, :], ps[:, bank, :].rearrange("q (c h t) -> q c h t", c=2, h=2), ACT.Copy)

                pe_did("t1a")
                did(p, "t1a", square(Tm, "a", 4))
                for n in range(2, 7):
                    for half, bank in (("a", 6), ("b", 7)):
                        pe_did(f"U{n}{half}")
                        did(p, f"U{n}{half}", square(Um, half, bank))
                    if n < 6:
                        pe_did(f"t{n}a")
                        did(p, f"t{n}a", square(Tm, "a", 4))
                pe_did("AV")
                did(p, "AV", nc.scalar.activation(AA[:, :, :, HS:P], ps[:, 2, :].rearrange("q (c h k) -> q c h k", c=NCP, h=2), ACT.Copy))
                pe_did("GHa")
                did(p, "GHa", nc.scalar.activation(GH[:, :, 0:4, :], ps[:, 3, :].rearrange("q (s g k) -> q g s k", s=4, g=2), ACT.Copy))
                pe_did("OV")
                did(p, "OV", nc.scalar.activation(OVb[:, :], ps[:, 0, :], ACT.Copy))
                ve_did("yc")
                did(p, "sq", nc.scalar.activation(ysq[:, :], yb[:, :], ACT.Square))
                pe_did("var")
                did(p, "sd", nc.scalar.activation(rstd[:, :], ps[:, 1, :], ACT.Sqrt, bias=v("gn_eps"), scale=1.0 / HS))
                ve_did("yn")
                did(p, "affine", nc.scalar.activation(yb[:, :], yb[:, :], ACT.Identity, bias=v("ln_b", p), scale=v("ln_w", p)))
            for p in range(PAIRS):
                act.wait_ge(vector_step, at(VE_STEPS, PAIRS - 1, "out"))
                nc.scalar.activation(act_hi[:, p, :], rG[:, p, :], ACT.Copy).then_inc(sem("mix_hi"), 1)

            for m in range(KT):
                high_n(U_OUT + m + AHEAD)
                squares(sem("x2_new"), sem("x2_sq"), m, sumsq[:, :] if m == 0 else sq_buf[:, m, :])
            for m in range(KT):
                nc.scalar.activation(act_hi[:, m, :], xT[:, m, :], ACT.Copy, scale=v("g_ffn2", m)).then_inc(sem("x2_hi"), 1)
            root(sem("x2_stat"), sem("x2_sd"))
            ffn(2, U_UP2, U_DN2)
            s2 = ffn_sems(2)
            for m in range(KT):
                squares(s2["x_new"], s2["nx_sq"], m, sumsq[:, :] if m == 0 else sq_buf[:, m, :])
            root(s2["stat"], s2["sd"])

        @block.vector
        def _(ve):
            after = ve.wait_ge
            count = {}

            def chain(ins, name=None):
                s = v_chain if name is None else sem(name)
                count[name] = count.get(name, 0) + 1
                ins.then_inc(s, 1)
                ve.wait_ge(s, count[name])

            def tt(o, a, b, op, name=None):
                chain(nc.vector.tensor_tensor(o, a, b, op), name)

            def stt(o, a, s, b, op0, op1, name=None):
                chain(nc.vector.scalar_tensor_tensor(o, a, s, b, op0, op1), name)

            def tsc(o, a, s1, s2, op0, op1, name=None):
                chain(nc.vector.tensor_scalar(o, a, s1, s2, op0, op1), name)

            after(sem("x_sd"), 1)
            chain(nc.vector.reciprocal(x_ss, x_ss), "x_rstd")
            for t in range(TT_):
                after(sem("xn_hi"), t + 1)
                stt(xn_lo[:, t * D:(t + 1) * D], x_tok[:, t, :], x_ss[:, t:t + 1], xn_hi[:, t * D:(t + 1) * D].bitcast(f32), MUL, SUB, "xn_lo")
            after(sem("cs_hi"), 1)
            tt(cs_lo, cs_raw[:, :, :].rearrange("p a b -> p (a b)"), cs_hi.bitcast(f32), SUB, "cs_lo")
            after(sem("c_silu"), 1)

            def wm(i):
                vv, k = divmod(i, KT)
                after(wm_full[i % 3], 16 * (i // 3 + 1))
                if k == 0:
                    if vv:
                        after(sem("mod_mm"), vv)
                    tsc(mod_acc[:, :], wm_ring[:, i % 3, :], c_silu[:, 0:1], None, MUL, ALU.bypass, "wm_used")
                else:
                    stt(mod_acc[:, :], wm_ring[:, i % 3, :], c_silu[:, k:k + 1], mod_acc[:, :], MUL, ADD, "wm_used")

            def mod_out(vv):
                after(sem("mod_mm"), vv + 1)
                tt(mods[:, vv * KT:(vv + 1) * KT], ps[:, 7, vv * KT:(vv + 1) * KT], v("b_mod", vv * KT, KT), ADD, "mod_read")

            for vv in (SH1, SC1):
                for k in range(KT):
                    wm(vv * KT + k)
                mod_out(vv)
            stt(gain, mods[:, SC1 * KT:(SC1 + 1) * KT], 1.0, v("g_mix", 0, KT), ADD, MUL)
            tsc(sh_dc, mods[:, SH1 * KT:(SH1 + 1) * KT], float(T), None, MUL, ALU.bypass)
            for m in range(KT):
                after(sem("y_raw"), 2 * KT)
                tsc(y_raw[:, m, :], y_raw[:, m, :], gain[:, m:m + 1], None, MUL, ALU.bypass)
                tt(y_raw[:, m, 0:1], y_raw[:, m, 0:1], sh_dc[:, m:m + 1], ADD, "y_mod")
                after(sem("y_hi"), m + 1)
                tt(y_lo[:, m * NF:(m + 1) * NF], y_raw[:, m, :], y_hi[:, m * NF:(m + 1) * NF].bitcast(f32), SUB, "y_lo")
            for t in range(KT):
                b = 2 * (t % 3)
                after(sem("q_new"), t + 1)
                if t >= 2:
                    after(sem("f_hi"), t - 1)
                f = f_buf[:, t % 2, :]
                tt(f[:, 0:NSIN], ps[:, b, 0:NSIN], q_buf[:, t % 2, :], SUB)
                chain(nc.vector.tensor_copy(f[:, NSIN:NSIN + 1], ps[:, b, NSIN:NSIN + 1]))
                tt(f[:, NSIN + 1:T][:, ::-1], ps[:, b, 1:NSIN], q_buf[:, t % 2, 1:NSIN], ADD, "f_new")
                after(sem("f_hi"), t + 1)
                tt(act_lo[:, t, :], f, act_hi[:, t, :].bitcast(f32), SUB, "f_lo")
            for k in range(KT):
                wm(GT1 * KT + k)
            mod_out(GT1)
            after(sem("loaded_xt"), 16)
            done = 3 * KT
            for m in range(KT):
                after(unit_used, U_FNET + m + 1)
                stt(xT[:, m, :], ps[:, m % 4, :], mod(GT1, m), xT[:, m, :], MUL, ADD, "x0_new")
                if m:
                    after(sem("x0_sq"), m + 1)
                    tt(sumsq[:, :], sumsq[:, :], sq_buf[:, m, :], ADD, "x0_sum")
                for i in range(done, done + 3):
                    wm(i)
                    if i % KT == KT - 1:
                        mod_out(i // KT)
                done += 3
            stt(gain2, mods[:, SC2 * KT:(SC2 + 1) * KT], 1.0, v("g_ffn", 0, KT), ADD, MUL)

            def inverse(s_sd, name):
                after(s_sd, 1)
                ve.wait_ge(s_sd, 1)
                chain(nc.vector.reciprocal(rstd[:, :], rstd[:, :]), name)

            inverse(sem("x0_sd"), "x0_rstd")
            for m in range(KT):
                if m >= 2:
                    after(sem("a_new"), m - 1)
                tt(t_buf[:, m % 2, :], xT[:, m, :], rstd[:, :], MUL, "t_new")
                after(sem("a_hi"), m + 1)
                tt(act_lo[:, m, :], a_buf[:, m % 2, :], act_hi[:, m, :].bitcast(f32), SUB, "a_lo")

            def ffn(stage, u_up):
                s = ffn_sems(stage)

                def tap(k, j):
                    return vec[:, bass.ds(VEC["conv"] + k * FT + j, 1)]

                def up_pair(i, first):
                    for q in range(2):
                        j = 2 * i + q
                        gate, val, g, u_ = ps[:, 2 * q, :], ps[:, 2 * q + 1, :], g_buf[:, q, :], u_buf[:, q, :]
                        if stage == 0:
                            ve.wait_ge(s["c1"], j + 1)
                            nc.vector.scalar_tensor_tensor(g[:, 1:T], gate[:, 0:T - 1], tap(0, j), g[:, 1:T], MUL, ADD).then_inc(s["c2"], 1)
                            ve.wait_ge(s["c2"], j + 1)
                            nc.vector.scalar_tensor_tensor(g[:, 0:T - 1], gate[:, 1:T], tap(2, j), g[:, 0:T - 1], MUL, ADD).then_inc(s["act_in"], 1)
                            ve.wait_ge(s["silu"], j + 1)
                            ve.wait_ge(unit_used, u_up + 2 * j + 2)
                            nc.vector.tensor_tensor(g, val, g, MUL).then_inc(s["hid"], 1)
                        else:
                            ve.wait_ge(unit_used, u_up + 2 * j + 1)
                            if not first:
                                ve.wait_ge(s["hid_lo"], j - 1)
                            nc.vector.tensor_tensor(g, gate, rstd[:, :], MUL).then_inc(s["act_in"], 1)
                            ve.wait_ge(unit_used, u_up + 2 * j + 2)
                            nc.vector.tensor_tensor(u_, val, rstd[:, :], MUL).then_inc(s["val_read"], 1)
                            ve.wait_ge(s["silu"], j + 1)
                            ve.wait_ge(s["val_read"], j + 1)
                            nc.vector.tensor_tensor(g, g, u_, MUL).then_inc(s["hid"], 1)
                        ve.wait_ge(s["hid_hi"], j + 1)
                        nc.vector.tensor_tensor(hid_lo[:, bass.ds(j * T, T)], g, hid_hi[:, bass.ds(j * T, T)].bitcast(f32), SUB).then_inc(s["hid_lo"], 1)

                up_pair(0, True)
                if stage == 1:
                    for m in range(KT):
                        stt(xT[:, m, :], xT[:, m, :], v("g_mid", m), sumsq[:, :], MUL, MUL)
                with ve.Fori(1, FT // 2) as i:
                    up_pair(i, False)
                ve.wait_ge(s["hid_lo"], FT)

            def next_x(stage, scale, g):
                s, f = ffn_sems(stage), f"f{stage}_"
                for m in range(KT):
                    if m < KT - 1:
                        after(s["down_tile"], m + 1)
                    else:
                        after(unit_used, (U_DN0, U_DN1, U_DN2)[stage] + FT)
                    stt(xT[:, m, :], ps[:, m, :], mod(GT2, m) if scale is None else scale, xT[:, m, :], MUL, ADD, f + "x_new")
                    if stage == 0:
                        after(s["nx_hi"], m + 1)
                        stt(act_lo[:, m, :], xT[:, m, :], g_both[:, m:m + 1], act_hi[:, m, :].bitcast(f32), MUL, SUB, f + "nx_lo")
                    if g is not None:
                        after(s["nx_hi"], m + 1)
                        stt(act_lo[:, m, :], xT[:, m, :], v(g, m), act_hi[:, m, :].bitcast(f32), MUL, SUB, f + "nx_lo")
                if stage == 0:
                    for m in range(1, KT):
                        after(s["nx_sq"], 2 * m + 1)
                        tt(sumsq[:, :], sumsq[:, :], sq_buf[:, m, :], ADD, f + "nx_sum")
                    for m in range(1, KT):
                        after(s["nx_sq"], 2 * m + 2)
                        tt(sq_mid[:, 0, :], sq_mid[:, 0, :], sq_mid[:, m, :], ADD, "mid_sum")
                    after(s["sd"], 1)
                    chain(nc.vector.reciprocal(sumsq[:, :], sumsq[:, :]))
                    after(sem("mid_stat"), 1)
                    stt(rstd[:, :], ps[:, 7, :], 1.0 / D, sumsq[:, :], MUL, MUL)
                    tt(rstd[:, :], rstd[:, :], sumsq[:, :], MUL, "mid_ms")
                    after(sem("mid_sd"), 1)
                    chain(nc.vector.reciprocal(rstd[:, :], rstd[:, :]))
                    tt(rstd[:, :], rstd[:, :], sumsq[:, :], MUL, f + "rstd")
                    return
                for m in range(1, KT):
                    after(s["nx_sq"], m + 1)
                    tt(sumsq[:, :], sumsq[:, :], sq_buf[:, m, :], ADD, f + "nx_sum")
                inverse(s["sd"], f + "rstd")

            ffn(0, U_UP0)
            tt(g_both, v("g_mid", 0, KT), v("g_ffn1", 0, KT), MUL, "g_both")
            next_x(0, None, None)
            ffn(1, U_UP1)
            next_x(1, 0.5, "g_in")

            chain(nc.vector.memset(pads[:, :, 0:1], 0.0))
            chain(nc.vector.memset(scan_mask[:, 0, :], 1.0))
            chain(nc.vector.memset(scan_mask[:, 0, 0:T:CH], 0.0))
            tsc(one_minus_ka, v("k_a", 0, PAIRS), -1.0, 1.0, MUL, ADD)

            def shifted(i, dst):
                after(unit_used, U_IN + i + 1)
                pad = pads[:, i % 2, :]
                tt(pad[:, 1:T + 1], ps[:, i % 4, :], rstd[:, :], MUL)
                tt(diff[:, :], pad[:, 0:T], pad[:, 1:T + 1], SUB)
                stt(dst, diff[:, :], v("mu", i), pad[:, 1:T + 1], MUL, ADD, "in_read")

            shifted(0, wa[:, 0, :])
            shifted(1, gx[:, 0, :])
            for p in range(PAIRS):
                i = 2 + 3 * p
                shifted(i, pk[:, 0, :])
                shifted(i + 1, rR[:, p, :])
                shifted(i + 2, rV[:, p, :])
                after(sem("za_read"), p + 1)
                chain(nc.vector.tensor_tensor_scan(cs[:, 0, :], scan_mask[:, 0, :], sg[:, 0, :], 0.0, MUL, ADD))
                tt(sg[:, 0, :], cs[:, 0, :], sg[:, 0, :], SUB, "cs_ready")
                after(sem("nr_ready"), p + 1)
                tsc(nr[:, 0, :], nr[:, 0, :], L2_EPS, None, MAX, ALU.bypass)
                chain(nc.vector.reciprocal(nr[:, 0, :], nr[:, 0, :]))
                stt(nr[:, 0, :], pk[:, 0, :], v("k_k", p), nr[:, 0, :], MUL, MUL)
                after(sem("exps"), p + 1)
                stt(rA[:, p, :], nr[:, 0, :], -1.0, sg[:, 0, :], MUL, MUL)
                tt(sq[:, 0, :], nr[:, 0, :], ag[:, 0, :], MUL)
                tt(rB[:, p, :], sq[:, 0, :], iv[:, 0, :], MUL)
                tsc(ag[:, 0, :], ag[:, 0, :], v("k_a", p), one_minus_ka[:, p:p + 1], MUL, ADD)
                tt(ag[:, 0, :], ag[:, 0, :], pk[:, 0, :], MUL)
                tt(rK[:, p, :], ag[:, 0, :], iv[:, 0, :], MUL)
                stt(pk[:, 0, :], rR[:, p, :], v("r_k", p), ag[:, 0, :], MUL, MUL, "rk_ready")
                chain(nc.vector.tensor_copy(pchunk[:, p, :], cs[:, 0, CH - 1:T:CH]))
                tt(rR[:, p, :], rR[:, p, :], cs[:, 0, :], MUL)
                after(sem("bonus_mm"), p + 1)
                tt(rBonus[:, p, :], ps[:, 6, :], rV[:, p, :], MUL, "prep")
            for b_ in (pool_a, pool_b, pool_c):
                chain(nc.vector.memset(b_[:, 0:PADW], 0.0))
            for g, win in enumerate(WINDOWS):
                i = 2 + 3 * PAIRS + g
                after(unit_used, U_IN + i + 1)
                tt(pool_a[:, PADW:], ps[:, i % 4, :], rstd[:, :], MUL, "in_read")
                src, k = pool_a, 1
                while k < win:
                    dst = pool_b if src is not pool_b else pool_c
                    chain(nc.vector.tensor_tensor(dst[:, PADW:], src[:, PADW:], src[:, PADW - k:PADW + T - k], ADD))
                    src, k = dst, 2 * k
                tt(pooled[:, g, 0:PADW], src[:, PADW:2 * PADW], inv_count[:, g * PADW:(g + 1) * PADW], MUL)
                tsc(pooled[:, g, PADW:], src[:, 2 * PADW:], 1.0 / win, None, MUL, ALU.bypass)
                tt(pooled[:, g, :], pooled[:, g, :], pool_a[:, PADW:], SUB, "pooled")
            for g in range(len(WINDOWS)):
                after(sem("pool_hi"), g + 1)
                stt(act_lo[:, PAIRS + g, :], ps[:, g, :], v("pool_scale", g), act_hi[:, PAIRS + g, :].bitcast(f32), MUL, SUB, "pool_lo")

            after(sem("loaded_masks"), 32)
            n_step = [0]

            def did(p, name, ins):
                n_step[0] += 1
                assert at(VE_STEPS, p, name) == n_step[0], (name, n_step)
                ins.then_inc(vector_step, 1)
                ve.wait_ge(vector_step, n_step[0])

            halves = {"a": slice(0, 2), "b": slice(2, 4)}

            def bank4(b):
                return ps[:, b, :].rearrange("q (c h t) -> q c h t", c=2, h=2)

            for p in range(PAIRS):
                def pe_did(name):
                    ve.wait_ge(tensor_step, at(PE_STEPS, p, name))

                def ac_did(name):
                    ve.wait_ge(scalar_step, at(AC_STEPS, p, name))

                for h in range(2):
                    other = slice((1 - h) * HS, (2 - h) * HS)
                    for k in (0, 2):
                        ins = nc.vector.memset(planes[other, :, k + h, :], 0.0)
                        if (h, k) != (1, 2):
                            chain(ins)
                did(p, "zero", ins)
                pe_did("tB")
                did(p, "tB", nc.vector.tensor_copy(BTt[:, :], ps[:, 1, :]))
                pe_did("tV")
                did(p, "tV", nc.vector.tensor_copy(VTt[:, :], ps[:, 3, :]))
                for c in range(NCP):
                    pe_did(f"L{c}")
                    did(p, f"L{c}", nc.vector.tensor_tensor(MB[:, c, :, :].rearrange("q h t -> q (h t)"), ps[:, 4 + c, :], mask4[:, :], MUL))
                for c in range(NCP):
                    pe_did(f"K{c}")
                    did(p, f"K{c}", nc.vector.tensor_tensor(MK[:, c, :, :].rearrange("q h t -> q (h t)"), ps[:, c, :], mask4[:, :], MUL))

                def level_mask(n, c):
                    return mask_lv[:, n:n + 1, :].unsqueeze(1).to_broadcast([P, c, 2, P])

                for half in "ab":
                    c = halves[half]
                    chain(nc.vector.tensor_tensor(TTm[:, c, :, :], MB[:, c, 0:2, :], level_mask(0, 2), MUL))
                    did(p, f"D1{half}", nc.vector.tensor_tensor(TTm[:, c, :, :], TTm[:, c, :, :],
                                                               ident.unsqueeze(1).unsqueeze(1).to_broadcast([P, 2, 2, P]), ADD))
                did(p, "X2", nc.vector.tensor_tensor(Xm[:, :, :, :], MB[:, :, 0:2, :], level_mask(1, NCP), MUL))
                pe_did("t1b")
                did(p, "t1b", nc.vector.tensor_copy(Tm[:, halves["b"], :, :], bank4(5)))
                for n in range(2, 7):
                    for half, bank in (("a", 0), ("b", 1)):
                        c = halves[half]
                        pe_did(f"D{n}{half}")
                        did(p, f"D{n}{half}", nc.vector.tensor_tensor(TTm[:, c, :, :], bank4(bank), TTm[:, c, :, :], ADD))
                    if n < 6:
                        did(p, f"X{n + 1}", nc.vector.tensor_tensor(Xm[:, :, :, :], MB[:, :, 0:2, :], level_mask(n, NCP), MUL))
                        pe_did(f"t{n}b")
                        did(p, f"t{n}b", nc.vector.tensor_copy(Tm[:, halves["b"], :, :], bank4(5)))
                pe_did("GHb")
                did(p, "GHb", nc.vector.tensor_copy(GH[:, :, 4:8, :], ps[:, 6, :].rearrange("q (s g k) -> q g s k", s=4, g=2)))
                pe_did("RP")
                did(p, "RP", nc.vector.tensor_tensor(RP[:, :], ps[:, 7, :], rR[:, p, :], ADD))
                for half, bank, odd in (("a", 1, 0), ("b", 4, 1)):
                    pe_did(f"MT{half}")
                    m4 = MT[:, odd:NCH:2, :]
                    chain(nc.vector.tensor_tensor(m4, ps[:, bank, :].rearrange("q (c t) -> q c t", c=4), ident.unsqueeze(1).to_broadcast([P, 4, P]), ADD))
                    did(p, f"MT{half}", nc.vector.tensor_tensor(m4, m4, mask_bd.unsqueeze(1).to_broadcast([P, 4, P]), MUL))
                for half, bank, odd in (("a", 5, 0), ("b", 2, 1)):
                    pe_did(f"N{half}")
                    for c in range(odd, NCH, 2):
                        ins = nc.vector.scalar_tensor_tensor(S[:, c, :], ps[:, bank, (c // 2) * P:(c // 2 + 1) * P], pchunk[:, p, c:c + 1], mask_bd, MUL, MUL)
                        if c < NCH - 2 + odd:
                            chain(ins)
                    did(p, f"N{half}", ins)
                for c in range(1, NCH - 1):
                    pe_did(f"S{c}")
                    did(p, f"S{c}", nc.vector.scalar_tensor_tensor(S[:, c, :], ps[:, 3 if c % 2 else 6, 0:P], pchunk[:, p, c:c + 1], S[:, c, :], MUL, ADD))
                ac_did("OV")
                pe_did("Y")
                chain(nc.vector.tensor_copy(yb[:, 0:CH], OVb[:, 0:CH]))
                did(p, "Y", nc.vector.tensor_tensor(yb[:, CH:T], ps[:, 7, CH:T], OVb[:, CH:T], ADD))
                pe_did("mean")
                did(p, "yc", nc.vector.scalar_tensor_tensor(yb[:, :], ps[:, 0, :], -1.0 / HS, yb[:, :], MUL, ADD))
                ac_did("sd")
                chain(nc.vector.reciprocal(rstd[:, :], rstd[:, :]))
                did(p, "yn", nc.vector.tensor_tensor(yb[:, :], yb[:, :], rstd[:, :], MUL))
                ac_did("affine")
                chain(nc.vector.tensor_tensor(yb[:, :], yb[:, :], rBonus[:, p, :], ADD))
                did(p, "out", nc.vector.tensor_tensor(rG[:, p, :], yb[:, :], rG[:, p, :], MUL))
            for p in range(PAIRS):
                after(sem("mix_hi"), p + 1)
                tt(act_lo[:, p, :], rG[:, p, :], act_hi[:, p, :].bitcast(f32), SUB, "mix_lo")

            for m in range(KT):
                after(unit_used, U_OUT + m + 1)
                tt(xT[:, m, :], ps[:, m % 4, :], xT[:, m, :], ADD, "x2_new")
                if m:
                    after(sem("x2_sq"), m + 1)
                    tt(sumsq[:, :], sumsq[:, :], sq_buf[:, m, :], ADD, "x2_sum")
            for m in range(KT):
                after(sem("x2_hi"), m + 1)
                stt(act_lo[:, m, :], xT[:, m, :], v("g_ffn2", m), act_hi[:, m, :].bitcast(f32), MUL, SUB, "x2_lo")
            inverse(sem("x2_sd"), "x2_rstd")
            ffn(2, U_UP2)
            next_x(2, 0.5, None)
            for m in range(KT):
                stt(act_out[:, m, :], xT[:, m, :], v("g_last", m), rstd[:, :], MUL, MUL, "y_out")

        @block.tensor
        def _(pe):
            after = pe.wait_ge

            def three(o, wh, wl, xh, xl, start, stop):
                nc.tensor.matmul(o, wh, xh, start=start, stop=False)
                nc.tensor.matmul(o, wh, xl, start=False, stop=False)
                return nc.tensor.matmul(o, wl, xh, start=False, stop=stop)

            def blk(slot, b):
                return w_hi[:, slot, b * P:(b + 1) * P], w_lo[:, slot, b * P:(b + 1) * P]

            def mod_columns(vv):
                after(sem("wm_used"), KT * (vv + 1))
                for m in range(KT):
                    last = nc.tensor.matmul(ps[:, 7, vv * KT + m:vv * KT + m + 1], mod_acc[:, m * P:(m + 1) * P], ones[:, 0:1], start=True, stop=True)
                last.then_inc(sem("mod_mm"), 1)

            after(sem("xn_lo"), TT_)
            after(sem("cs_lo"), 1)
            for m in range(KT):
                b = 2 * (m % 3)
                if m >= 3:
                    after(sem("y_raw"), 2 * (m - 2))
                for bank, c0, n in ((b, 0, NCOS), (b + 1, NCOS, NSIN)):
                    for k in range(TT_):
                        w = slice(k * D + m * P, k * D + (m + 1) * P)
                        x = slice(k * NF + c0, k * NF + c0 + n)
                        last = three(ps[:, bank, 0:n], xn_hi[:, w], xn_lo[:, w], cs_hi[:, x], cs_lo[:, x], k == 0, k == TT_ - 1)
                last.then_inc(sem("seq_mm"), 1)
            mod_columns(SH1)
            mod_columns(SC1)
            after(lo_done, U_DFT + 1)
            for t in range(KT):
                g, mm = divmod(t, 2)
                b = 2 * (t % 3)
                after(sem("y_lo"), 2 * g + 2)
                if t >= 3:
                    after(sem("f_new"), t - 2)
                for f, c0, n in ((0, 0, NCOS), (1, NCOS, NSIN)):
                    for kk in range(2):
                        x = slice((2 * g + kk) * NF + c0, (2 * g + kk) * NF + c0 + n)
                        last = three(ps[:, b + f, 0:n], *blk(0, 4 * f + 2 * kk + mm), y_hi[:, x], y_lo[:, x], kk == 0, kk == 1)
                last.then_inc(sem("chan_mm"), 1)
            after(sem("chan_mm"), KT)
            pe.sem_inc(unit_used, 1)

            def unit_by_output(u, slot, bank, ready=None):
                after(lo_done, u + 1)
                for k in range(KT):
                    if ready is not None:
                        after(ready, k + 1)
                    last = three(ps[:, bank, :], *blk(slot, k), act_hi[:, k, :], act_lo[:, k, :], k == 0, k == KT - 1)
                last.then_inc(unit_used, 1)

            after(sem("f_lo"), KT)
            for m in range(KT):
                if m >= 4:
                    after(sem("x0_new"), m - 3)
                unit_by_output(U_FNET + m, (U_FNET + m) % RING, m % 4)
                if m == 2:
                    mod_columns(GT1)
                if m == 5:
                    mod_columns(SH2)
            mod_columns(SC2)

            def stat(s_sum, n, s_stat, bank=6, sums=sumsq[:, :]):
                after(s_sum, n)
                nc.tensor.matmul(ps[:, bank, :], ones, sums, start=True, stop=True).then_inc(s_stat, 1)

            stat(sem("x0_sum"), KT - 1, sem("x0_stat"))
            mod_columns(GT2)

            def ffn(stage, u_up, u_dn, ready, mid):
                s = ffn_sems(stage)

                def up_pair(i, first):
                    for q in range(2):
                        j = 2 * i + q
                        for h in range(2):
                            off = u_up + 2 * q + h
                            if not first:
                                if stage == 0:
                                    pe.wait_ge(s["act_in"] if h == 0 else s["hid"], j - 1)
                                else:
                                    pe.wait_ge(s["act_in"] if h == 0 else s["val_read"], j - 1)
                            unit_by_output(4 * i + off, off % RING, 2 * q + h, ready if first and q == 0 and h == 0 else None)
                        if first and q == 0:
                            mid()

                up_pair(0, True)
                with pe.Fori(1, FT // 2) as i:
                    up_pair(i, False)

                def down(kt, u, slot, x, start, stop, signal=True):
                    after(lo_done, u + 1)
                    after(s["hid_lo"], kt + 1)
                    for m in range(KT):
                        last = three(ps[:, m, :], *blk(slot, m), hid_hi[:, x], hid_lo[:, x], start, stop)
                    last.then_inc(unit_used, 1)

                after(s["hid"], FT)
                for kt in range(4):
                    down(kt, u_dn + kt, (u_dn + kt) % RING, slice(kt * T, (kt + 1) * T), kt == 0, False)
                with pe.Fori(1, (FT - 2) // 4) as i:
                    for j in range(4):
                        down(4 * i + j, 4 * i + (u_dn + j), (u_dn + j) % RING, bass.ds((4 * i + j) * T, T), False, False)
                after(lo_done, u_dn + FT)
                after(s["hid_lo"], FT)
                for m in range(KT):
                    for kt in (FT - 2, FT - 1):
                        x = slice(kt * T, (kt + 1) * T)
                        last = three(ps[:, m, :], *blk((u_dn + kt) % RING, m), hid_hi[:, x], hid_lo[:, x], False, kt == FT - 1)
                    last.then_inc(s["down_tile"], 1)
                after(s["down_tile"], KT)
                pe.sem_inc(unit_used, 2)

            ffn(0, U_UP0, U_DN0, sem("a_lo"), lambda: None)
            s0, s1, s2 = (ffn_sems(i) for i in range(3))

            def mid_stats():
                after(s0["x_new"], KT)
                stat(s0["nx_sum"], KT - 1, s0["stat"])
                stat(sem("mid_sum"), KT - 1, sem("mid_stat"), 7, sq_mid[:, 0, :])

            ffn(1, U_UP1, U_DN1, s0["nx_lo"], mid_stats)

            def small_products(i):
                if 2 <= i < 2 + 3 * PAIRS and (i - 2) % 3 == 1:
                    p = (i - 2) // 3
                    cols = slice(p * P, (p + 1) * P)
                    after(sem("wa_ready"), 1)
                    after(sem("loaded_lora"), 48)
                    if p:
                        after(sem("za_read"), p)
                    nc.tensor.matmul(ps[:, 4, :], lora[:, 0, cols], wa[:, 0, :], start=True, stop=True)
                    nc.tensor.matmul(ps[:, 5, :], lora[:, 1, cols], wa[:, 0, :], start=True, stop=True).then_inc(sem("za_mm"), 1)
                    after(sem("g_in"), 1)
                    if p:
                        after(sem("g_read"), p)
                    nc.tensor.matmul(ps[:, 7, :], g_lora[:, cols], gx[:, 0, :], start=True, stop=True).then_inc(sem("g_mm"), 1)
                if 2 <= i < 2 + 3 * PAIRS and (i - 2) % 3 == 2:
                    p = (i - 2) // 3
                    after(sem("sq_ready"), p + 1)
                    if p:
                        after(sem("prep"), p)
                    nc.tensor.matmul(ps[:, 6, :], bones, sq[:, 0, :], start=True, stop=True).then_inc(sem("ss_mm"), 1)
                if 5 <= i < 5 + 3 * PAIRS and (i - 5) % 3 == 1:
                    p = (i - 5) // 3
                    after(sem("rk_ready"), p + 1)
                    nc.tensor.matmul(ps[:, 6, :], bones, pk[:, 0, :], start=True, stop=True).then_inc(sem("bonus_mm"), 1)

            for i in range(len(IN_STARTS)):
                if i == 0:
                    after(s1["x_new"], KT)
                if i >= 4:
                    after(sem("in_read"), i - 3)
                unit_by_output(U_IN + i, (U_IN + i) % RING, i % 4, s1["nx_lo"] if i == 0 else None)
                if i == 0:
                    stat(s1["nx_sum"], KT - 1, s1["stat"])
                small_products(i)
            for g in range(len(WINDOWS)):
                after(sem("pooled"), g + 1)
                after(sem("in_read"), len(IN_STARTS))
                nc.tensor.matmul(ps[:, g, :], w_pool[:, g, :], pooled[:, g, :], start=True, stop=True).then_inc(sem("pool_mm"), 1)

            n_step = [0]

            def did(p, name, ins):
                n_step[0] += 1
                assert at(PE_STEPS, p, name) == n_step[0], name
                ins.then_inc(tensor_step, 1)

            after(sem("pool_lo"), len(WINDOWS))
            after(sem("prep"), PAIRS)
            for p in range(PAIRS):
                def ve_did(name, q=None):
                    q = p if q is None else q
                    if q >= 0:
                        pe.wait_ge(vector_step, at(VE_STEPS, q, name))

                def ac_did(name, q=None):
                    q = p if q is None else q
                    if q >= 0:
                        pe.wait_ge(scalar_step, at(AC_STEPS, q, name))

                ve_did("out", p - 1)
                for b, (name, src) in enumerate((("tA", rA), ("tB", rB), ("tK", rK), ("tV", rV))):
                    for c in range(NCP):
                        cols = slice(c * P, (c + 1) * P)
                        last = nc.tensor.transpose(ps[:, b, cols], src[:, p, cols], ident)
                    did(p, name, last)
                ac_did("planes")
                for c in range(NCP):
                    did(p, f"L{c}", nc.tensor.matmul(ps[:, 4 + c, :], rB[:, p, c * P:(c + 1) * P], planes[:, c, :, :].rearrange("q h t -> q (h t)"), start=True, stop=True))
                ac_did("tK")
                ve_did("tV")
                for c in range(NCP):
                    did(p, f"K{c}", nc.tensor.matmul(ps[:, c, :], rK[:, p, c * P:(c + 1) * P], planes[:, c, :, :].rearrange("q h t -> q (h t)"), start=True, stop=True))

                def systems(half):
                    c0 = 0 if half == "a" else 2
                    return [(c, h, slice(((c - c0) * 2 + h) * P, ((c - c0) * 2 + h + 1) * P)) for c in (c0, c0 + 1) for h in range(2)]

                for half, bank in (("a", 4), ("b", 5)):
                    ve_did(f"D1{half}")
                    for c, h, o in systems(half):
                        last = nc.tensor.transpose(ps[:, bank, o], TTm[:, c, h, :], ident)
                    did(p, f"t1{half}", last)
                for n in range(2, 7):
                    for half, bank in (("a", 6), ("b", 7)):
                        ve_did(f"X{n}")
                        if half == "a":
                            ac_did(f"t{n - 1}a")
                        else:
                            ve_did(f"t{n - 1}b")
                        for c, h, o in systems(half):
                            last = nc.tensor.matmul(ps[:, bank, o], Xm[:, c, h, :], Tm[:, c, h, :], start=True, stop=True)
                        did(p, f"U{n}{half}", last)
                    for half, bank in (("a", 0), ("b", 1)):
                        ac_did(f"U{n}{half}")
                        if n == 2:
                            ve_did(f"K{bank}")
                        for c, h, o in systems(half):
                            last = nc.tensor.matmul(ps[:, bank, o], Um[:, c, h, :], TTm[:, c, h, :], start=True, stop=True)
                        did(p, f"D{n}{half}", last)
                    if n < 6:
                        for half, bank in (("a", 4), ("b", 5)):
                            ve_did(f"D{n}{half}")
                            for c, h, o in systems(half):
                                last = nc.tensor.transpose(ps[:, bank, o], TTm[:, c, h, :], ident)
                            did(p, f"t{n}{half}", last)
                ve_did("D6b")
                ac_did("tA")
                for c in range(NCP):
                    for h in range(2):
                        last = nc.tensor.matmul(ps[:, 2, (2 * c + h) * HS:(2 * c + h + 1) * HS], MK[:, c, h, :], VTt[:, c * P + h * HS:c * P + (h + 1) * HS], start=True, stop=True)
                did(p, "AV", last)
                ac_did("AV")
                for half, bank in (("a", 3), ("b", 6)):
                    for c, h, o in systems(half):
                        last = nc.tensor.matmul(ps[:, bank, o], TTm[:, c, h, :], AA[:, c, h, :], start=True, stop=True)
                    did(p, f"GH{half}", last)
                ac_did("GHa")
                ve_did("GHb")
                for c in range(NCP):
                    for h in range(2):
                        r = slice(h * HS, (h + 1) * HS)
                        last = nc.tensor.matmul(ps[r, 7, c * P:(c + 1) * P], GH[:, 0, 2 * c + h, :], MB[:, c, 2 + h, :], start=True, stop=True)
                did(p, "RP", last)
                for c in range(NCP):
                    for h in range(2):
                        r, o = slice(h * HS, (h + 1) * HS), slice(c * P, (c + 1) * P)
                        nc.tensor.matmul(ps[r, 0, o], GH[:, 1, 2 * c + h, :], MB[:, c, 2 + h, :], start=True, stop=False)
                        last = nc.tensor.matmul(ps[r, 0, o], VTt[:, c * P + h * HS:c * P + (h + 1) * HS], MK[:, c, 2 + h, :], start=False, stop=True)
                did(p, "OV", last)
                for half, bank, odd in (("a", 1, 0), ("b", 4, 1)):
                    for c in range(odd, NCH, 2):
                        cp, r = c // 2, slice(odd * CH, (odd + 1) * CH)
                        last = nc.tensor.matmul(ps[:, bank, cp * P:(cp + 1) * P], GH[r, 0, 2 * cp:2 * cp + 2, :].rearrange("q s k -> q (s k)"), BTt[r, cp * P:(cp + 1) * P], start=True, stop=True)
                    did(p, f"MT{half}", last)
                for half, bank, odd in (("a", 5, 0), ("b", 2, 1)):
                    for c in range(odd, NCH, 2):
                        cp, r = c // 2, slice(odd * CH, (odd + 1) * CH)
                        o = ps[:, bank, cp * P:(cp + 1) * P]
                        nc.tensor.matmul(o, BTt[r, cp * P:(cp + 1) * P], GH[r, 1, 2 * cp:2 * cp + 2, :].rearrange("q s k -> q (s k)"), start=True, stop=False)
                        last = nc.tensor.matmul(o, KTt[r, cp * P:(cp + 1) * P], VTt[r, cp * P:(cp + 1) * P], start=False, stop=True)
                    did(p, f"N{half}", last)
                ve_did("Nb")
                for c in range(1, NCH - 1):
                    if c > 1:
                        ve_did(f"S{c - 1}")
                    did(p, f"S{c}", nc.tensor.matmul(ps[:, 3 if c % 2 else 6, 0:P], MT[:, c, :], S[:, c - 1, :], start=True, stop=True))
                ve_did(f"S{NCH - 2}")
                for c in range(1, NCH):
                    last = nc.tensor.matmul(ps[:, 7, c * CH:(c + 1) * CH], S[:, c - 1, :], RP[:, c * CH:(c + 1) * CH], start=True, stop=True)
                did(p, "Y", last)
                ve_did("Y")
                did(p, "mean", nc.tensor.matmul(ps[:, 0, :], bones, yb[:, :], start=True, stop=True))
                ac_did("sq")
                did(p, "var", nc.tensor.matmul(ps[:, 1, :], bones, ysq[:, :], start=True, stop=True))

            after(sem("mix_lo"), PAIRS)
            for m in range(KT):
                if m >= 4:
                    after(sem("x2_new"), m - 3)
                unit_by_output(U_OUT + m, (U_OUT + m) % RING, m % 4)
            after(sem("x2_new"), KT)
            ffn(2, U_UP2, U_DN2, sem("x2_lo"), lambda: stat(sem("x2_sum"), KT - 1, sem("x2_stat")))
            after(s2["x_new"], KT)
            stat(s2["nx_sum"], KT - 1, s2["stat"])


def _columns(a):
    return np.asarray(a).reshape(-1, P).T


def _by_output(w):
    return w.reshape(KT, P, -1, P).transpose(2, 1, 0, 3).reshape(-1, P, D)


def _tables():
    l = np.arange(T)
    cos_k, sin_k = np.arange(NCOS), np.arange(NSIN)
    cs = np.concatenate([np.cos(2 * np.pi * (np.outer(l, cos_k) % T) / T), np.sin(2 * np.pi * (np.outer(l, sin_k) % T) / T)], 1)
    cs[:, NCOS] = 0.0
    cs = cs.reshape(TT_, P, NF).transpose(1, 0, 2)
    c = np.arange(FG)
    ang = 2 * np.pi * (np.outer(c, c) % FG) / FG
    norm = 1.0 / np.sqrt(T * FG)
    chan = np.stack([np.cos(ang) * norm, np.sin(ang) * norm]).reshape(2, 2, P, 2, P).transpose(2, 0, 1, 3, 4).reshape(P, D)
    i = np.arange(P)
    inv = np.stack([1.0 / np.minimum(np.arange(PADW) + 1, w) for w in WINDOWS]).reshape(1, -1).repeat(P, 0)
    const = np.concatenate([np.eye(P), np.ones((P, P)), (i[:, None] // HS == i // HS) * 1.0, inv], 1)
    s, t = i[:, None], i[None, :]
    same = s // CH == t // CH
    strict, incl = same & (s < t), same & (s <= t)
    levels = [(t // b % 2 == 1) & (s // b == t // b - 1) for b in LEVELS]
    mask = np.concatenate([strict, strict, incl, incl] + levels + [s // HS == t // HS], 1)
    return [np.ascontiguousarray(a, dtype=np.float32) for a in (cs, chan, const, mask)]


def kernel(**inputs):
    import concourse.bacc as bacc
    from concourse.bass_utils import run_bass_kernel_spmd

    g = {k: np.asarray(a) for k, a in inputs.items()}
    cs, chan, const, mask = _tables()
    w_in = g["w_in_2"][0]
    mu = np.zeros(1600 + P, np.float32)
    mu[:g["mu_shift_2"].shape[1]] = g["mu_shift_2"][0]
    eps = np.full((P, 1), EPS, np.float32)
    vec = np.concatenate(
        [_columns(g["c"][0]), _columns(g["b_mod"][0]), _columns(g["g_norm_mix"][0]), _columns(g["g_norm_ffn"][0]),
         _columns(g["w_ffn_conv"][0]), _columns(g["b_ffn_conv"][0]), _columns(g["ffn1_norm_2"][0]), _columns(g["mix_norm_2"][0])]
        + [_columns(mu[s:s + P]) for s in IN_STARTS_RW]
        + [_columns(g[n][0]) for n in ("w0_2", "a0_2", "k_k_2", "k_a_2", "r_k_2", "ln_w_2", "ln_b_2", "pool_scale_2", "ffn2_norm_2")]
        + [_columns(g["g_final"]), _columns(g["final_norm_2"]), eps, np.full((P, 1), GN_EPS, np.float32)], 1)

    def gated(a, b):
        return np.stack([_by_output(a), _by_output(b)], 1).reshape(-1, P, D)

    up = g["w_ffn_up"][0]
    units = np.concatenate(
        [chan[None], _by_output(g["w_fnet_out"][0]), gated(up[:, :F], up[:, F:]), g["w_ffn_down"][0].reshape(FT, P, D),
         gated(g["ffn1_w_gate_2"][0], g["ffn1_w_up_2"][0]), g["ffn1_w_down_2"][0].reshape(FT, P, D)]
        + [_by_output(w_in[:, s:s + P]) for s in IN_STARTS]
        + [_by_output(g["w_out_2"][0]), gated(g["ffn2_w_gate_2"][0], g["ffn2_w_up_2"][0]), g["ffn2_w_down_2"][0].reshape(FT, P, D)])
    w_mod = g["w_mod"][0].reshape(KT, P, 6, D).transpose(2, 0, 1, 3).reshape(6 * KT, P, D)
    lora = np.zeros((P, 3, RW), np.float32)
    lora[0:32, 0] = g["w_lora_up_2"][0]
    lora[32:64, 1] = g["a_lora_up_2"][0]
    lora[0:96, 2] = g["g_lora_up_2"][0]
    x = g["x"][0]
    arrays = {
        "vectors": vec, "constants": const, "masks": mask, "tokens": x, "tokens_by_channel": x.T.reshape(KT, P, T).transpose(1, 0, 2),
        "seq_transform": cs, "mod_units": w_mod, "weight_units": units, "low_rank": lora,
        "pool_weights": g["w_pool_2"][0].transpose(1, 0, 2),
    }
    arrays = {k: np.ascontiguousarray(a) for k, a in arrays.items()}
    nc = bacc.Bacc("TRN2", target_bir_lowering=False, num_devices=1)
    args = [nc.dram_tensor(k, a.shape, mybir.dt.from_np(a.dtype), kind="ExternalInput").ap() for k, a in arrays.items()]
    result = nc.dram_tensor("result", (D, T), mybir.dt.float32, kind="ExternalOutput").ap()
    build(nc, *args, result)
    r = run_bass_kernel_spmd(nc, [arrays], core_ids=[0])
    return np.ascontiguousarray(r.results[0]["result"].T).reshape(1, T, D)
```

```python
from contextlib import ExitStack

import numpy as np
import concourse.bass as bass
from concourse import mybir

P = 128
T = 512
D = 1024
KT = D // P
F = 2816
FT = F // P
TT_ = T // P
FG = 256
NCOS = T // 2 + 2
NSIN = T // 2
NF = NCOS + NSIN
RW = 512
HS = 64
PAIRS = RW // P
CH = 64
NCH = T // CH
NCP = NCH // 2
EPS = 1e-6
GN_EPS = 64e-5
L2_EPS = 1e-12
KAPPA = float(np.exp(-0.5))
WINDOWS = (2, 4, 8, 16)
PADW = 16
LEVELS = (1, 2, 4, 8, 16, 32)

IN_STARTS_RW = [1536, 1600] + [s + P * p for p in range(PAIRS) for s in (512, 0, 1024)]
IN_STARTS = IN_STARTS_RW + [1696 + P * g for g in range(len(WINDOWS))]
U_DFT = 0
U_FNET = 1
U_UP0 = U_FNET + KT
U_DN0 = U_UP0 + 2 * FT
U_UP1 = U_DN0 + FT
U_DN1 = U_UP1 + 2 * FT
U_IN = U_DN1 + FT
U_OUT = U_IN + len(IN_STARTS)
U_UP2 = U_OUT + KT
U_DN2 = U_UP2 + 2 * FT
NU = U_DN2 + FT
RING = 4
AHEAD = 3

VEC = {}
NVEC = 0
for _name, _n in (("c", KT), ("b_mod", 6 * KT), ("g_mix", KT), ("g_ffn", KT), ("conv", 3 * FT), ("b_conv", FT),
                  ("g_ffn1", KT), ("g_in", KT), ("mu", len(IN_STARTS_RW)), ("w0", PAIRS), ("a0", PAIRS),
                  ("k_k", PAIRS), ("k_a", PAIRS), ("r_k", PAIRS), ("ln_w", PAIRS), ("ln_b", PAIRS),
                  ("pool_scale", len(WINDOWS)), ("g_ffn2", KT), ("g_mid", KT), ("g_last", KT), ("eps", 1), ("gn_eps", 1)):
    VEC[_name] = NVEC
    NVEC += _n
NCONST = 3 * P + len(WINDOWS) * PADW
NMASK = 4 * P + len(LEVELS) * P + P

INVERT = range(2, len(LEVELS) + 1)
LAST = len(LEVELS)


def fnet_bank(m):
    return 6 if m == 0 else (m - 1) % 4


class Buffers:

    def __init__(self, bank, MB, MK, planes, TT, T, U, X, AA, BT, KT, VT, MT, GH, S, RP, y, ysq, OV, sd):
        self.bank, self.MB, self.MK, self.planes, self.TT, self.T = bank, MB, MK, planes, TT, T
        self.U, self.X, self.AA, self.BT, self.KT, self.VT = U, X, AA, BT, KT, VT
        self.MT, self.GH, self.S, self.RP, self.y, self.ysq, self.OV, self.sd = MT, GH, S, RP, y, ysq, OV, sd


def _per_level(inner, outer):
    return [x.format(n=n) for n in INVERT for x in inner + (outer if n < LAST else [])]


PE_STEPS = (["tA", "tB", "tK", "tV"] + [f"L{i}" for i in range(NCP)] + [f"K{i}" for i in range(NCP)] + ["t1a", "t1b"]
            + _per_level(["U{n}a", "U{n}b", "D{n}a", "D{n}b"], ["t{n}a", "t{n}b"])
            + ["AV", "GHa", "GHb", "RP", "OV", "MTa", "MTb", "Na", "Nb"] + [f"S{c}" for c in range(1, NCH - 1)]
            + ["Y", "mean", "var"])
VE_STEPS = (["tB"] + [f"L{i}" for i in range(NCP)] + [f"K{i}" for i in range(NCP)] + ["D1a", "D1b", "t1b"]
            + _per_level(["D{n}a", "D{n}b"], ["t{n}b"])
            + ["GHb", "RP", "MTa", "MTb", "Na", "Nb"] + [f"S{c}" for c in range(1, NCH - 1)]
            + ["Y", "yc", "yn", "out"])
AC_STEPS = (["planes", "tA", "tK", "tV", "t1a"] + _per_level(["U{n}a", "U{n}b"], ["t{n}a"])
            + ["AV", "GHa", "OV", "sq", "sd", "affine"])
PO_STEPS = ["zero"] + [f"X{n}" for n in INVERT]


def at(steps, pair, name):
    return pair // 2 * len(steps) + steps.index(name) + 1


def in_turns(pair_program):
    for first in range(0, PAIRS, 2):
        for _ in zip(pair_program(first), pair_program(first + 1)):
            pass


def build(nc, a_vec, a_const, a_mask, a_x, a_xt, a_cs, a_wmod, a_w, a_lora, a_pool, out):
    f32, f32r = mybir.dt.float32, mybir.dt.float32r
    ACT = mybir.ActivationFunctionType
    ALU = mybir.AluOpType
    MUL, ADD, SUB, MAX = ALU.mult, ALU.add, ALU.subtract, ALU.max

    with ExitStack() as ctx:
        lo_edge = (nc.sbuf_base + 63) // 64 * 64
        place = [lo_edge]

        def reserve(n_floats):
            o = place[0]
            place[0] += (4 * n_floats + 31) // 32 * 32
            return o

        def view(name, shape, offset, dt=f32):
            return nc.alloc_sbuf_tensor_at(name, shape, dt, offset=offset)

        def fresh(name, shape, dt=f32):
            return view(name, shape, reserve(int(np.prod(shape[1:]))), dt)

        raw = fresh("raw", [P, RING, D])
        o_whi, o_wlo = reserve(RING * D), reserve(RING * D)
        w_hi = view("w_hi", [P, RING, D], o_whi, f32r)
        w_lo = view("w_lo", [P, RING, D], o_wlo, f32r)
        xT = fresh("xT", [P, KT, T])
        o_act = reserve(2 * KT * T)
        act_hi = view("act_hi", [P, KT, T], o_act, f32r)
        act_lo = view("act_lo", [P, KT, T], o_act + 4 * KT * T, f32r)
        o_hid = reserve(2 * FT * T)
        hid_hi = view("hid_hi", [P, FT * T], o_hid, f32r)
        hid_lo = view("hid_lo", [P, FT * T], o_hid + 4 * FT * T, f32r)
        o_misc = reserve(3 * D)
        o_acc = reserve(D)
        sumsq = fresh("sumsq", [P, T])
        o_rstd = reserve(T)
        rstd = view("rstd", [P, T], o_rstd)
        vec = fresh("vec", [P, NVEC])
        const = fresh("const", [P, NCONST])
        mods = fresh("mods", [P, 6 * KT])
        small = fresh("small", [P, 64])
        assert place[0] <= nc.sbuf_usable_end, (place[0], nc.sbuf_usable_end)

        ident, ones, bones = const[:, 0:P], const[:, P:2 * P], const[:, 2 * P:3 * P]
        inv_count = const[:, 3 * P:]
        c_silu, gain, sh_dc = small[:, 0:8], small[:, 8:16], small[:, 16:24]
        x_ss, gain2, one_minus_ka, g_both = small[:, 24:28], small[:, 28:36], small[:, 36:40], small[:, 40:48]
        y_dc = small[:, 48:56]

        def v(name, i=0, n=1):
            return vec[:, VEC[name] + i:VEC[name] + i + n]

        def mod(which, m):
            return mods[:, which * KT + m:which * KT + m + 1]

        SH1, SC1, GT1, SH2, SC2, GT2 = range(6)

        x_tok = view("x_tok", [P, TT_, D], o_act)
        cs_raw = view("cs_raw", [P, TT_, NF], o_act + 4 * TT_ * D)
        y_raw = view("y_raw", [P, KT, NF], o_act)
        xn_hi, xn_lo = hid_hi[:, 0:TT_ * D], hid_lo[:, 0:TT_ * D]
        cs_hi, cs_lo = (h[:, TT_ * D:TT_ * (D + NF)] for h in (hid_hi, hid_lo))
        y_hi, y_lo = (h[:, TT_ * (D + NF):TT_ * (D + NF) + KT * NF] for h in (hid_hi, hid_lo))
        f_buf = view("f_buf", [P, 2, T], o_hid)
        q_buf = view("q_buf", [P, 2, NSIN], o_hid + 4 * 2 * T)
        sq_buf = view("sq_buf", [P, KT, T], o_hid)
        sq_mid = view("sq_mid", [P, KT, T], o_hid + 4 * KT * T)
        wm_ring = view("wm_ring", [P, 3, D], o_misc)
        mod_acc = view("mod_acc", [P, D], o_acc)
        junk = view("junk", [P, D], o_hid + 4 * FT * T + 4 * TT_ * (D + NF))

        g_buf = view("g_buf", [P, 2, T], o_misc)
        u_buf = view("u_buf", [P, 2, T], o_misc + 4 * 2 * T)
        t_buf = view("t_buf", [P, 2, T], o_hid + 4 * 8 * T)
        a_buf = view("a_buf", [P, 2, T], o_hid + 4 * 10 * T)
        o_tb = o_misc + 4 * 4 * T

        def tiles(name, first, n=1):
            return view(name, [P, n, T], o_hid + 4 * T * first)

        rA, rR, rB, rK = (tiles(n, 4 * i, 4) for i, n in enumerate(("rA", "rR", "rB", "rK")))
        rV, rBonus, rG = tiles("rV", 16, 4), tiles("rBonus", 20, 4), tiles("rG", 24, 4)
        pooled = tiles("pooled", 28, 4)
        pk, sg, ag, cs, iv, nr, sq = (tiles(n, 32 + i) for i, n in enumerate(("pk", "sg", "ag", "cs", "iv", "nr", "sqk")))
        wa, gx, scan_mask = tiles("wa", 39), tiles("gx", 40), tiles("scan_mask", 41)
        pads = view("pads", [P, 2, T + 4], o_misc + 4 * T)
        diff = view("diff", [P, T], o_misc)
        lora = view("lora", [P, 2, RW], o_acc)
        g_lora = view("g_lora", [P, RW], o_tb)
        w_pool = view("w_pool", [P, len(WINDOWS), P], o_tb + 4 * T)
        pool_a = view("pool_a", [P, PADW + T], o_misc)
        pool_b = view("pool_b", [P, PADW + T], o_hid + 4 * T * 42)
        pool_c = view("pool_c", [P, PADW + T], o_hid + 4 * T * 32)
        pchunk = fresh("pchunk", [P, PAIRS, NCH])
        assert place[0] <= nc.sbuf_usable_end, (place[0], nc.sbuf_usable_end)

        act_out = view("act_out", [P, KT, T], o_act)

        def half_set(n, **places):
            def w(name, shape):
                return view(f"{name}{n}", shape, places[name])
            return Buffers(
                MB=w("MB", [P, NCP, 4, P]), MK=w("MK", [P, NCP, 4, P]), planes=w("planes", [P, NCP, 4, P]), TT=w("TT", [P, NCP, 2, P]),
                T=w("T", [P, NCP, 2, P]), U=w("U", [P, NCP, 2, P]), X=w("X", [P, NCP, 2, P]), AA=w("AA", [P, NCP, 2, P]),
                BT=w("BT", [P, T]), KT=w("KT", [P, T]), VT=w("VT", [P, T]),
                MT=view(f"MT{n}", [P, NCH, P], places["planes"]), GH=view(f"GH{n}", [P, 2, 2 * NCP, HS], places["planes"] + 8 * T),
                S=view(f"S{n}", [P, NCH, P], places["U"]), RP=view(f"RP{n}", [P, T], places["X"]),
                y=view(f"y{n}", [P, T], places["T"]), ysq=view(f"ysq{n}", [P, T], places["T"] + 4 * T),
                OV=view(f"OV{n}", [P, T], places["AA"]), sd=view(f"sd{n}", [P, T], places["AA"] + 4 * T), bank=4 * n)

        t4 = 4 * T
        sets = [half_set(0, MB=o_act, MK=o_act + 4 * t4, planes=o_act + 8 * t4, TT=o_hid + 32 * t4, T=o_hid + 34 * t4, U=o_hid + 36 * t4,
                         X=o_hid + 38 * t4, AA=o_hid + 40 * t4, BT=o_act + 12 * t4, KT=o_act + 13 * t4, VT=o_act + 14 * t4),
                half_set(1, MB=o_whi, MK=o_whi + 4 * t4, planes=o_wlo, TT=o_wlo + 4 * t4, T=o_wlo + 6 * t4, U=o_hid + 42 * t4,
                         X=o_misc, AA=o_misc + 2 * t4, BT=o_misc + 4 * t4, KT=o_act + 15 * t4, VT=o_rstd)]
        mask4 = sumsq
        mask_lv = view("mask_lv", [P, len(LEVELS) + 1, P], o_acc)
        mask_bd = mask_lv[:, len(LEVELS), :]

        ps = ctx.enter_context(nc.psum_tensor("ps", [P, 8, T], f32))

        sems = {}

        def sem(name):
            if name not in sems:
                sems[name] = ctx.enter_context(nc.semaphore(name))
            return sems[name]

        raw_full = [sem(f"raw_full{i}") for i in range(RING)]
        wm_full = [sem(f"wm_full{i}") for i in range(3)]
        hi_done, lo_done = sem("hi_done"), sem("lo_done")
        unit_used = sem("unit_used")
        for n in ("loaded_vec", "loaded_const", "loaded_cs", "loaded_xt", "loaded_lora", "loaded_masks"):
            sem(n)
        tensor_step, vector_step, scalar_step, pool_step = ([sem(f"{e}_step{i}") for i in range(2)] for e in ("tensor", "vector", "scalar", "pool"))
        v_chain, a_chain = sem("v_chain"), sem("a_chain")
        block = ctx.enter_context(nc.Block())

        def step_waits(eng, p):
            def on(sems_, steps):
                return lambda name: eng.wait_ge(sems_[p % 2], at(steps, p, name))
            return on(tensor_step, PE_STEPS), on(vector_step, VE_STEPS), on(scalar_step, AC_STEPS), on(pool_step, PO_STEPS)

        def ffn_sems(s):
            return {n: sem(f"f{s}_{n}") for n in ("gate_read", "act_in", "silu", "val_read", "hid", "hid_hi", "hid_lo", "c1", "c2",
                                                  "down_tile", "x_new", "nx_hi", "nx_sq", "nx_lo", "nx_sum", "stat", "sd", "rstd")}

        @block.sync
        def _(sp):
            sp.dma_start(vec[:, :], a_vec).then_inc(sem("loaded_vec"), 16)
            for t in range(TT_):
                sp.dma_start(x_tok[:, t, :], a_x[t * P:(t + 1) * P, :]).then_inc(sem(f"loaded_x{t}"), 16)
            sp.dma_start(cs_raw[:, :, :], a_cs).then_inc(sem("loaded_cs"), 16)
            sp.dma_start(const[:, :], a_const).then_inc(sem("loaded_const"), 16)

            def load_unit(u, slot, turn):
                sp.dma_start(raw[:, slot, :], a_w[u]).then_inc(raw_full[slot], 16)

            def load_wm(i):
                if i >= 3:
                    sp.wait_ge(sem("wm_used"), i - 2)
                sp.dma_start(wm_ring[:, i % 3, :], a_wmod[i]).then_inc(wm_full[i % 3], 16)

            u = 0
            for i in range(6 * KT):
                load_wm(i)
                if i == 3:
                    sp.dma_start(xT[:, :, :], a_xt).then_inc(sem("loaded_xt"), 16)
                if i in (10, 16, 17, 18) or (i > 19 and i % 3 == 0):
                    if u >= RING:
                        sp.wait_ge(lo_done, u - RING + 1)
                    load_unit(u, u % RING, 0)
                    u += 1

            def load_through(first, last):
                n = first
                while n % RING and n < last:
                    sp.wait_ge(lo_done, n - RING + 1)
                    load_unit(n, n % RING, 0)
                    n += 1
                turns = (last - n) // RING
                if turns > 1:
                    with sp.Fori(0, turns) as i:
                        for j in range(RING):
                            sp.wait_ge(lo_done, i * RING + (n + j - RING + 1))
                            sp.dma_start(raw[:, j, :], a_w[bass.ds(i * RING + (n + j), 1)].rearrange("a p n -> p (a n)")).then_inc(raw_full[j], 16)
                    n += turns * RING
                while n < last:
                    sp.wait_ge(lo_done, n - RING + 1)
                    load_unit(n, n % RING, 0)
                    n += 1

            load_through(u, U_UP0 + 8)
            sp.wait_ge(sem("mod_mm"), 6)
            sp.dma_start(lora[:, :, :], a_lora[:, 0:2, :]).then_inc(sem("loaded_lora"), 16)
            sp.dma_start(g_lora[:, :], a_lora[:, 2, :]).then_inc(sem("loaded_lora"), 16)
            sp.dma_start(w_pool[:, :, :], a_pool).then_inc(sem("loaded_lora"), 16)
            load_through(U_UP0 + 8, U_OUT + 2)
            sp.wait_ge(sem("za_read"), PAIRS)
            sp.wait_ge(sem("in_read"), len(IN_STARTS))
            sp.dma_start(mask4[:, :], a_mask[:, 0:4 * P]).then_inc(sem("loaded_masks"), 16)
            sp.dma_start(mask_lv[:, :, :], a_mask[:, 4 * P:].rearrange("p (l t) -> p l t", t=P)).then_inc(sem("loaded_masks"), 16)
            load_through(U_OUT + 2, NU)
            for m in range(KT):
                sp.wait_ge(sem("y_out"), m + 1)
                sp.dma_start(out[m * P:(m + 1) * P, :], act_out[:, m, :]).then_inc(sem("stored"), 16)
            sp.wait_ge(sem("stored"), 16 * KT)

        @block.gpsimd
        def _(pool):
            def low(u, slot):
                pool.wait_ge(hi_done, u + 1)
                nc.gpsimd.tensor_tensor(w_lo[:, slot, :], raw[:, slot, :], w_hi[:, slot, :].bitcast(f32), SUB).then_inc(lo_done, 1)

            def low_through(first, last):
                assert first % RING == 0
                with pool.Fori(0, (last - first) // RING) as i:
                    for j in range(RING):
                        low(i * RING + (first + j), j)
                for u in range(first + (last - first) // RING * RING, last):
                    low(u, u % RING)

            low_through(0, U_OUT)
            u_next = U_OUT

            n_step = [0, 0]

            def pair(p):
                pe_did, ve_did, ac_did, _ = step_waits(pool, p)
                b = sets[p % 2]

                def did(name, ins):
                    n_step[p % 2] += 1
                    assert at(PO_STEPS, p, name) == n_step[p % 2]
                    ins.then_inc(pool_step[p % 2], 1)

                if p >= 2:
                    pool.wait_ge(vector_step[p % 2], at(VE_STEPS, p - 2, "out"))
                else:
                    pool.wait_ge(sem("in_done"), 1)
                for h in range(2):
                    other = slice((1 - h) * HS, (2 - h) * HS)
                    for k in (0, 2):
                        ins = nc.gpsimd.memset(b.planes[other, :, k + h, :], 0.0)
                        if (h, k) != (1, 2):
                            n_chain[0] += 1
                            ins.then_inc(sem("pool_chain"), 1)
                            pool.wait_ge(sem("pool_chain"), n_chain[0])
                did("zero", ins)
                yield
                for n in INVERT:
                    if n == 2:
                        ve_did(f"L{NCP - 1}")
                    else:
                        pe_did(f"U{n - 1}b")
                    for c in range(NCP):
                        ins = nc.gpsimd.tensor_tensor(b.X[:, c, :, :], b.MB[:, c, 0:2, :], mask_lv[:, n - 1:n, :].to_broadcast([P, 2, P]), MUL)
                        if c < NCP - 1:
                            n_chain[0] += 1
                            ins.then_inc(sem("pool_chain"), 1)
                    did(f"X{n}", ins)
                    yield

            n_chain = [0]
            pool.wait_ge(sem("loaded_masks"), 32)
            in_turns(pair)
            while u_next % RING:
                low(u_next, u_next % RING)
                u_next += 1
            low_through(u_next, NU)

        @block.scalar
        def _(act):
            def after(s, n):
                act.wait_ge(s, n)

            def high(u, slot, turn, first=False):
                act.wait_ge(raw_full[slot], 16 * (turn + 1))
                if not first:
                    act.wait_ge(unit_used, u - RING + 1)
                nc.scalar.activation(w_hi[:, slot, :], raw[:, slot, :], ACT.Copy).then_inc(hi_done, 1)

            def high_n(u):
                if u < NU:
                    high(u, u % RING, u // RING, u < RING)

            n_chain = [0]

            def chain(ins):
                n_chain[0] += 1
                ins.then_inc(a_chain, 1)
                act.wait_ge(a_chain, n_chain[0])

            after(sem("loaded_vec"), 16)
            nc.scalar.activation(c_silu, v("c", 0, KT), ACT.Silu).then_inc(sem("c_silu"), 1)
            for t in range(TT_):
                after(sem(f"loaded_x{t}"), 16)
                chain(nc.scalar.activation(junk[:, :], x_tok[:, t, :], ACT.Square, accum_out=x_ss[:, t:t + 1]))
            nc.scalar.activation(x_ss, x_ss, ACT.Sqrt, bias=v("eps"), scale=1.0 / D).then_inc(sem("x_sd"), 1)
            after(sem("loaded_cs"), 16)
            nc.scalar.activation(cs_hi, cs_raw[:, :, :].rearrange("p a b -> p (a b)"), ACT.Copy).then_inc(sem("cs_hi"), 1)
            after(sem("x_rstd"), 1)
            for t in range(TT_):
                nc.scalar.activation(xn_hi[:, t * D:(t + 1) * D], x_tok[:, t, :], ACT.Copy, scale=x_ss[:, t:t + 1]).then_inc(sem("xn_hi"), 1)
            after(sem("cs_lo"), 1)
            for m in range(KT):
                b = 2 * (m % 3)
                after(sem("seq_mm"), m + 1)
                nc.scalar.activation(y_raw[:, m, 0:NCOS], ps[:, b, 0:NCOS], ACT.Copy).then_inc(sem("y_raw"), 1)
                nc.scalar.activation(y_raw[:, m, NCOS:NF], ps[:, b + 1, 0:NSIN], ACT.Copy).then_inc(sem("y_raw"), 1)
            for u in range(AHEAD):
                high_n(u)
            after(sem("dc"), 1)
            nc.scalar.activation(y_hi.rearrange("p (m f) -> p m f", f=NF)[:, :, 0], y_dc, ACT.Copy).then_inc(sem("dc_hi"), 1)
            for m in range(KT):
                nc.scalar.activation(y_hi[:, m * NF + 1:(m + 1) * NF], y_raw[:, m, 1:NF], ACT.Copy, scale=gain[:, m:m + 1]).then_inc(sem("y_hi"), 1)
            high_n(AHEAD)
            for t in range(KT):
                after(sem("chan_mm"), t + 1)
                nc.scalar.activation(q_buf[:, t % 2, :], ps[:, 2 * (t % 3) + 1, 0:NSIN], ACT.Copy).then_inc(sem("q_new"), 1)
                after(sem("f_new"), t + 1)
                nc.scalar.activation(act_hi[:, t, :], f_buf[:, t % 2, :], ACT.Copy).then_inc(sem("f_hi"), 1)

            def squares(s_new, s_sq, m, dst, ready=None):
                after(s_new, m + 1)
                if ready is not None:
                    after(*ready)
                nc.scalar.activation(dst, xT[:, m, :], ACT.Square).then_inc(s_sq, 1)

            for m in range(KT):
                high_n(U_FNET + m + AHEAD)
                squares(sem("x0_new"), sem("x0_sq"), m, sumsq[:, :] if m == 0 else sq_buf[:, m, :])

            def root(s_stat, s_sd):
                after(s_stat, 1)
                nc.scalar.activation(rstd[:, :], ps[:, 6, :], ACT.Sqrt, bias=v("eps"), scale=1.0 / D).then_inc(s_sd, 1)

            root(sem("x0_stat"), sem("x0_sd"))
            for m in range(KT):
                after(sem("t_new"), m + 1)
                if m >= 2:
                    after(sem("a_lo"), m - 1)
                nc.scalar.activation(a_buf[:, m % 2, :], t_buf[:, m % 2, :], ACT.Identity, bias=mod(SH2, m), scale=gain2[:, m:m + 1]).then_inc(sem("a_new"), 1)
                after(sem("a_new"), m + 1)
                nc.scalar.activation(act_hi[:, m, :], a_buf[:, m % 2, :], ACT.Copy).then_inc(sem("a_hi"), 1)

            def ffn(stage, u_up, u_dn):
                s = ffn_sems(stage)

                def up_pair(i, first):
                    for q in range(2):
                        j = 2 * i + q
                        for h in range(2):
                            off = u_up + 2 * q + h + AHEAD
                            high(4 * i + off, off % RING, i + off // RING)
                        if stage == 0:
                            act.wait_ge(unit_used, u_up + 2 * j + 1)
                            if not first:
                                act.wait_ge(s["hid_lo"], j - 1)
                            nc.scalar.activation(g_buf[:, q, :], ps[:, 2 * q, :], ACT.Identity, bias=b_conv(j), scale=tap(1, j)).then_inc(s["c1"], 1)
                        act.wait_ge(s["act_in"], j + 1)
                        nc.scalar.activation(g_buf[:, q, :], g_buf[:, q, :], ACT.Silu).then_inc(s["silu"], 1)
                        act.wait_ge(s["hid"], j + 1)
                        nc.scalar.activation(hid_hi[:, bass.ds(j * T, T)], g_buf[:, q, :], ACT.Copy).then_inc(s["hid_hi"], 1)

                up_pair(0, True)
                with act.Fori(1, FT // 2) as i:
                    up_pair(i, False)
                for kt in range(FT):
                    high_n(u_dn + kt + AHEAD)

            def b_conv(j):
                return vec[:, bass.ds(VEC["b_conv"] + j, 1)]

            def tap(k, j):
                return vec[:, bass.ds(VEC["conv"] + k * FT + j, 1)]

            def next_input(s, m, g):
                after(s["x_new"], m + 1)
                nc.scalar.activation(act_hi[:, m, :], xT[:, m, :], ACT.Copy, scale=v(g, m)).then_inc(s["nx_hi"], 1)
                nc.scalar.activation(sumsq[:, :] if m == 0 else sq_buf[:, m, :], xT[:, m, :], ACT.Square).then_inc(s["nx_sq"], 1)

            after(sem("wm_used"), 6 * KT)
            ffn(0, U_UP0, U_DN0)
            s0 = ffn_sems(0)
            after(sem("g_both"), 1)
            for m in range(KT):
                after(s0["x_new"], m + 1)
                nc.scalar.activation(act_hi[:, m, :], xT[:, m, :], ACT.Copy, scale=g_both[:, m:m + 1]).then_inc(s0["nx_hi"], 1)
                nc.scalar.activation(sumsq[:, :] if m == 0 else sq_buf[:, m, :], xT[:, m, :], ACT.Square).then_inc(s0["nx_sq"], 1)
                nc.scalar.activation(sq_mid[:, m, :], xT[:, m, :], ACT.Square, scale=v("g_mid", m)).then_inc(s0["nx_sq"], 1)
            after(s0["stat"], 1)
            nc.scalar.activation(sumsq[:, :], ps[:, 6, :], ACT.Sqrt, bias=v("eps"), scale=1.0 / D).then_inc(s0["sd"], 1)
            after(sem("mid_ms"), 1)
            nc.scalar.activation(rstd[:, :], rstd[:, :], ACT.Sqrt).then_inc(sem("mid_sd"), 1)
            ffn(1, U_UP1, U_DN1)
            s1 = ffn_sems(1)
            for m in range(KT):
                next_input(s1, m, "g_in")
            root(s1["stat"], s1["sd"])

            for i in range(len(IN_STARTS)):
                if U_IN + i + AHEAD < U_OUT:
                    high_n(U_IN + i + AHEAD)
                if i == 0:
                    after(sem("in_read"), 1)
                    nc.scalar.activation(wa[0:32, 0, :], wa[0:32, 0, :], ACT.Tanh).then_inc(sem("wa_ready"), 1)
                if i == 1:
                    after(sem("in_read"), 2)
                    nc.scalar.activation(gx[:, 0, :], gx[:, 0, :], ACT.Sigmoid).then_inc(sem("g_in"), 1)
                if 2 <= i < 2 + 3 * PAIRS and (i - 2) % 3 == 2:
                    p = (i - 2) // 3
                    after(sem("za_mm"), p + 1)
                    if p:
                        after(sem("prep"), p)
                    chain(nc.scalar.activation(sg[:, 0, :], ps[:, 4, :], ACT.Sigmoid, bias=v("w0", p)))
                    nc.scalar.activation(ag[:, 0, :], ps[:, 5, :], ACT.Sigmoid, bias=v("a0", p)).then_inc(sem("za_read"), 1)
                    after(sem("in_read"), 3 + 3 * p)
                    nc.scalar.activation(sq[:, 0, :], pk[:, 0, :], ACT.Square, scale=v("k_k", p)).then_inc(sem("sq_ready"), 1)
                    after(sem("ss_mm"), p + 1)
                    nc.scalar.activation(nr[:, 0, :], ps[:, 6, :], ACT.Sqrt).then_inc(sem("nr_ready"), 1)
                    after(sem("cs_ready"), p + 1)
                    chain(nc.scalar.activation(iv[:, 0, :], cs[:, 0, :], ACT.Exp, scale=KAPPA))
                    chain(nc.scalar.activation(sg[:, 0, :], sg[:, 0, :], ACT.Exp, scale=-KAPPA))
                    nc.scalar.activation(cs[:, 0, :], cs[:, 0, :], ACT.Exp, scale=-KAPPA).then_inc(sem("exps"), 1)
                    after(sem("g_mm"), p + 1)
                    nc.scalar.activation(rG[:, p, :], ps[:, 7, :], ACT.Copy).then_inc(sem("g_read"), 1)
            n_step = [0, 0]

            def pair(p):
                pe_did, ve_did, ac_did, po_did = step_waits(act, p)
                b = sets[p % 2]

                def did(name, ins):
                    n_step[p % 2] += 1
                    assert at(AC_STEPS, p, name) == n_step[p % 2], name
                    ins.then_inc(scalar_step[p % 2], 1)

                def copy(name, dst, bank, *pattern, **sizes):
                    pe_did(name)
                    src = ps[:, b.bank + bank, :]
                    did(name, nc.scalar.activation(dst, src.rearrange(*pattern, **sizes) if pattern else src, ACT.Copy))

                def squares_out(name, dst, half, bank):
                    copy(name, dst[:, slice(0, 2) if half == "a" else slice(2, 4), :, :], bank, "q (c h t) -> q c h t", c=2, h=2)

                po_did("zero")
                for k, src in ((0, rA), (2, rR)):
                    for h in range(2):
                        r = slice(h * HS, (h + 1) * HS)
                        ins = nc.scalar.activation(b.planes[r, :, k + h, :], src[r, p, :].rearrange("q (c t) -> q c t", t=P), ACT.Copy)
                        if (k, h) != (2, 1):
                            chain(ins)
                did("planes", ins)
                copy("tA", b.AA[:, :, :, 0:HS], 0, "q (c h k) -> q c h k", c=NCP, h=2)
                copy("tK", b.KT[:, :], 2)
                copy("tV", b.VT[:, :], 3)
                yield
                yield
                squares_out("t1a", b.T, "a", 0)
                yield
                for n in INVERT:
                    squares_out(f"U{n}a", b.U, "a", 2)
                    squares_out(f"U{n}b", b.U, "b", 3)
                    yield
                    yield
                    if n < LAST:
                        squares_out(f"t{n}a", b.T, "a", 2)
                        yield
                copy("AV", b.AA[:, :, :, HS:P], 2, "q (c h k) -> q c h k", c=NCP, h=2)
                yield
                copy("GHa", b.GH[:, :, 0:4, :], 0, "q (s g k) -> q g s k", s=4, g=2)
                yield
                copy("OV", b.OV[:, :], 2)
                yield
                yield
                for _ in range(1, NCH - 1):
                    yield
                yield
                ve_did("yc")
                did("sq", nc.scalar.activation(b.ysq[:, :], b.y[:, :], ACT.Square))
                yield
                pe_did("var")
                did("sd", nc.scalar.activation(b.sd[:, :], ps[:, b.bank + 1, :], ACT.Sqrt, bias=v("gn_eps"), scale=1.0 / HS))
                yield
                ve_did("yn")
                did("affine", nc.scalar.activation(b.y[:, :], b.y[:, :], ACT.Identity, bias=v("ln_b", p), scale=v("ln_w", p)))
                yield

            in_turns(pair)
            for q in range(2):
                act.wait_ge(vector_step[q], at(VE_STEPS, PAIRS - 2 + q, "out"))
            for u in range(U_OUT, U_OUT + AHEAD):
                high_n(u)
            for p in range(PAIRS):
                nc.scalar.activation(act_hi[:, p, :], rG[:, p, :], ACT.Copy).then_inc(sem("mix_hi"), 1)
            for g in range(len(WINDOWS)):
                after(sem("pool_mm"), g + 1)
                nc.scalar.activation(act_hi[:, PAIRS + g, :], ps[:, g, :], ACT.Copy, scale=v("pool_scale", g)).then_inc(sem("pool_hi"), 1)

            for m in range(KT):
                high_n(U_OUT + m + AHEAD)
                squares(sem("x2_new"), sem("x2_sq"), m, sumsq[:, :] if m == 0 else sq_buf[:, m, :])
            for m in range(KT):
                nc.scalar.activation(act_hi[:, m, :], xT[:, m, :], ACT.Copy, scale=v("g_ffn2", m)).then_inc(sem("x2_hi"), 1)
            root(sem("x2_stat"), sem("x2_sd"))
            ffn(2, U_UP2, U_DN2)
            s2 = ffn_sems(2)
            for m in range(KT):
                squares(s2["x_new"], s2["nx_sq"], m, sumsq[:, :] if m == 0 else sq_buf[:, m, :])
            root(s2["stat"], s2["sd"])

        @block.vector
        def _(ve):
            after = ve.wait_ge
            count = {}

            def chain(ins, name=None):
                s = v_chain if name is None else sem(name)
                count[name] = count.get(name, 0) + 1
                ins.then_inc(s, 1)
                ve.wait_ge(s, count[name])

            def tt(o, a, b, op, name=None):
                chain(nc.vector.tensor_tensor(o, a, b, op), name)

            def stt(o, a, s, b, op0, op1, name=None):
                chain(nc.vector.scalar_tensor_tensor(o, a, s, b, op0, op1), name)

            def tsc(o, a, s1, s2, op0, op1, name=None):
                chain(nc.vector.tensor_scalar(o, a, s1, s2, op0, op1), name)

            after(sem("x_sd"), 1)
            chain(nc.vector.reciprocal(x_ss, x_ss), "x_rstd")
            after(sem("cs_hi"), 1)
            tt(cs_lo, cs_raw[:, :, :].rearrange("p a b -> p (a b)"), cs_hi.bitcast(f32), SUB, "cs_lo")
            for t in range(TT_):
                after(sem("xn_hi"), t + 1)
                stt(xn_lo[:, t * D:(t + 1) * D], x_tok[:, t, :], x_ss[:, t:t + 1], xn_hi[:, t * D:(t + 1) * D].bitcast(f32), MUL, SUB, "xn_lo")
            after(sem("c_silu"), 1)

            def wm(i):
                vv, k = divmod(i, KT)
                after(wm_full[i % 3], 16 * (i // 3 + 1))
                if k == 0:
                    if vv:
                        after(sem("mod_mm"), vv)
                    tsc(mod_acc[:, :], wm_ring[:, i % 3, :], c_silu[:, 0:1], None, MUL, ALU.bypass, "wm_used")
                else:
                    stt(mod_acc[:, :], wm_ring[:, i % 3, :], c_silu[:, k:k + 1], mod_acc[:, :], MUL, ADD, "wm_used")

            def mod_out(vv):
                after(sem("mod_mm"), vv + 1)
                tt(mods[:, vv * KT:(vv + 1) * KT], ps[:, 7, vv * KT:(vv + 1) * KT], v("b_mod", vv * KT, KT), ADD, "mod_read")

            for vv in (SH1, SC1):
                for k in range(KT):
                    wm(vv * KT + k)
                mod_out(vv)
            stt(gain, mods[:, SC1 * KT:(SC1 + 1) * KT], 1.0, v("g_mix", 0, KT), ADD, MUL)
            tsc(sh_dc, mods[:, SH1 * KT:(SH1 + 1) * KT], float(T), None, MUL, ALU.bypass)
            after(sem("y_raw"), 2 * KT)
            tt(y_dc, y_raw[:, :, 0], gain, MUL)
            tt(y_dc, y_dc, sh_dc, ADD, "dc")
            after(sem("dc_hi"), 1)
            tt(y_lo.rearrange("p (m f) -> p m f", f=NF)[:, :, 0], y_dc, y_hi.rearrange("p (m f) -> p m f", f=NF)[:, :, 0].bitcast(f32), SUB)
            for m in range(KT):
                after(sem("y_hi"), m + 1)
                stt(y_lo[:, m * NF + 1:(m + 1) * NF], y_raw[:, m, 1:NF], gain[:, m:m + 1], y_hi[:, m * NF + 1:(m + 1) * NF].bitcast(f32), MUL, SUB, "y_lo")

            def f_low(t):
                after(sem("f_hi"), t + 1)
                tt(act_lo[:, t, :], f_buf[:, t % 2, :], act_hi[:, t, :].bitcast(f32), SUB, "f_lo")

            for t in range(KT):
                b = 2 * (t % 3)
                after(sem("q_new"), t + 1)
                f = f_buf[:, t % 2, :]
                tt(f[:, 0:NSIN], ps[:, b, 0:NSIN], q_buf[:, t % 2, :], SUB)
                chain(nc.vector.tensor_copy(f[:, NSIN:NSIN + 1], ps[:, b, NSIN:NSIN + 1]))
                tt(f[:, NSIN + 1:T][:, ::-1], ps[:, b, 1:NSIN], q_buf[:, t % 2, 1:NSIN], ADD, "f_new")
                if t:
                    f_low(t - 1)
            f_low(KT - 1)
            for k in range(KT):
                wm(GT1 * KT + k)
            mod_out(GT1)
            after(sem("loaded_xt"), 16)
            done = 3 * KT
            for m in range(KT):
                after(unit_used, U_FNET + m + 1)
                stt(xT[:, m, :], ps[:, fnet_bank(m), :], mod(GT1, m), xT[:, m, :], MUL, ADD, "x0_new")
                for i in range(done, min(done + 3, 5 * KT)):
                    wm(i)
                    if i % KT == KT - 1:
                        mod_out(i // KT)
                done += 3
                if m:
                    after(sem("x0_sq"), m + 1)
                    tt(sumsq[:, :], sumsq[:, :], sq_buf[:, m, :], ADD, "x0_sum")
            stt(gain2, mods[:, SC2 * KT:(SC2 + 1) * KT], 1.0, v("g_ffn", 0, KT), ADD, MUL)

            def inverse(s_sd, name):
                after(s_sd, 1)
                ve.wait_ge(s_sd, 1)
                chain(nc.vector.reciprocal(rstd[:, :], rstd[:, :]), name)

            inverse(sem("x0_sd"), "x0_rstd")
            def a_low(m):
                after(sem("a_hi"), m + 1)
                tt(act_lo[:, m, :], a_buf[:, m % 2, :], act_hi[:, m, :].bitcast(f32), SUB, "a_lo")

            for m in range(KT):
                if m >= 2:
                    after(sem("a_new"), m - 1)
                tt(t_buf[:, m % 2, :], xT[:, m, :], rstd[:, :], MUL, "t_new")
                if m:
                    a_low(m - 1)
            a_low(KT - 1)
            for k in range(KT):
                wm(GT2 * KT + k)

            def ffn(stage, u_up):
                s = ffn_sems(stage)

                def tap(k, j):
                    return vec[:, bass.ds(VEC["conv"] + k * FT + j, 1)]

                def up_pair(i, first):
                    for q in range(2):
                        j = 2 * i + q
                        gate, val, g, u_ = ps[:, 2 * q, :], ps[:, 2 * q + 1, :], g_buf[:, q, :], u_buf[:, q, :]
                        if stage == 0:
                            ve.wait_ge(s["c1"], j + 1)
                            nc.vector.scalar_tensor_tensor(g[:, 1:T], gate[:, 0:T - 1], tap(0, j), g[:, 1:T], MUL, ADD).then_inc(s["c2"], 1)
                            ve.wait_ge(s["c2"], j + 1)
                            nc.vector.scalar_tensor_tensor(g[:, 0:T - 1], gate[:, 1:T], tap(2, j), g[:, 0:T - 1], MUL, ADD).then_inc(s["act_in"], 1)
                            ve.wait_ge(s["silu"], j + 1)
                            ve.wait_ge(unit_used, u_up + 2 * j + 2)
                            nc.vector.tensor_tensor(g, val, g, MUL).then_inc(s["hid"], 1)
                        else:
                            ve.wait_ge(unit_used, u_up + 2 * j + 1)
                            if not first:
                                ve.wait_ge(s["hid_lo"], j - 1)
                            nc.vector.tensor_tensor(g, gate, rstd[:, :], MUL).then_inc(s["act_in"], 1)
                            ve.wait_ge(unit_used, u_up + 2 * j + 2)
                            nc.vector.tensor_tensor(u_, val, rstd[:, :], MUL).then_inc(s["val_read"], 1)
                            ve.wait_ge(s["silu"], j + 1)
                            ve.wait_ge(s["val_read"], j + 1)
                            nc.vector.tensor_tensor(g, g, u_, MUL).then_inc(s["hid"], 1)
                        ve.wait_ge(s["hid_hi"], j + 1)
                        nc.vector.tensor_tensor(hid_lo[:, bass.ds(j * T, T)], g, hid_hi[:, bass.ds(j * T, T)].bitcast(f32), SUB).then_inc(s["hid_lo"], 1)

                up_pair(0, True)
                if stage == 0:
                    mod_out(GT2)
                if stage == 1:
                    ve.wait_ge(ffn_sems(0)["sd"], 1)
                    chain(nc.vector.reciprocal(sumsq[:, :], sumsq[:, :]))
                    for m in range(KT):
                        stt(xT[:, m, :], xT[:, m, :], v("g_mid", m), sumsq[:, :], MUL, MUL)
                with ve.Fori(1, FT // 2) as i:
                    up_pair(i, False)
                ve.wait_ge(s["hid_lo"], FT)

            def next_x(stage, scale, g):
                s, f = ffn_sems(stage), f"f{stage}_"
                gains = g_both if stage == 0 else None if g is None else v(g, 0, KT)

                def low(m):
                    after(s["nx_hi"], m + 1)
                    stt(act_lo[:, m, :], xT[:, m, :], gains[:, m:m + 1], act_hi[:, m, :].bitcast(f32), MUL, SUB, f + "nx_lo")

                for m in range(KT):
                    after(s["down_tile"], m + 1)
                    stt(xT[:, m, :], ps[:, m, :], mod(GT2, m) if scale is None else scale, xT[:, m, :], MUL, ADD, f + "x_new")
                    if gains is not None and m:
                        low(m - 1)
                if gains is not None:
                    low(KT - 1)
                if stage == 0:
                    for m in range(1, KT):
                        after(s["nx_sq"], 2 * m + 1)
                        tt(sumsq[:, :], sumsq[:, :], sq_buf[:, m, :], ADD, f + "nx_sum")
                    for m in range(1, KT):
                        after(s["nx_sq"], 2 * m + 2)
                        tt(sq_mid[:, 0, :], sq_mid[:, 0, :], sq_mid[:, m, :], ADD, "mid_sum")
                    after(s["sd"], 1)
                    tsc(rstd[:, :], ps[:, 6, :], EPS / D, EPS * EPS, MUL, ADD)
                    after(sem("mid_stat"), 1)
                    stt(rstd[:, :], ps[:, 7, :], 1.0 / D, rstd[:, :], MUL, ADD, "mid_ms")
                    after(sem("mid_sd"), 1)
                    chain(nc.vector.reciprocal(rstd[:, :], rstd[:, :]), f + "rstd")
                    return
                for m in range(1, KT):
                    after(s["nx_sq"], m + 1)
                    tt(sumsq[:, :], sumsq[:, :], sq_buf[:, m, :], ADD, f + "nx_sum")
                inverse(s["sd"], f + "rstd")

            ffn(0, U_UP0)
            tt(g_both, v("g_mid", 0, KT), v("g_ffn1", 0, KT), MUL, "g_both")
            next_x(0, None, None)
            ffn(1, U_UP1)
            next_x(1, 0.5, "g_in")

            chain(nc.vector.memset(pads[:, :, 0:1], 0.0))
            chain(nc.vector.memset(scan_mask[:, 0, :], 1.0))
            chain(nc.vector.memset(scan_mask[:, 0, 0:T:CH], 0.0))
            tsc(one_minus_ka, v("k_a", 0, PAIRS), -1.0, 1.0, MUL, ADD)

            def shifted(i, dst):
                after(unit_used, U_IN + i + 1)
                pad = pads[:, i % 2, :]
                tt(pad[:, 1:T + 1], ps[:, i % 4, :], rstd[:, :], MUL)
                tt(diff[:, :], pad[:, 0:T], pad[:, 1:T + 1], SUB)
                stt(dst, diff[:, :], v("mu", i), pad[:, 1:T + 1], MUL, ADD, "in_read")

            shifted(0, wa[:, 0, :])
            shifted(1, gx[:, 0, :])
            for p in range(PAIRS):
                i = 2 + 3 * p
                shifted(i, pk[:, 0, :])
                shifted(i + 1, rR[:, p, :])
                shifted(i + 2, rV[:, p, :])
                after(sem("za_read"), p + 1)
                chain(nc.vector.tensor_tensor_scan(cs[:, 0, :], scan_mask[:, 0, :], sg[:, 0, :], 0.0, MUL, ADD))
                tt(sg[:, 0, :], cs[:, 0, :], sg[:, 0, :], SUB, "cs_ready")
                after(sem("nr_ready"), p + 1)
                tsc(nr[:, 0, :], nr[:, 0, :], L2_EPS, None, MAX, ALU.bypass)
                chain(nc.vector.reciprocal(nr[:, 0, :], nr[:, 0, :]))
                stt(nr[:, 0, :], pk[:, 0, :], v("k_k", p), nr[:, 0, :], MUL, MUL)
                after(sem("exps"), p + 1)
                stt(rA[:, p, :], nr[:, 0, :], -1.0, sg[:, 0, :], MUL, MUL)
                tt(sq[:, 0, :], nr[:, 0, :], ag[:, 0, :], MUL)
                tt(rB[:, p, :], sq[:, 0, :], iv[:, 0, :], MUL)
                tsc(ag[:, 0, :], ag[:, 0, :], v("k_a", p), one_minus_ka[:, p:p + 1], MUL, ADD)
                tt(ag[:, 0, :], ag[:, 0, :], pk[:, 0, :], MUL)
                tt(rK[:, p, :], ag[:, 0, :], iv[:, 0, :], MUL)
                stt(pk[:, 0, :], rR[:, p, :], v("r_k", p), ag[:, 0, :], MUL, MUL, "rk_ready")
                chain(nc.vector.tensor_copy(pchunk[:, p, :], cs[:, 0, CH - 1:T:CH]))
                tt(rR[:, p, :], rR[:, p, :], cs[:, 0, :], MUL)
                after(sem("bonus_mm"), p + 1)
                tt(rBonus[:, p, :], ps[:, 6, :], rV[:, p, :], MUL, "prep")
            for b_ in (pool_a, pool_b, pool_c):
                chain(nc.vector.memset(b_[:, 0:PADW], 0.0))
            for g, win in enumerate(WINDOWS):
                i = 2 + 3 * PAIRS + g
                after(unit_used, U_IN + i + 1)
                tt(pool_a[:, PADW:], ps[:, i % 4, :], rstd[:, :], MUL, "in_read")
                src, k = pool_a, 1
                while k < win:
                    dst = pool_b if src is not pool_b else pool_c
                    chain(nc.vector.tensor_tensor(dst[:, PADW:], src[:, PADW:], src[:, PADW - k:PADW + T - k], ADD))
                    src, k = dst, 2 * k
                tt(pooled[:, g, 0:PADW], src[:, PADW:2 * PADW], inv_count[:, g * PADW:(g + 1) * PADW], MUL)
                tsc(pooled[:, g, PADW:], src[:, 2 * PADW:], 1.0 / win, None, MUL, ALU.bypass)
                tt(pooled[:, g, :], pooled[:, g, :], pool_a[:, PADW:], SUB, "pooled")

            after(unit_used, U_OUT)
            ve.sem_inc(sem("in_done"), 1)
            after(sem("loaded_masks"), 32)
            n_step = [0, 0]

            def pair(p):
                pe_did, ve_did, ac_did, po_did = step_waits(ve, p)
                b = sets[p % 2]

                def did(name, ins):
                    n_step[p % 2] += 1
                    assert at(VE_STEPS, p, name) == n_step[p % 2], name
                    ins.then_inc(vector_step[p % 2], 1)

                def bank(k, n=1):
                    return ps[:, b.bank + k, :]

                def bank4(k):
                    return bank(k).rearrange("q (c h t) -> q c h t", c=2, h=2)

                halves = (("a", slice(0, 2)), ("b", slice(2, 4)))
                pe_did("tB")
                did("tB", nc.vector.tensor_copy(b.BT[:, :], bank(1)))
                yield
                for k, M in (("L", b.MB), ("K", b.MK)):
                    for c in range(NCP):
                        pe_did(f"{k}{c}")
                        did(f"{k}{c}", nc.vector.tensor_tensor(M[:, c, :, :].rearrange("q h t -> q (h t)"), bank(c), mask4[:, :], MUL))
                ve_did(f"L{NCP - 1}")
                for half, c in halves:
                    chain(nc.vector.tensor_tensor(b.TT[:, c, :, :], b.MB[:, c, 0:2, :], mask_lv[:, 0:1, :].unsqueeze(1).to_broadcast([P, 2, 2, P]), MUL))
                    did(f"D1{half}", nc.vector.tensor_tensor(b.TT[:, c, :, :], b.TT[:, c, :, :],
                                                            ident.unsqueeze(1).unsqueeze(1).to_broadcast([P, 2, 2, P]), ADD))
                yield
                pe_did("t1b")
                did("t1b", nc.vector.tensor_copy(b.T[:, 2:4, :, :], bank4(1)))
                yield
                for n in INVERT:
                    yield
                    for k, (half, c) in enumerate(halves):
                        pe_did(f"D{n}{half}")
                        did(f"D{n}{half}", nc.vector.tensor_tensor(b.TT[:, c, :, :], bank4(k), b.TT[:, c, :, :], ADD))
                    yield
                    if n < LAST:
                        pe_did(f"t{n}b")
                        did(f"t{n}b", nc.vector.tensor_copy(b.T[:, 2:4, :, :], bank4(3)))
                        yield
                yield
                pe_did("GHb")
                did("GHb", nc.vector.tensor_copy(b.GH[:, :, 4:8, :], bank(1).rearrange("q (s g k) -> q g s k", s=4, g=2)))
                yield
                pe_did("RP")
                did("RP", nc.vector.tensor_tensor(b.RP[:, :], bank(3), rR[:, p, :], ADD))
                yield
                for half, k, odd in (("a", 0, 0), ("b", 1, 1)):
                    pe_did(f"MT{half}")
                    m4 = b.MT[:, odd:NCH:2, :]
                    chain(nc.vector.tensor_tensor(m4, bank(k).rearrange("q (c t) -> q c t", c=4), ident.unsqueeze(1).to_broadcast([P, 4, P]), ADD))
                    did(f"MT{half}", nc.vector.tensor_tensor(m4, m4, mask_bd.unsqueeze(1).to_broadcast([P, 4, P]), MUL))
                for half, k, odd in (("a", 3, 0), ("b", 2, 1)):
                    pe_did(f"N{half}")
                    for c in range(odd, NCH, 2):
                        ins = nc.vector.scalar_tensor_tensor(b.S[:, c, :], bank(k)[:, (c // 2) * P:(c // 2 + 1) * P], pchunk[:, p, c:c + 1], mask_bd, MUL, MUL)
                        if c < NCH - 2 + odd:
                            ins.then_inc(sem("n_chain"), 1)
                    did(f"N{half}", ins)
                yield
                for c in range(1, NCH - 1):
                    pe_did(f"S{c}")
                    ve_did("Nb")
                    did(f"S{c}", nc.vector.scalar_tensor_tensor(b.S[:, c, :], bank((c + 1) % 2)[:, 0:P], pchunk[:, p, c:c + 1], b.S[:, c, :], MUL, ADD))
                    yield
                ac_did("OV")
                pe_did("Y")
                chain(nc.vector.tensor_copy(b.y[:, 0:CH], b.OV[:, 0:CH]))
                did("Y", nc.vector.tensor_tensor(b.y[:, CH:T], bank(3)[:, CH:T], b.OV[:, CH:T], ADD))
                yield
                pe_did("mean")
                ve_did("Y")
                did("yc", nc.vector.scalar_tensor_tensor(b.y[:, :], bank(0), -1.0 / HS, b.y[:, :], MUL, ADD))
                yield
                ac_did("sd")
                chain(nc.vector.reciprocal(b.sd[:, :], b.sd[:, :]))
                did("yn", nc.vector.tensor_tensor(b.y[:, :], b.y[:, :], b.sd[:, :], MUL))
                yield
                ac_did("affine")
                chain(nc.vector.tensor_tensor(b.y[:, :], b.y[:, :], rBonus[:, p, :], ADD))
                did("out", nc.vector.tensor_tensor(rG[:, p, :], b.y[:, :], rG[:, p, :], MUL))
                yield

            in_turns(pair)
            for p in range(PAIRS):
                after(sem("mix_hi"), p + 1)
                tt(act_lo[:, p, :], rG[:, p, :], act_hi[:, p, :].bitcast(f32), SUB, "mix_lo")
            for g in range(len(WINDOWS)):
                after(sem("pool_hi"), g + 1)
                stt(act_lo[:, PAIRS + g, :], ps[:, g, :], v("pool_scale", g), act_hi[:, PAIRS + g, :].bitcast(f32), MUL, SUB, "pool_lo")

            for m in range(KT):
                after(unit_used, U_OUT + m + 1)
                tt(xT[:, m, :], ps[:, m % 4, :], xT[:, m, :], ADD, "x2_new")
                if m:
                    after(sem("x2_sq"), m + 1)
                    tt(sumsq[:, :], sumsq[:, :], sq_buf[:, m, :], ADD, "x2_sum")
            for m in range(KT):
                after(sem("x2_hi"), m + 1)
                stt(act_lo[:, m, :], xT[:, m, :], v("g_ffn2", m), act_hi[:, m, :].bitcast(f32), MUL, SUB, "x2_lo")
            inverse(sem("x2_sd"), "x2_rstd")
            ffn(2, U_UP2)
            next_x(2, 0.5, None)
            for m in range(KT):
                stt(act_out[:, m, :], xT[:, m, :], v("g_last", m), rstd[:, :], MUL, MUL, "y_out")

        @block.tensor
        def _(pe):
            after = pe.wait_ge

            def three(o, wh, wl, xh, xl, start, stop):
                nc.tensor.matmul(o, wh, xh, start=start, stop=False)
                nc.tensor.matmul(o, wh, xl, start=False, stop=False)
                return nc.tensor.matmul(o, wl, xh, start=False, stop=stop)

            def blk(slot, b):
                return w_hi[:, slot, b * P:(b + 1) * P], w_lo[:, slot, b * P:(b + 1) * P]

            def mod_columns(vv):
                after(sem("wm_used"), KT * (vv + 1))
                for m in range(KT):
                    last = nc.tensor.matmul(ps[:, 7, vv * KT + m:vv * KT + m + 1], mod_acc[:, m * P:(m + 1) * P], ones[:, 0:1], start=True, stop=True)
                last.then_inc(sem("mod_mm"), 1)

            after(sem("cs_lo"), 1)
            for m in range(KT):
                b = 2 * (m % 3)
                if m >= 3:
                    after(sem("y_raw"), 2 * (m - 2))
                for bank, c0, n in ((b, 0, NCOS), (b + 1, NCOS, NSIN)):
                    for k in range(TT_):
                        after(sem("xn_lo"), k + 1)
                        w = slice(k * D + m * P, k * D + (m + 1) * P)
                        x = slice(k * NF + c0, k * NF + c0 + n)
                        last = three(ps[:, bank, 0:n], xn_hi[:, w], xn_lo[:, w], cs_hi[:, x], cs_lo[:, x], k == 0, k == TT_ - 1)
                last.then_inc(sem("seq_mm"), 1)
            after(sem("loaded_const"), 16)
            mod_columns(SH1)
            mod_columns(SC1)
            after(lo_done, U_DFT + 1)
            for t in range(KT):
                g, mm = divmod(t, 2)
                b = 2 * (t % 3)
                after(sem("y_lo"), 2 * g + 2)
                if t >= 3:
                    after(sem("f_new"), t - 2)
                for f, c0, n in ((0, 0, NCOS), (1, NCOS, NSIN)):
                    for kk in range(2):
                        x = slice((2 * g + kk) * NF + c0, (2 * g + kk) * NF + c0 + n)
                        last = three(ps[:, b + f, 0:n], *blk(0, 4 * f + 2 * kk + mm), y_hi[:, x], y_lo[:, x], kk == 0, kk == 1)
                last.then_inc(sem("chan_mm"), 1)
            after(sem("chan_mm"), KT)
            pe.sem_inc(unit_used, 1)

            def unit_by_output(u, slot, bank, ready=None):
                after(lo_done, u + 1)
                for k in range(KT):
                    if ready is not None:
                        after(ready, k + 1)
                    last = three(ps[:, bank, :], *blk(slot, k), act_hi[:, k, :], act_lo[:, k, :], k == 0, k == KT - 1)
                last.then_inc(unit_used, 1)

            for m in range(KT):
                if m >= 4:
                    after(sem("x0_new"), m - 3)
                unit_by_output(U_FNET + m, (U_FNET + m) % RING, fnet_bank(m), sem("f_lo") if m == 0 else None)
                if m == 2:
                    mod_columns(GT1)
                if m == 5:
                    mod_columns(SH2)
            mod_columns(SC2)

            def stat(s_sum, n, s_stat, bank=6, sums=sumsq[:, :]):
                after(s_sum, n)
                nc.tensor.matmul(ps[:, bank, :], ones, sums, start=True, stop=True).then_inc(s_stat, 1)

            stat(sem("x0_sum"), KT - 1, sem("x0_stat"))

            def ffn(stage, u_up, u_dn, ready, mid):
                s = ffn_sems(stage)

                def up_pair(i, first):
                    for q in range(2):
                        j = 2 * i + q
                        for h in range(2):
                            off = u_up + 2 * q + h
                            if not first:
                                if stage == 0:
                                    pe.wait_ge(s["act_in"] if h == 0 else s["hid"], j - 1)
                                else:
                                    pe.wait_ge(s["act_in"] if h == 0 else s["val_read"], j - 1)
                            unit_by_output(4 * i + off, off % RING, 2 * q + h, ready if first and q == 0 and h == 0 else None)
                        if first and q == 0:
                            mid()

                up_pair(0, True)
                with pe.Fori(1, FT // 2) as i:
                    up_pair(i, False)

                def down(kt, u, slot, x, start, stop, signal=True):
                    after(lo_done, u + 1)
                    after(s["hid_lo"], kt + 1)
                    for m in range(KT):
                        last = three(ps[:, m, :], *blk(slot, m), hid_hi[:, x], hid_lo[:, x], start, stop)
                    last.then_inc(unit_used, 1)

                after(lo_done, u_dn + 1)
                for m in (4, 5, 6, 7, 0, 1, 2, 3):
                    if m == 0:
                        after(s["hid"], FT)
                    last = three(ps[:, m, :], *blk(u_dn % RING, m), hid_hi[:, 0:T], hid_lo[:, 0:T], True, False)
                last.then_inc(unit_used, 1)
                for kt in range(1, 4):
                    down(kt, u_dn + kt, (u_dn + kt) % RING, slice(kt * T, (kt + 1) * T), False, False)
                with pe.Fori(1, (FT - 2) // 4) as i:
                    for j in range(4):
                        down(4 * i + j, 4 * i + (u_dn + j), (u_dn + j) % RING, bass.ds((4 * i + j) * T, T), False, False)
                after(lo_done, u_dn + FT)
                after(s["hid_lo"], FT)
                for m in range(KT):
                    for kt in (FT - 2, FT - 1):
                        x = slice(kt * T, (kt + 1) * T)
                        last = three(ps[:, m, :], *blk((u_dn + kt) % RING, m), hid_hi[:, x], hid_lo[:, x], False, kt == FT - 1)
                    last.then_inc(s["down_tile"], 1)
                after(s["down_tile"], KT)
                pe.sem_inc(unit_used, 2)

            ffn(0, U_UP0, U_DN0, sem("a_lo"), lambda: mod_columns(GT2))
            s0, s1, s2 = (ffn_sems(i) for i in range(3))

            def mid_stats():
                after(s0["x_new"], KT)
                stat(s0["nx_sum"], KT - 1, s0["stat"])
                stat(sem("mid_sum"), KT - 1, sem("mid_stat"), 7, sq_mid[:, 0, :])

            ffn(1, U_UP1, U_DN1, s0["nx_lo"], mid_stats)

            def small_products(i):
                if 2 <= i < 2 + 3 * PAIRS and (i - 2) % 3 == 1:
                    p = (i - 2) // 3
                    cols = slice(p * P, (p + 1) * P)
                    after(sem("wa_ready"), 1)
                    after(sem("loaded_lora"), 48)
                    if p:
                        after(sem("za_read"), p)
                    nc.tensor.matmul(ps[:, 4, :], lora[:, 0, cols], wa[:, 0, :], start=True, stop=True)
                    nc.tensor.matmul(ps[:, 5, :], lora[:, 1, cols], wa[:, 0, :], start=True, stop=True).then_inc(sem("za_mm"), 1)
                    after(sem("g_in"), 1)
                    if p:
                        after(sem("g_read"), p)
                    nc.tensor.matmul(ps[:, 7, :], g_lora[:, cols], gx[:, 0, :], start=True, stop=True).then_inc(sem("g_mm"), 1)
                if 2 <= i < 2 + 3 * PAIRS and (i - 2) % 3 == 2:
                    p = (i - 2) // 3
                    after(sem("sq_ready"), p + 1)
                    if p:
                        after(sem("prep"), p)
                    nc.tensor.matmul(ps[:, 6, :], bones, sq[:, 0, :], start=True, stop=True).then_inc(sem("ss_mm"), 1)
                if 5 <= i < 5 + 3 * PAIRS and (i - 5) % 3 == 1:
                    p = (i - 5) // 3
                    after(sem("rk_ready"), p + 1)
                    nc.tensor.matmul(ps[:, 6, :], bones, pk[:, 0, :], start=True, stop=True).then_inc(sem("bonus_mm"), 1)

            for i in range(len(IN_STARTS)):
                if i == 0:
                    after(s1["x_new"], KT)
                if i >= 4:
                    after(sem("in_read"), i - 3)
                unit_by_output(U_IN + i, (U_IN + i) % RING, i % 4, s1["nx_lo"] if i == 0 else None)
                if i == 0:
                    stat(s1["nx_sum"], KT - 1, s1["stat"])
                small_products(i)

            after(sem("in_done"), 1)
            n_step = [0, 0]

            def pair(p):
                _, ve_did, ac_did, po_did = step_waits(pe, p)
                b = sets[p % 2]

                def did(name, ins):
                    n_step[p % 2] += 1
                    assert at(PE_STEPS, p, name) == n_step[p % 2], name
                    ins.then_inc(tensor_step[p % 2], 1)

                def bank(k):
                    return ps[:, b.bank + k, :]

                if p >= 2:
                    pe.wait_ge(vector_step[p % 2], at(VE_STEPS, p - 2, "out"))
                for k, (name, src) in enumerate((("tA", rA), ("tB", rB), ("tK", rK), ("tV", rV))):
                    for c in range(NCP):
                        cols = slice(c * P, (c + 1) * P)
                        last = nc.tensor.transpose(bank(k)[:, cols], src[:, p, cols], ident)
                    did(name, last)
                yield
                ac_did("planes")
                ac_did("tV")
                ve_did("tB")
                for k, src in (("L", rB), ("K", rK)):
                    for c in range(NCP):
                        if k == "K":
                            ve_did(f"L{c}")
                        did(f"{k}{c}", nc.tensor.matmul(bank(c), src[:, p, c * P:(c + 1) * P], b.planes[:, c, :, :].rearrange("q h t -> q (h t)"), start=True, stop=True))
                yield

                def systems(half):
                    c0 = 0 if half == "a" else 2
                    return [(c, h, slice(((c - c0) * 2 + h) * P, ((c - c0) * 2 + h + 1) * P)) for c in (c0, c0 + 1) for h in range(2)]

                def flip(n, k0):
                    for k, half in enumerate("ab"):
                        ve_did(f"D{n}{half}")
                        for c, h, o in systems(half):
                            last = nc.tensor.transpose(bank(k0 + k)[:, o], b.TT[:, c, h, :], ident)
                        did(f"t{n}{half}", last)

                flip(1, 0)
                yield
                for n in INVERT:
                    for k, half in enumerate("ab"):
                        po_did(f"X{n}")
                        (ac_did if half == "a" else ve_did)(f"t{n - 1}{half}")
                        for c, h, o in systems(half):
                            last = nc.tensor.matmul(bank(2 + k)[:, o], b.X[:, c, h, :], b.T[:, c, h, :], start=True, stop=True)
                        did(f"U{n}{half}", last)
                    yield
                    for k, half in enumerate("ab"):
                        ac_did(f"U{n}{half}")
                        for c, h, o in systems(half):
                            last = nc.tensor.matmul(bank(k)[:, o], b.U[:, c, h, :], b.TT[:, c, h, :], start=True, stop=True)
                        did(f"D{n}{half}", last)
                    yield
                    if n < LAST:
                        flip(n, 2)
                        yield
                for c in range(NCP):
                    for h in range(2):
                        last = nc.tensor.matmul(bank(2)[:, (2 * c + h) * HS:(2 * c + h + 1) * HS], b.MK[:, c, h, :], b.VT[:, c * P + h * HS:c * P + (h + 1) * HS], start=True, stop=True)
                did("AV", last)
                yield
                ac_did("AV")
                for k, half in enumerate("ab"):
                    ve_did(f"D{LAST}{half}")
                    for c, h, o in systems(half):
                        last = nc.tensor.matmul(bank(k)[:, o], b.TT[:, c, h, :], b.AA[:, c, h, :], start=True, stop=True)
                    did(f"GH{half}", last)
                yield
                ac_did("GHa")
                ve_did("GHb")
                for c in range(NCP):
                    for h in range(2):
                        r = slice(h * HS, (h + 1) * HS)
                        last = nc.tensor.matmul(ps[r, b.bank + 3, c * P:(c + 1) * P], b.GH[:, 0, 2 * c + h, :], b.MB[:, c, 2 + h, :], start=True, stop=True)
                did("RP", last)
                for c in range(NCP):
                    for h in range(2):
                        r, o = slice(h * HS, (h + 1) * HS), slice(c * P, (c + 1) * P)
                        nc.tensor.matmul(ps[r, b.bank + 2, o], b.GH[:, 1, 2 * c + h, :], b.MB[:, c, 2 + h, :], start=True, stop=False)
                        last = nc.tensor.matmul(ps[r, b.bank + 2, o], b.VT[:, c * P + h * HS:c * P + (h + 1) * HS], b.MK[:, c, 2 + h, :], start=False, stop=True)
                did("OV", last)
                yield
                for half, k, odd in (("a", 0, 0), ("b", 1, 1)):
                    for c in range(odd, NCH, 2):
                        cp, r = c // 2, slice(odd * CH, (odd + 1) * CH)
                        last = nc.tensor.matmul(bank(k)[:, cp * P:(cp + 1) * P], b.GH[r, 0, 2 * cp:2 * cp + 2, :].rearrange("q s k -> q (s k)"), b.BT[r, cp * P:(cp + 1) * P], start=True, stop=True)
                    did(f"MT{half}", last)
                for half, k, odd in (("a", 3, 0), ("b", 2, 1)):
                    if odd:
                        ac_did("OV")
                    else:
                        ve_did("RP")
                    for c in range(odd, NCH, 2):
                        cp, r = c // 2, slice(odd * CH, (odd + 1) * CH)
                        o = bank(k)[:, cp * P:(cp + 1) * P]
                        nc.tensor.matmul(o, b.BT[r, cp * P:(cp + 1) * P], b.GH[r, 1, 2 * cp:2 * cp + 2, :].rearrange("q s k -> q (s k)"), start=True, stop=False)
                        last = nc.tensor.matmul(o, b.KT[r, cp * P:(cp + 1) * P], b.VT[r, cp * P:(cp + 1) * P], start=False, stop=True)
                    did(f"N{half}", last)
                yield
                ve_did("Nb")
                for c in range(1, NCH - 1):
                    if c > 1:
                        ve_did(f"S{c - 1}")
                    did(f"S{c}", nc.tensor.matmul(bank((c + 1) % 2)[:, 0:P], b.MT[:, c, :], b.S[:, c - 1, :], start=True, stop=True))
                    yield
                ve_did(f"S{NCH - 2}")
                for c in range(1, NCH):
                    last = nc.tensor.matmul(bank(3)[:, c * CH:(c + 1) * CH], b.S[:, c - 1, :], b.RP[:, c * CH:(c + 1) * CH], start=True, stop=True)
                did("Y", last)
                yield
                ve_did("Y")
                did("mean", nc.tensor.matmul(bank(0), bones, b.y[:, :], start=True, stop=True))
                yield
                ac_did("sq")
                did("var", nc.tensor.matmul(bank(1), bones, b.ysq[:, :], start=True, stop=True))
                yield
                yield

            in_turns(pair)
            for g in range(len(WINDOWS)):
                for q in range(2):
                    pe.wait_ge(vector_step[q], at(VE_STEPS, PAIRS - 2 + q, "out"))
                nc.tensor.matmul(ps[:, g, :], w_pool[:, g, :], pooled[:, g, :], start=True, stop=True).then_inc(sem("pool_mm"), 1)

            after(sem("mix_lo"), PAIRS)
            after(sem("pool_lo"), len(WINDOWS))
            for m in range(KT):
                if m >= 4:
                    after(sem("x2_new"), m - 3)
                unit_by_output(U_OUT + m, (U_OUT + m) % RING, m % 4)
            after(sem("x2_new"), KT)
            ffn(2, U_UP2, U_DN2, sem("x2_lo"), lambda: stat(sem("x2_sum"), KT - 1, sem("x2_stat")))
            after(s2["x_new"], KT)
            stat(s2["nx_sum"], KT - 1, s2["stat"])


def _columns(a):
    return np.asarray(a).reshape(-1, P).T


def _by_output(w):
    return w.reshape(KT, P, -1, P).transpose(2, 1, 0, 3).reshape(-1, P, D)


def _tables():
    l = np.arange(T)
    cos_k, sin_k = np.arange(NCOS), np.arange(NSIN)
    cs = np.concatenate([np.cos(2 * np.pi * (np.outer(l, cos_k) % T) / T), np.sin(2 * np.pi * (np.outer(l, sin_k) % T) / T)], 1)
    cs[:, NCOS] = 0.0
    cs = cs.reshape(TT_, P, NF).transpose(1, 0, 2)
    c = np.arange(FG)
    ang = 2 * np.pi * (np.outer(c, c) % FG) / FG
    norm = 1.0 / np.sqrt(T * FG)
    chan = np.stack([np.cos(ang) * norm, np.sin(ang) * norm]).reshape(2, 2, P, 2, P).transpose(2, 0, 1, 3, 4).reshape(P, D)
    i = np.arange(P)
    inv = np.stack([1.0 / np.minimum(np.arange(PADW) + 1, w) for w in WINDOWS]).reshape(1, -1).repeat(P, 0)
    const = np.concatenate([np.eye(P), np.ones((P, P)), (i[:, None] // HS == i // HS) * 1.0, inv], 1)
    s, t = i[:, None], i[None, :]
    same = s // CH == t // CH
    strict, incl = same & (s < t), same & (s <= t)
    levels = [(t // b % 2 == 1) & (s // b == t // b - 1) for b in LEVELS]
    mask = np.concatenate([strict, strict, incl, incl] + levels + [s // HS == t // HS], 1)
    return [np.ascontiguousarray(a, dtype=np.float32) for a in (cs, chan, const, mask)]


def kernel(**inputs):
    import concourse.bacc as bacc
    from concourse.bass_utils import run_bass_kernel_spmd

    g = {k: np.asarray(a) for k, a in inputs.items()}
    cs, chan, const, mask = _tables()
    w_in = g["w_in_2"][0]
    mu = np.zeros(1600 + P, np.float32)
    mu[:g["mu_shift_2"].shape[1]] = g["mu_shift_2"][0]
    eps = np.full((P, 1), EPS, np.float32)
    vec = np.concatenate(
        [_columns(g["c"][0]), _columns(g["b_mod"][0]), _columns(g["g_norm_mix"][0]), _columns(g["g_norm_ffn"][0]),
         _columns(g["w_ffn_conv"][0]), _columns(g["b_ffn_conv"][0]), _columns(g["ffn1_norm_2"][0]), _columns(g["mix_norm_2"][0])]
        + [_columns(mu[s:s + P]) for s in IN_STARTS_RW]
        + [_columns(g[n][0]) for n in ("w0_2", "a0_2", "k_k_2", "k_a_2", "r_k_2", "ln_w_2", "ln_b_2", "pool_scale_2", "ffn2_norm_2")]
        + [_columns(g["g_final"]), _columns(g["final_norm_2"]), eps, np.full((P, 1), GN_EPS, np.float32)], 1)

    def gated(a, b):
        return np.stack([_by_output(a), _by_output(b)], 1).reshape(-1, P, D)

    up = g["w_ffn_up"][0]
    units = np.concatenate(
        [chan[None], _by_output(g["w_fnet_out"][0]), gated(up[:, :F], up[:, F:]), g["w_ffn_down"][0].reshape(FT, P, D),
         gated(g["ffn1_w_gate_2"][0], g["ffn1_w_up_2"][0]), g["ffn1_w_down_2"][0].reshape(FT, P, D)]
        + [_by_output(w_in[:, s:s + P]) for s in IN_STARTS]
        + [_by_output(g["w_out_2"][0]), gated(g["ffn2_w_gate_2"][0], g["ffn2_w_up_2"][0]), g["ffn2_w_down_2"][0].reshape(FT, P, D)])
    w_mod = g["w_mod"][0].reshape(KT, P, 6, D).transpose(2, 0, 1, 3).reshape(6 * KT, P, D)
    lora = np.zeros((P, 3, RW), np.float32)
    lora[0:32, 0] = g["w_lora_up_2"][0]
    lora[32:64, 1] = g["a_lora_up_2"][0]
    lora[0:96, 2] = g["g_lora_up_2"][0]
    x = g["x"][0]
    arrays = {
        "vectors": vec, "constants": const, "masks": mask, "tokens": x, "tokens_by_channel": x.T.reshape(KT, P, T).transpose(1, 0, 2),
        "seq_transform": cs, "mod_units": w_mod, "weight_units": units, "low_rank": lora,
        "pool_weights": g["w_pool_2"][0].transpose(1, 0, 2),
    }
    arrays = {k: np.ascontiguousarray(a) for k, a in arrays.items()}
    nc = bacc.Bacc("TRN2", target_bir_lowering=False, num_devices=1)
    args = [nc.dram_tensor(k, a.shape, mybir.dt.from_np(a.dtype), kind="ExternalInput").ap() for k, a in arrays.items()]
    result = nc.dram_tensor("result", (D, T), mybir.dt.float32, kind="ExternalOutput").ap()
    build(nc, *args, result)
    r = run_bass_kernel_spmd(nc, [arrays], core_ids=[0])
    return np.ascontiguousarray(r.results[0]["result"].T).reshape(1, T, D)
```

```python
from contextlib import ExitStack

import numpy as np
import concourse.bass as bass
from concourse import mybir

P = 128
T = 512
D = 1024
KT = D // P
F = 2816
FT = F // P
TT_ = T // P
FG = 256
NCOS = T // 2 + 2
NSIN = T // 2
NF = NCOS + NSIN
RW = 512
HS = 64
PAIRS = RW // P
CH = 64
NCH = T // CH
NCP = NCH // 2
EPS = 1e-6
GN_EPS = 64e-5
L2_EPS = 1e-12
KAPPA = float(np.exp(-0.5))
WINDOWS = (2, 4, 8, 16)
PADW = 16
LEVELS = (1, 2, 4, 8, 16, 32)

IN_STARTS_RW = [1536, 1600] + [s + P * p for p in range(PAIRS) for s in (512, 0, 1024)]
IN_STARTS = IN_STARTS_RW + [1696 + P * g for g in range(len(WINDOWS))]
U_DFT = 0
U_FNET = 1
U_UP0 = U_FNET + KT
U_DN0 = U_UP0 + 2 * FT
U_UP1 = U_DN0 + FT
U_DN1 = U_UP1 + 2 * FT
U_IN = U_DN1 + FT
U_OUT = U_IN + len(IN_STARTS)
U_UP2 = U_OUT + KT
U_DN2 = U_UP2 + 2 * FT
NU = U_DN2 + FT
RING = 4
AHEAD = 3

Y_POOL = 3
Y_ORDER = sorted([("y_out", m + 1, m) for m in range(KT - Y_POOL)] + [("y_out_pool", m + 1, KT - Y_POOL + m) for m in range(Y_POOL)],
                 key=lambda y: y[1] * (9 if y[0] == "y_out_pool" else 5))
SQ_LAG = 3

VEC = {}
NVEC = 0
for _name, _n in (("c", KT), ("b_mod", 6 * KT), ("g_mix", KT), ("g_ffn", KT), ("conv", 3 * FT), ("b_conv", FT),
                  ("g_ffn1", KT), ("g_in", KT), ("mu", len(IN_STARTS_RW)), ("w0", PAIRS), ("a0", PAIRS),
                  ("k_k", PAIRS), ("k_a", PAIRS), ("r_k", PAIRS), ("ln_w", PAIRS), ("ln_b", PAIRS),
                  ("pool_scale", len(WINDOWS)), ("g_ffn2", KT), ("g_mid", KT), ("g_last", KT), ("eps", 1), ("gn_eps", 1)):
    VEC[_name] = NVEC
    NVEC += _n
NCONST = 3 * P + len(WINDOWS) * PADW
NMASK = 4 * P + len(LEVELS) * P + P

INVERT = range(2, len(LEVELS) + 1)
LAST = len(LEVELS)


def fnet_bank(m):
    return (m + 6) % 7


WM_MID = 11


def wm_places():
    last, turns, res = {}, {}, []
    for i in range(6 * KT):
        if i < 2 * KT:
            n = i % 7
        elif i < 5 * KT:
            n = (i - 2 * KT) % WM_MID
            n += 4 if n > 2 else 0
        else:
            n = 15 + i % 4
        flag = n if n < 15 else n - 12
        turns[flag] = turns.get(flag, 0) + 1
        res.append((n, flag, turns[flag], last.get(n)))
        last[n] = i
    return res


class Buffers:

    def __init__(self, bank, MB, MK, TT, T, U, X, AA, BT, KT, VT, MT, GH, S, RP, y, ysq, OV, sd):
        self.bank, self.MB, self.MK, self.TT, self.T = bank, MB, MK, TT, T
        self.U, self.X, self.AA, self.BT, self.KT, self.VT = U, X, AA, BT, KT, VT
        self.MT, self.GH, self.S, self.RP, self.y, self.ysq, self.OV, self.sd = MT, GH, S, RP, y, ysq, OV, sd


def _per_level(inner, outer):
    return [x.format(n=n) for n in INVERT for x in inner + (outer if n < LAST else [])]


PE_STEPS = (["tA", "tB", "tK", "tV"] + [f"L{i}" for i in range(NCP)] + [f"K{i}" for i in range(NCP)] + ["t1a", "t1b"]
            + _per_level(["U{n}a", "U{n}b", "D{n}a", "D{n}b"], ["t{n}a", "t{n}b"])
            + ["AV", "GHa", "GHb", "RP", "OV", "MTa", "MTb", "Na", "Nb"] + [f"S{c}" for c in range(1, NCH - 1)]
            + ["Y", "mean", "var"])
VE_STEPS = (["tB"] + [f"L{i}" for i in range(NCP)] + [f"K{i}" for i in range(NCP)] + ["D1a", "D1b", "t1b"]
            + _per_level(["D{n}a", "D{n}b"], ["t{n}b"])
            + ["GHb", "RP", "MTa", "MTb", "Na", "Nb"] + [f"S{c}" for c in range(1, NCH - 1)]
            + ["Y", "yc", "yn", "out"])
AC_STEPS = (["tA", "tK", "tV", "t1a"] + _per_level(["U{n}a", "U{n}b"], ["t{n}a"])
            + ["AV", "GHa", "OV", "sq", "sd", "affine"])
PO_STEPS = [f"X{n}" for n in INVERT]


def at(steps, pair, name):
    return pair // 2 * len(steps) + steps.index(name) + 1


LAG = 14


def in_turns(pair_program, closing):
    def lane(q):
        for p in range(q, PAIRS, 2):
            yield from pair_program(p)

    even, odd, after_even = lane(0), lane(1), closing()
    for _ in range(LAG):
        next(even)
    for _ in even:
        next(odd)
    for _ in odd:
        next(after_even, None)
    for _ in after_even:
        pass


def build(nc, a_vec, a_const, a_mask, a_x, a_xt, a_cs, a_wmod, a_w, a_lora, a_pool, out):
    f32, f32r = mybir.dt.float32, mybir.dt.float32r
    ACT = mybir.ActivationFunctionType
    ALU = mybir.AluOpType
    MUL, ADD, SUB, MAX = ALU.mult, ALU.add, ALU.subtract, ALU.max

    with ExitStack() as ctx:
        lo_edge = (nc.sbuf_base + 63) // 64 * 64
        place = [lo_edge]

        def reserve(n_floats):
            o = place[0]
            place[0] += (4 * n_floats + 31) // 32 * 32
            return o

        def view(name, shape, offset, dt=f32):
            return nc.alloc_sbuf_tensor_at(name, shape, dt, offset=offset)

        def fresh(name, shape, dt=f32):
            return view(name, shape, reserve(int(np.prod(shape[1:]))), dt)

        raw = fresh("raw", [P, RING, D])
        o_whi, o_wlo = reserve(RING * D), reserve(RING * D)
        w_hi = view("w_hi", [P, RING, D], o_whi, f32r)
        w_lo = view("w_lo", [P, RING, D], o_wlo, f32r)
        o_x = reserve(KT * T)
        xT = view("xT", [P, KT, T], o_x)
        o_act = reserve(2 * KT * T)
        act_hi = view("act_hi", [P, KT, T], o_act, f32r)
        act_lo = view("act_lo", [P, KT, T], o_act + 4 * KT * T, f32r)
        o_hid = reserve(2 * FT * T)
        hid_hi = view("hid_hi", [P, FT * T], o_hid, f32r)
        hid_lo = view("hid_lo", [P, FT * T], o_hid + 4 * FT * T, f32r)
        o_misc = reserve(3 * D)
        o_acc = reserve(D)
        o_sums = reserve(2 * T)
        sumsq = view("sumsq", [P, T], o_sums)
        o_rstd = o_sums + 4 * T
        rstd = view("rstd", [P, T], o_rstd)
        vec = fresh("vec", [P, NVEC])
        const = fresh("const", [P, NCONST])
        mods = fresh("mods", [P, 6 * KT])
        small = fresh("small", [P, 64])
        assert place[0] <= nc.sbuf_usable_end, (place[0], nc.sbuf_usable_end)

        ident, ones, bones = const[:, 0:P], const[:, P:2 * P], const[:, 2 * P:3 * P]
        inv_count = const[:, 3 * P:]
        c_silu, gain, sh_dc = small[:, 0:8], small[:, 8:16], small[:, 16:24]
        x_ss, gain2, one_minus_ka, g_both = small[:, 24:28], small[:, 28:36], small[:, 36:40], small[:, 40:48]
        y_dc, g_mid2 = small[:, 48:56], small[:, 56:64]

        def v(name, i=0, n=1):
            return vec[:, VEC[name] + i:VEC[name] + i + n]

        def mod(which, m):
            return mods[:, which * KT + m:which * KT + m + 1]

        SH1, SC1, GT1, SH2, SC2, GT2 = range(6)

        x_tok = view("x_tok", [P, TT_, D], o_act)
        cs_raw = view("cs_raw", [P, TT_, NF], o_act + 4 * TT_ * D)
        y_raw = view("y_raw", [P, KT, NF], o_act)
        xn_hi, xn_lo = hid_hi[:, 0:TT_ * D], hid_lo[:, 0:TT_ * D]
        cs_hi, cs_lo = (h[:, TT_ * D:TT_ * (D + NF)] for h in (hid_hi, hid_lo))
        y_hi, y_lo = (h[:, TT_ * (D + NF):TT_ * (D + NF) + KT * NF] for h in (hid_hi, hid_lo))
        f_buf = view("f_buf", [P, 2, T], o_hid)
        q_buf = view("q_buf", [P, 2, NSIN], o_hid + 4 * 2 * T)
        sq_buf = view("sq_buf", [P, KT, T], o_hid)
        mid_sq = view("mid_sq", [P, T], o_hid + 4 * KT * T)
        wm_ring = view("wm_ring", [P, 3, D], o_misc)
        wm_early = view("wm_early", [P, 4, D], o_x)
        wm_mid = view("wm_mid", [P, 6, D], o_hid + 4 * FT * T)
        wm_mid2 = view("wm_mid2", [P, 2, D], o_hid + 4 * TT_ * D)
        wm_late = view("wm_late", [P, 4, D], o_hid + 4 * (FT * T - 4 * D))
        mod_acc = view("mod_acc", [P, D], o_acc)
        mod_acc3 = view("mod_acc3", [P, D], o_hid + 4 * (FT * T + 7 * D))
        mod_acc2 = view("mod_acc2", [P, D], o_sums)
        junk = view("junk", [P, D], o_hid + 4 * FT * T + 4 * TT_ * (D + NF))

        g_buf = view("g_buf", [P, 2, T], o_misc)
        u_buf = view("u_buf", [P, 2, T], o_misc + 4 * 2 * T)
        t_buf = view("t_buf", [P, 2, T], o_hid + 4 * 8 * T)
        a_buf = view("a_buf", [P, 2, T], o_hid + 4 * 10 * T)
        o_tb = o_misc + 4 * 4 * T

        def tiles(name, first, n=1):
            return view(name, [P, n, T], o_hid + 4 * T * first)

        rAR = view("rAR", [P, 2, PAIRS, T], o_hid)
        rA, rR = rAR[:, 0, :, :], rAR[:, 1, :, :]
        rB, rK = tiles("rB", 8, 4), tiles("rK", 12, 4)
        rV, rBonus, rG = tiles("rV", 16, 4), tiles("rBonus", 20, 4), tiles("rG", 24, 4)
        pooled = tiles("pooled", 28, 4)
        pk, sg, ag, cs, iv, nr, sq = (tiles(n, 32 + i) for i, n in enumerate(("pk", "sg", "ag", "cs", "iv", "nr", "sqk")))
        wa, gx, scan_mask = tiles("wa", 39), tiles("gx", 40), tiles("scan_mask", 41)
        pads = view("pads", [P, 2, T + 4], o_misc + 4 * T)
        diff = view("diff", [P, T], o_misc)
        lora = view("lora", [P, 2, RW], o_acc)
        g_lora = view("g_lora", [P, RW], o_tb)
        w_pool = view("w_pool", [P, len(WINDOWS), P], o_tb + 4 * T)
        pool_b = view("pool_b", [P, PADW + T], o_hid + 4 * T * 42)
        pool_c = view("pool_c", [P, PADW + T], o_misc)
        pchunk = fresh("pchunk", [P, PAIRS, NCH])
        assert place[0] <= nc.sbuf_usable_end, (place[0], nc.sbuf_usable_end)

        act_out = view("act_out", [P, KT, T], o_act)

        def half_set(n, **places):
            def w(name, shape):
                return view(f"{name}{n}", shape, places[name])
            return Buffers(
                MB=w("MB", [P, NCP, 4, P]), MK=w("MK", [P, NCP, 4, P]), TT=w("TT", [P, NCP, 2, P]),
                T=w("T", [P, NCP, 2, P]), U=w("U", [P, NCP, 2, P]), X=w("X", [P, NCP, 2, P]), AA=w("AA", [P, NCP, 2, P]),
                BT=w("BT", [P, T]), KT=w("KT", [P, T]), VT=w("VT", [P, T]),
                MT=w("MT", [P, NCH, P]), GH=w("GH", [P, 2, 2 * NCP, HS]),
                S=view(f"S{n}", [P, NCH, P], places["U"]), RP=view(f"RP{n}", [P, T], places["X"]),
                y=view(f"y{n}", [P, T], places["BT"]), ysq=view(f"ysq{n}", [P, T], places["VT"]),
                OV=view(f"OV{n}", [P, T], places["AA"]), sd=view(f"sd{n}", [P, T], places["AA"] + 4 * T), bank=4 * n)

        t4 = 4 * T
        sets = [half_set(0, MB=o_act, MK=o_act + 4 * t4, MT=o_act + 8 * t4, GH=o_act + 10 * t4, TT=o_hid + 32 * t4, T=o_hid + 34 * t4, U=o_hid + 36 * t4,
                         X=o_hid + 38 * t4, AA=o_hid + 40 * t4, BT=o_act + 12 * t4, KT=o_act + 13 * t4, VT=o_act + 14 * t4),
                half_set(1, MB=o_whi, MK=o_whi + 4 * t4, MT=o_wlo + 2 * t4, GH=o_wlo, TT=o_wlo + 6 * t4, T=o_wlo + 4 * t4, U=o_hid + 42 * t4,
                         X=o_misc, AA=o_misc + 2 * t4, BT=o_misc + 4 * t4, KT=o_act + 15 * t4, VT=o_rstd)]
        mask4 = sumsq
        mask2 = sumsq.rearrange("p (k t) -> p k t", t=P)[:, 1:3, :]
        mask_lv = view("mask_lv", [P, len(LEVELS) + 1, P], o_acc)
        mask_bd = mask_lv[:, len(LEVELS), :]

        ps = ctx.enter_context(nc.psum_tensor("ps", [P, 8, T], f32))

        sems = {}

        def sem(name):
            if name not in sems:
                sems[name] = ctx.enter_context(nc.semaphore(name))
            return sems[name]

        raw_full = [sem(f"raw_full{i}") for i in range(RING)]
        wm_full = [sem(f"wm_full{i}") for i in range(15)]
        wm_place = wm_places()

        def wm_buf(n):
            tensor, first = [x for x in ((wm_ring, 0), (wm_early, 3), (wm_mid, 7), (wm_mid2, 13), (wm_late, 15)) if x[1] <= n][-1]
            return tensor[:, n - first, :]

        mod_accs = {SH1: (mod_acc, None), SC1: (mod_acc2, None), GT1: (mod_acc, SH1), SH2: (mod_acc3, None), SC2: (mod_acc, GT1), GT2: (mod_acc3, SH2)}

        def acc_of(vv):
            return mod_accs[vv][0][:, :]

        hi_done, lo_done = sem("hi_done"), sem("lo_done")
        unit_used = sem("unit_used")
        tensor_step, vector_step, scalar_step, pool_step = ([sem(f"{e}_step{i}") for i in range(2)] for e in ("tensor", "vector", "scalar", "pool"))
        v_chain, a_chain = sem("v_chain"), sem("a_chain")
        block = ctx.enter_context(nc.Block())

        def step_waits(eng, p):
            def on(sems_, steps):
                return lambda name: eng.wait_ge(sems_[p % 2], at(steps, p, name))
            return on(tensor_step, PE_STEPS), on(vector_step, VE_STEPS), on(scalar_step, AC_STEPS), on(pool_step, PO_STEPS)

        def ffn_sems(s):
            names = ["act_in", "silu", "hid", "hid_hi", "hid_lo", "down_tile", "x_new", "nx_sq", "nx_sum", "stat", "sd"]
            names += ["c1", "c2"] if s == 0 else ["val_read"]
            names += ["nx_hi", "nx_lo"] if s < 2 else ["rstd"]
            return {n: sem(f"f{s}_{n}") for n in names}

        @block.sync
        def _(sp):
            sp.dma_start(vec[:, :], a_vec).then_inc(sem("loaded_vec"), 16)
            for t in range(TT_):
                sp.dma_start(x_tok[:, t, :], a_x[t * P:(t + 1) * P, :]).then_inc(sem(f"loaded_x{t}"), 16)
            sp.dma_start(cs_raw[:, :, :], a_cs).then_inc(sem("loaded_cs"), 16)
            sp.dma_start(const[:, :], a_const).then_inc(sem("loaded_const"), 16)

            def load_unit(u):
                if u >= RING:
                    sp.wait_ge(lo_done, u - RING + 1)
                sp.dma_start(raw[:, u % RING, :], a_w[u]).then_inc(raw_full[u % RING], 16)

            def load_wm(i):
                n, flag, _, before = wm_place[i]
                if before is not None:
                    sp.wait_ge(sem("wm_used"), before + 1)
                sp.dma_start(wm_buf(n), a_wmod[i]).then_inc(wm_full[flag], 16)

            for i in range(2 * KT):
                load_wm(i)
                if i == 12:
                    load_unit(0)
            for i in range(2 * KT, 5 * KT):
                if i == 2 * KT + 3:
                    for u in range(1, RING):
                        load_unit(u)
                    u = RING
                    sp.wait_ge(sem("seq_mm"), KT)
                load_wm(i)
                if i == 2 * KT + WM_MID - 1:
                    sp.wait_ge(sem("wm_used"), 2 * KT)
                    sp.dma_start(xT[:, :, :], a_xt).then_inc(sem("loaded_xt"), 16)
                    load_unit(u)
                    u += 1
                if i >= 2 * KT + WM_MID and i % 2 == 1:
                    load_unit(u)
                    u += 1

            def load_through(first, last):
                n = first
                while n % RING and n < last:
                    load_unit(n)
                    n += 1
                turns = (last - n) // RING
                if turns > 1:
                    with sp.Fori(0, turns) as i:
                        for j in range(RING):
                            sp.wait_ge(lo_done, i * RING + (n + j - RING + 1))
                            sp.dma_start(raw[:, j, :], a_w[bass.ds(i * RING + (n + j), 1)].rearrange("a p n -> p (a n)")).then_inc(raw_full[j], 16)
                    n += turns * RING
                while n < last:
                    load_unit(n)
                    n += 1

            sp.wait_ge(sem("chan_mm"), KT)
            for i in range(5 * KT, 5 * KT + 4):
                load_wm(i)
            load_through(u, U_UP0 + 7)
            for i in range(5 * KT + 4, 6 * KT - 1):
                load_wm(i)
            load_through(U_UP0 + 7, U_UP0 + 11)
            load_wm(6 * KT - 1)
            load_through(U_UP0 + 11, U_UP0 + 20)
            sp.wait_ge(sem("mod_mm"), 6)
            sp.dma_start(lora[:, :, :], a_lora[:, 0:2, :]).then_inc(sem("loaded_lora"), 16)
            sp.dma_start(g_lora[:, :], a_lora[:, 2, :]).then_inc(sem("loaded_lora"), 16)
            sp.dma_start(w_pool[:, :, :], a_pool).then_inc(sem("loaded_lora"), 16)
            load_through(U_UP0 + 20, U_OUT + 2)
            sp.wait_ge(sem("za_read"), PAIRS)
            sp.wait_ge(ffn_sems(1)["stat"], 1)
            sp.dma_start(mask4[:, :], a_mask[:, 0:4 * P]).then_inc(sem("loaded_masks"), 16)
            sp.dma_start(mask_lv[:, :, :], a_mask[:, 4 * P:].rearrange("p (l t) -> p l t", t=P)).then_inc(sem("loaded_masks"), 16)
            load_through(U_OUT + 2, NU)
            for ready, n, m in Y_ORDER:
                sp.wait_ge(sem(ready), n)
                sp.dma_start(out[m * P:(m + 1) * P, :], act_out[:, m, :]).then_inc(sem("stored"), 16)
            sp.wait_ge(sem("stored"), 16 * KT)

        @block.gpsimd
        def _(pool):
            def low(u, slot):
                pool.wait_ge(hi_done, u + 1)
                nc.gpsimd.tensor_tensor(w_lo[:, slot, :], raw[:, slot, :], w_hi[:, slot, :].bitcast(f32), SUB).then_inc(lo_done, 1)

            def low_through(first, last):
                n = first
                while n % RING and n < last:
                    low(n, n % RING)
                    n += 1
                turns = (last - n) // RING
                if turns > 1:
                    with pool.Fori(0, turns) as i:
                        for j in range(RING):
                            low(i * RING + (n + j), j)
                    n += turns * RING
                while n < last:
                    low(n, n % RING)
                    n += 1

            def sum_squares(stage):
                s = ffn_sems(stage)
                for m in range(1, KT):
                    pool.wait_ge(s["nx_sq"], m + 1)
                    if m > 1:
                        pool.wait_ge(s["nx_sum"], m - 1)
                    nc.gpsimd.tensor_tensor(sumsq[:, :], sq_buf[:, 0, :] if m == 1 else sumsq[:, :], sq_buf[:, m, :], ADD).then_inc(s["nx_sum"], 1)

            low_through(0, U_UP1 + AHEAD - 1)
            sum_squares(0)
            low_through(U_UP1 + AHEAD - 1, U_IN + AHEAD - 1)
            sum_squares(1)
            low_through(U_IN + AHEAD - 1, U_OUT)
            u_next = U_OUT

            def pooling(g, win):
                def step(ins):
                    n_chain[0] += 1
                    ins.then_inc(sem("pool_chain"), 1)
                    pool.wait_ge(sem("pool_chain"), n_chain[0])

                x = pooled[:, g, :]
                pool.wait_ge(sem("in_read"), 2 + 3 * PAIRS + g + 1)
                step(nc.gpsimd.tensor_tensor(pool_b[:, PADW:PADW + 1], x[:, 0:1], ones[:, 0:1], MUL))
                step(nc.gpsimd.tensor_tensor(pool_b[:, PADW + 1:], x[:, 1:T], x[:, 0:T - 1], ADD))
                src, k = pool_b, 2
                while k < win:
                    dst = pool_b if src is not pool_b else pool_c
                    step(nc.gpsimd.tensor_tensor(dst[:, PADW:], src[:, PADW:], src[:, PADW - k:PADW + T - k], ADD))
                    src, k = dst, 2 * k
                inv = inv_count[:, g * PADW:(g + 1) * PADW]
                step(nc.gpsimd.tensor_tensor(src[:, PADW:2 * PADW], src[:, PADW:2 * PADW], inv, MUL))
                step(nc.gpsimd.tensor_tensor(src[:, 2 * PADW:], src[:, 2 * PADW:], inv[:, PADW - 1:PADW].to_broadcast([P, T - PADW]), MUL))
                nc.gpsimd.tensor_tensor(x, src[:, PADW:], x, SUB).then_inc(sem("pooled"), 1)
                pool.wait_ge(sem("pooled"), g + 1)

            n_chain = [0]
            pool.wait_ge(sem("in_read"), 2 + 3 * PAIRS)
            for b_ in (pool_b, pool_c):
                n_chain[0] += 1
                nc.gpsimd.memset(b_[:, 0:PADW], 0.0).then_inc(sem("pool_chain"), 1)
                pool.wait_ge(sem("pool_chain"), n_chain[0])
            for g in range(len(WINDOWS) - 1):
                pooling(g, WINDOWS[g])

            n_step = [0, 0]

            def pair(p):
                pe_did, ve_did, ac_did, _ = step_waits(pool, p)
                b = sets[p % 2]

                def did(name, ins):
                    n_step[p % 2] += 1
                    assert at(PO_STEPS, p, name) == n_step[p % 2]
                    ins.then_inc(pool_step[p % 2], 1)

                yield
                yield
                def joining(n):
                    if n == 2:
                        ve_did(f"L{NCP - 1}")
                    else:
                        pe_did(f"U{n - 1}b")
                    for c in range(NCP):
                        ins = nc.gpsimd.tensor_tensor(b.X[:, c, :, :], b.MB[:, c, 0:2, :], mask_lv[:, n - 1:n, :].to_broadcast([P, 2, P]), MUL)
                        if c < NCP - 1:
                            n_chain[0] += 1
                            ins.then_inc(sem("pool_chain"), 1)
                    did(f"X{n}", ins)

                joining(INVERT[0])
                if p == 0:
                    pooling(len(WINDOWS) - 1, WINDOWS[-1])
                yield
                for n in INVERT:
                    yield
                    if n < LAST:
                        joining(n + 1)
                        yield
                    yield
                for _ in range(4 + NCH + 4):
                    yield

            def closing():
                nonlocal u_next
                for name in ("GHb", "Nb", f"S{NCH - 2}", f"S{NCH - 2}"):
                    yield
                    pool.wait_ge(tensor_step[1], at(PE_STEPS, PAIRS - 1, name))
                    low(u_next, u_next % RING)
                    u_next += 1

            pool.wait_ge(sem("loaded_masks"), 32)
            in_turns(pair, closing)
            low_through(u_next, NU)
            pool.wait_ge(sem("y_gained"), KT)
            pool.wait_ge(ffn_sems(2)["rstd"], 1)
            for m in range(KT - Y_POOL, KT):
                nc.gpsimd.tensor_tensor(act_out[:, m, :], act_out[:, m, :], rstd[:, :], MUL).then_inc(sem("y_out_pool"), 1)

        @block.scalar
        def _(act):
            def after(s, n):
                act.wait_ge(s, n)

            def high(u, slot, turn, first=False):
                act.wait_ge(raw_full[slot], 16 * (turn + 1))
                if not first:
                    act.wait_ge(unit_used, u - RING + 1)
                nc.scalar.activation(w_hi[:, slot, :], raw[:, slot, :], ACT.Copy).then_inc(hi_done, 1)

            def high_n(u):
                if u < NU:
                    high(u, u % RING, u // RING, u < RING)

            n_chain = [0]

            def chain(ins):
                n_chain[0] += 1
                ins.then_inc(a_chain, 1)
                act.wait_ge(a_chain, n_chain[0])

            after(sem("loaded_vec"), 16)
            nc.scalar.activation(c_silu, v("c", 0, KT), ACT.Silu).then_inc(sem("c_silu"), 1)
            for t in range(TT_):
                after(sem(f"loaded_x{t}"), 16)
                chain(nc.scalar.activation(junk[:, :], x_tok[:, t, :], ACT.Square, accum_out=x_ss[:, t:t + 1]))
            nc.scalar.activation(x_ss, x_ss, ACT.Sqrt, bias=v("eps"), scale=1.0 / D).then_inc(sem("x_sd"), 1)
            after(sem("loaded_cs"), 16)
            nc.scalar.activation(cs_hi, cs_raw[:, :, :].rearrange("p a b -> p (a b)"), ACT.Copy).then_inc(sem("cs_hi"), 1)
            after(sem("x_rstd"), 1)
            for t in range(TT_):
                nc.scalar.activation(xn_hi[:, t * D:(t + 1) * D], x_tok[:, t, :], ACT.Copy, scale=x_ss[:, t:t + 1]).then_inc(sem("xn_hi"), 1)
            after(sem("cs_lo"), 1)
            for m in range(KT):
                b = 2 * (m % 3)
                after(sem("seq_mm"), m + 1)
                nc.scalar.activation(y_raw[:, m, 0:NCOS], ps[:, b, 0:NCOS], ACT.Copy).then_inc(sem("y_raw"), 1)
                nc.scalar.activation(y_raw[:, m, NCOS:NF], ps[:, b + 1, 0:NSIN], ACT.Copy).then_inc(sem("y_raw"), 1)
            high_n(0)
            after(sem("dc"), 1)
            nc.scalar.activation(y_hi.rearrange("p (m f) -> p m f", f=NF)[:, :, 0], y_dc, ACT.Copy).then_inc(sem("dc_hi"), 1)
            for m in range(KT):
                nc.scalar.activation(y_hi[:, m * NF + 1:(m + 1) * NF], y_raw[:, m, 1:NF], ACT.Copy, scale=gain[:, m:m + 1]).then_inc(sem("y_hi"), 1)
            for t in range(KT):
                after(sem("chan_mm"), t + 1)
                nc.scalar.activation(q_buf[:, t % 2, :], ps[:, 2 * (t % 3) + 1, 0:NSIN], ACT.Copy).then_inc(sem("q_new"), 1)
                after(sem("f_new"), t + 1)
                nc.scalar.activation(act_hi[:, t, :], f_buf[:, t % 2, :], ACT.Copy).then_inc(sem("f_hi"), 1)
                if t % 2 == 1 and t < 2 * AHEAD:
                    high_n((t + 1) // 2)

            def squares(s_new, s_sq, m, dst, ready=None):
                after(s_new, m + 1)
                if ready is not None:
                    after(*ready)
                nc.scalar.activation(dst, xT[:, m, :], ACT.Square).then_inc(s_sq, 1)

            def x0_square(m):
                squares(sem("x0_new"), sem("x0_sq"), m, sumsq[:, :] if m == 0 else sq_buf[:, m, :])

            for m in range(KT):
                high_n(U_FNET + m + AHEAD)
                if m >= SQ_LAG:
                    x0_square(m - SQ_LAG)
            for m in range(KT - SQ_LAG, KT):
                x0_square(m)

            def root(s_stat, s_sd):
                after(s_stat, 1)
                nc.scalar.activation(rstd[:, :], ps[:, 6, :], ACT.Sqrt, bias=v("eps"), scale=1.0 / D).then_inc(s_sd, 1)

            root(sem("x0_stat"), sem("x0_sd"))
            for m in range(KT):
                after(sem("t_new"), m + 1)
                if m >= 2:
                    after(sem("a_lo"), m - 1)
                nc.scalar.activation(a_buf[:, m % 2, :], t_buf[:, m % 2, :], ACT.Identity, bias=mod(SH2, m), scale=gain2[:, m:m + 1]).then_inc(sem("a_new"), 1)
                after(sem("a_new"), m + 1)
                nc.scalar.activation(act_hi[:, m, :], a_buf[:, m % 2, :], ACT.Copy).then_inc(sem("a_hi"), 1)

            def ffn(stage, u_up, u_dn):
                s = ffn_sems(stage)

                def up_pair(i, first):
                    for q in range(2):
                        j = 2 * i + q
                        for h in range(2):
                            off = u_up + 2 * q + h + AHEAD
                            high(4 * i + off, off % RING, i + off // RING)
                        if stage == 0:
                            act.wait_ge(unit_used, u_up + 2 * j + 1)
                            if not first:
                                act.wait_ge(s["hid_lo"], j - 1)
                            nc.scalar.activation(g_buf[:, q, :], ps[:, 2 * q, :], ACT.Identity, bias=b_conv(j), scale=tap(1, j)).then_inc(s["c1"], 1)
                        act.wait_ge(s["act_in"], j + 1)
                        nc.scalar.activation(g_buf[:, q, :], g_buf[:, q, :], ACT.Silu).then_inc(s["silu"], 1)
                        act.wait_ge(s["hid"], j + 1)
                        nc.scalar.activation(hid_hi[:, bass.ds(j * T, T)], g_buf[:, q, :], ACT.Copy).then_inc(s["hid_hi"], 1)

                up_pair(0, True)
                with act.Fori(1, FT // 2) as i:
                    up_pair(i, False)
                for kt in range(FT - 1):
                    high_n(u_dn + kt + AHEAD)

            def b_conv(j):
                return vec[:, bass.ds(VEC["b_conv"] + j, 1)]

            def tap(k, j):
                return vec[:, bass.ds(VEC["conv"] + k * FT + j, 1)]

            def next_input(s, m, g):
                after(s["x_new"], m + 1)
                nc.scalar.activation(act_hi[:, m, :], xT[:, m, :], ACT.Copy, scale=v(g, m)).then_inc(s["nx_hi"], 1)
                if m == KT - 1:
                    high_n(U_IN + AHEAD - 1)
                nc.scalar.activation(sq_buf[:, m, :], xT[:, m, :], ACT.Square).then_inc(s["nx_sq"], 1)

            after(sem("wm_used"), 5 * KT)
            ffn(0, U_UP0, U_DN0)
            s0 = ffn_sems(0)
            after(sem("g_both"), 1)
            for m in range(KT):
                after(s0["x_new"], m + 1)
                nc.scalar.activation(act_hi[:, m, :], xT[:, m, :], ACT.Copy, scale=g_both[:, m:m + 1]).then_inc(s0["nx_hi"], 1)
                if m == KT - 1:
                    high_n(U_UP1 + AHEAD - 1)
                nc.scalar.activation(sq_buf[:, m, :], xT[:, m, :], ACT.Square).then_inc(s0["nx_sq"], 1)
            after(s0["stat"], 1)
            nc.scalar.activation(sumsq[:, :], ps[:, 6, :], ACT.Sqrt, bias=v("eps"), scale=1.0 / D).then_inc(s0["sd"], 1)
            after(sem("mid_ms"), 1)
            nc.scalar.activation(rstd[:, :], rstd[:, :], ACT.Sqrt).then_inc(sem("mid_sd"), 1)
            ffn(1, U_UP1, U_DN1)
            s1 = ffn_sems(1)
            for m in range(KT):
                next_input(s1, m, "g_in")
            root(s1["stat"], s1["sd"])

            for i in range(len(IN_STARTS)):
                if U_IN + i + AHEAD < U_OUT:
                    high_n(U_IN + i + AHEAD)
                if i == 0:
                    after(sem("in_read"), 1)
                    nc.scalar.activation(wa[0:32, 0, :], wa[0:32, 0, :], ACT.Tanh).then_inc(sem("wa_ready"), 1)
                if i == 1:
                    after(sem("in_read"), 2)
                    nc.scalar.activation(gx[:, 0, :], gx[:, 0, :], ACT.Sigmoid).then_inc(sem("g_in"), 1)
                if 2 <= i < 2 + 3 * PAIRS and (i - 2) % 3 == 2:
                    p = (i - 2) // 3
                    after(sem("za_mm"), p + 1)
                    if p:
                        after(sem("prep"), p)
                    chain(nc.scalar.activation(sg[:, 0, :], ps[:, 4, :], ACT.Sigmoid, bias=v("w0", p)))
                    nc.scalar.activation(ag[:, 0, :], ps[:, 5, :], ACT.Sigmoid, bias=v("a0", p)).then_inc(sem("za_read"), 1)
                    after(sem("in_read"), 3 + 3 * p)
                    nc.scalar.activation(sq[:, 0, :], pk[:, 0, :], ACT.Square, scale=v("k_k", p)).then_inc(sem("sq_ready"), 1)
                    after(sem("ss_mm"), p + 1)
                    nc.scalar.activation(nr[:, 0, :], ps[:, 6, :], ACT.Sqrt).then_inc(sem("nr_ready"), 1)
                    after(sem("cs_ready"), p + 1)
                    chain(nc.scalar.activation(iv[:, 0, :], cs[:, 0, :], ACT.Exp, scale=KAPPA))
                    chain(nc.scalar.activation(sg[:, 0, :], sg[:, 0, :], ACT.Exp, scale=-KAPPA))
                    nc.scalar.activation(cs[:, 0, :], cs[:, 0, :], ACT.Exp, scale=-KAPPA).then_inc(sem("exps"), 1)
                    after(sem("g_mm"), p + 1)
                    nc.scalar.activation(rG[:, p, :], ps[:, 7, :], ACT.Copy).then_inc(sem("g_read"), 1)
            n_step = [0, 0]

            def pair(p):
                pe_did, ve_did, ac_did, po_did = step_waits(act, p)
                b = sets[p % 2]

                def did(name, ins):
                    n_step[p % 2] += 1
                    assert at(AC_STEPS, p, name) == n_step[p % 2], name
                    ins.then_inc(scalar_step[p % 2], 1)

                def copy(name, dst, bank, *pattern, **sizes):
                    pe_did(name)
                    src = ps[:, b.bank + bank, :]
                    did(name, nc.scalar.activation(dst, src.rearrange(*pattern, **sizes) if pattern else src, ACT.Copy))

                def squares_out(name, dst, half, bank):
                    copy(name, dst[:, slice(0, 2) if half == "a" else slice(2, 4), :, :], bank, "q (c h t) -> q c h t", c=2, h=2)

                copy("tA", b.AA[:, :, :, 0:HS], 0, "q (c h k) -> q c h k", c=NCP, h=2)
                copy("tK", b.KT[:, :], 2)
                copy("tV", b.VT[:, :], 3)
                yield
                yield
                squares_out("t1a", b.T, "a", 0)
                yield
                for n in INVERT:
                    squares_out(f"U{n}a", b.U, "a", 2)
                    squares_out(f"U{n}b", b.U, "b", 3)
                    yield
                    yield
                    if n < LAST:
                        squares_out(f"t{n}a", b.T, "a", 2)
                        yield
                copy("AV", b.AA[:, :, :, HS:P], 2, "q (c h k) -> q c h k", c=NCP, h=2)
                yield
                copy("GHa", b.GH[:, :, 0:4, :], 0, "q (s g k) -> q g s k", s=4, g=2)
                yield
                copy("OV", b.OV[:, :], 2)
                yield
                yield
                for _ in range(1, NCH - 1):
                    yield
                yield
                ve_did("yc")
                did("sq", nc.scalar.activation(b.ysq[:, :], b.y[:, :], ACT.Square))
                yield
                pe_did("var")
                did("sd", nc.scalar.activation(b.sd[:, :], ps[:, b.bank + 1, :], ACT.Sqrt, bias=v("gn_eps"), scale=1.0 / HS))
                yield
                ve_did("yn")
                did("affine", nc.scalar.activation(b.y[:, :], b.y[:, :], ACT.Identity, bias=v("ln_b", p), scale=v("ln_w", p)))
                yield

            def mix_hi(p):
                nc.scalar.activation(act_hi[:, p, :], rG[:, p, :], ACT.Copy).then_inc(sem("mix_hi"), 1)

            def pool_hi(g):
                after(sem("pool_mm"), g + 1)
                nc.scalar.activation(act_hi[:, PAIRS + g, :], ps[:, g, :], ACT.Copy, scale=v("pool_scale", g)).then_inc(sem("pool_hi"), 1)

            def closing():
                act.wait_ge(vector_step[0], at(VE_STEPS, PAIRS - 2, "out"))
                mix_hi(0)
                act.wait_ge(vector_step[1], at(VE_STEPS, PAIRS - 3, "out"))
                mix_hi(1)
                yield
                mix_hi(2)
                pool_hi(0)
                yield
                pool_hi(1)
                pool_hi(2)
                yield
                act.wait_ge(tensor_step[1], at(PE_STEPS, PAIRS - 1, "OV"))
                high_n(U_OUT)
                pool_hi(3)
                yield
                for u in range(U_OUT + 1, U_OUT + RING):
                    high_n(u)
                    yield

            in_turns(pair, closing)
            act.wait_ge(vector_step[1], at(VE_STEPS, PAIRS - 1, "out"))
            mix_hi(PAIRS - 1)

            for m in range(KT):
                if m:
                    high_n(U_OUT + m + AHEAD)
                squares(sem("x2_new"), sem("x2_sq"), m, sumsq[:, :] if m == 0 else sq_buf[:, m, :])
            for m in range(KT):
                nc.scalar.activation(act_hi[:, m, :], xT[:, m, :], ACT.Copy, scale=v("g_ffn2", m)).then_inc(sem("x2_hi"), 1)
            root(sem("x2_stat"), sem("x2_sd"))
            ffn(2, U_UP2, U_DN2)
            s2 = ffn_sems(2)

            def gained(m):
                nc.scalar.activation(act_out[:, m, :], xT[:, m, :], ACT.Copy, scale=v("g_last", m)).then_inc(sem("y_gained"), 1)

            for m in range(KT):
                squares(s2["x_new"], s2["nx_sq"], m, sumsq[:, :] if m == 0 else sq_buf[:, m, :])
                if m:
                    gained(m - 1)
            gained(KT - 1)
            root(s2["stat"], s2["sd"])

        @block.vector
        def _(ve):
            after = ve.wait_ge
            count = {}

            def chain(ins, name=None):
                s = v_chain if name is None else sem(name)
                count[name] = count.get(name, 0) + 1
                ins.then_inc(s, 1)
                ve.wait_ge(s, count[name])

            def tt(o, a, b, op, name=None):
                chain(nc.vector.tensor_tensor(o, a, b, op), name)

            def stt(o, a, s, b, op0, op1, name=None):
                chain(nc.vector.scalar_tensor_tensor(o, a, s, b, op0, op1), name)

            def tsc(o, a, s1, s2, op0, op1, name=None):
                chain(nc.vector.tensor_scalar(o, a, s1, s2, op0, op1), name)

            after(sem("x_sd"), 1)
            chain(nc.vector.reciprocal(x_ss, x_ss), "x_rstd")
            after(sem("cs_hi"), 1)
            tt(cs_lo, cs_raw[:, :, :].rearrange("p a b -> p (a b)"), cs_hi.bitcast(f32), SUB, "cs_lo")
            for t in range(TT_):
                after(sem("xn_hi"), t + 1)
                stt(xn_lo[:, t * D:(t + 1) * D], x_tok[:, t, :], x_ss[:, t:t + 1], xn_hi[:, t * D:(t + 1) * D].bitcast(f32), MUL, SUB, "xn_lo")
            after(sem("c_silu"), 1)

            def wm(i):
                vv, k = divmod(i, KT)
                n, flag, turn, _ = wm_place[i]
                acc = acc_of(vv)
                after(wm_full[flag], 16 * turn)
                if k == 0:
                    if mod_accs[vv][1] is not None:
                        after(sem("mod_mm"), mod_accs[vv][1] + 1)
                    tsc(acc, wm_buf(n), c_silu[:, 0:1], None, MUL, ALU.bypass, "wm_used")
                else:
                    stt(acc, wm_buf(n), c_silu[:, k:k + 1], acc, MUL, ADD, "wm_used")

            def mod_out(vv):
                after(sem("mod_mm"), vv + 1)
                tt(mods[:, vv * KT:(vv + 1) * KT], ps[:, 7, vv * KT:(vv + 1) * KT], v("b_mod", vv * KT, KT), ADD, "mod_read")

            for vv in (SH1, SC1):
                for k in range(KT):
                    wm(vv * KT + k)
            mod_out(SH1)
            for k in range(3):
                wm(GT1 * KT + k)
            mod_out(SC1)
            stt(gain, mods[:, SC1 * KT:(SC1 + 1) * KT], 1.0, v("g_mix", 0, KT), ADD, MUL)
            tsc(sh_dc, mods[:, SH1 * KT:(SH1 + 1) * KT], float(T), None, MUL, ALU.bypass)
            after(sem("y_raw"), 2 * KT)
            tt(y_dc, y_raw[:, :, 0], gain, MUL)
            tt(y_dc, y_dc, sh_dc, ADD, "dc")
            after(sem("dc_hi"), 1)
            tt(y_lo.rearrange("p (m f) -> p m f", f=NF)[:, :, 0], y_dc, y_hi.rearrange("p (m f) -> p m f", f=NF)[:, :, 0].bitcast(f32), SUB)
            for m in range(KT):
                after(sem("y_hi"), m + 1)
                stt(y_lo[:, m * NF + 1:(m + 1) * NF], y_raw[:, m, 1:NF], gain[:, m:m + 1], y_hi[:, m * NF + 1:(m + 1) * NF].bitcast(f32), MUL, SUB, "y_lo")

            def f_low(t):
                after(sem("f_hi"), t + 1)
                tt(act_lo[:, t, :], f_buf[:, t % 2, :], act_hi[:, t, :].bitcast(f32), SUB, "f_lo")

            for t in range(KT):
                b = 2 * (t % 3)
                after(sem("q_new"), t + 1)
                f = f_buf[:, t % 2, :]
                tt(f[:, 0:NSIN], ps[:, b, 0:NSIN], q_buf[:, t % 2, :], SUB)
                chain(nc.vector.tensor_copy(f[:, NSIN:NSIN + 1], ps[:, b, NSIN:NSIN + 1]))
                tt(f[:, NSIN + 1:T][:, ::-1], ps[:, b, 1:NSIN], q_buf[:, t % 2, 1:NSIN], ADD, "f_new")
                if t:
                    f_low(t - 1)
            f_low(KT - 1)
            for k in range(3, KT):
                wm(GT1 * KT + k)
            mod_out(GT1)
            after(sem("loaded_xt"), 16)
            after(sem("chan_mm"), KT)
            done = 3 * KT

            def x0_sum(m):
                after(sem("x0_sq"), m + 1)
                tt(sumsq[:, :], sumsq[:, :], sq_buf[:, m, :], ADD, "x0_sum")

            for m in range(KT):
                for i in range(done, min(done + 3, 5 * KT)):
                    wm(i)
                done += 3
                if m == 5:
                    mod_out(SH2)
                if m == KT - 1:
                    mod_out(SC2)
                    stt(gain2, mods[:, SC2 * KT:(SC2 + 1) * KT], 1.0, v("g_ffn", 0, KT), ADD, MUL)
                if m > SQ_LAG:
                    x0_sum(m - SQ_LAG)
                if m == KT - 1:
                    x0_sum(KT - SQ_LAG)
                after(unit_used, U_FNET + m + 1)
                stt(xT[:, m, :], ps[:, fnet_bank(m), :], mod(GT1, m), xT[:, m, :], MUL, ADD, "x0_new")
            for m in range(KT - SQ_LAG + 1, KT):
                x0_sum(m)

            def inverse(s_sd, name=None):
                after(s_sd, 1)
                chain(nc.vector.reciprocal(rstd[:, :], rstd[:, :]), name)

            inverse(sem("x0_sd"))
            def a_low(m):
                after(sem("a_hi"), m + 1)
                tt(act_lo[:, m, :], a_buf[:, m % 2, :], act_hi[:, m, :].bitcast(f32), SUB, "a_lo")

            for m in range(KT):
                if m >= 2:
                    after(sem("a_new"), m - 1)
                tt(t_buf[:, m % 2, :], xT[:, m, :], rstd[:, :], MUL, "t_new")
                if m:
                    a_low(m - 1)
            a_low(KT - 1)

            def ffn(stage, u_up):
                s = ffn_sems(stage)

                def tap(k, j):
                    return vec[:, bass.ds(VEC["conv"] + k * FT + j, 1)]

                def up_pair(i, first):
                    for q in range(2):
                        j = 2 * i + q
                        gate, val, g, u_ = ps[:, 2 * q, :], ps[:, 2 * q + 1, :], g_buf[:, q, :], u_buf[:, q, :]
                        if stage == 0:
                            ve.wait_ge(s["c1"], j + 1)
                            nc.vector.scalar_tensor_tensor(g[:, 1:T], gate[:, 0:T - 1], tap(0, j), g[:, 1:T], MUL, ADD).then_inc(s["c2"], 1)
                            ve.wait_ge(s["c2"], j + 1)
                            nc.vector.scalar_tensor_tensor(g[:, 0:T - 1], gate[:, 1:T], tap(2, j), g[:, 0:T - 1], MUL, ADD).then_inc(s["act_in"], 1)
                            ve.wait_ge(s["silu"], j + 1)
                            ve.wait_ge(unit_used, u_up + 2 * j + 2)
                            nc.vector.tensor_tensor(g, val, g, MUL).then_inc(s["hid"], 1)
                        else:
                            ve.wait_ge(unit_used, u_up + 2 * j + 1)
                            if not first:
                                ve.wait_ge(s["hid_lo"], j - 1)
                            nc.vector.tensor_tensor(g, gate, rstd[:, :], MUL).then_inc(s["act_in"], 1)
                            ve.wait_ge(unit_used, u_up + 2 * j + 2)
                            nc.vector.tensor_tensor(u_, val, rstd[:, :], MUL).then_inc(s["val_read"], 1)
                            ve.wait_ge(s["silu"], j + 1)
                            ve.wait_ge(s["val_read"], j + 1)
                            nc.vector.tensor_tensor(g, g, u_, MUL).then_inc(s["hid"], 1)
                        ve.wait_ge(s["hid_hi"], j + 1)
                        nc.vector.tensor_tensor(hid_lo[:, bass.ds(j * T, T)], g, hid_hi[:, bass.ds(j * T, T)].bitcast(f32), SUB).then_inc(s["hid_lo"], 1)

                up_pair(0, True)
                if stage == 0:
                    for i in range(1, 4):
                        for k in range(3 * i - 3, min(3 * i, KT)):
                            wm(GT2 * KT + k)
                        up_pair(i, False)
                    mod_out(GT2)
                if stage == 1:
                    ve.wait_ge(ffn_sems(0)["sd"], 1)
                    chain(nc.vector.reciprocal(sumsq[:, :], sumsq[:, :]))
                    for m in range(KT):
                        stt(xT[:, m, :], xT[:, m, :], v("g_mid", m), sumsq[:, :], MUL, MUL)
                with ve.Fori(4 if stage == 0 else 1, FT // 2) as i:
                    up_pair(i, False)
                ve.wait_ge(s["hid_lo"], FT)

            def next_x(stage, scale, g):
                s, f = ffn_sems(stage), f"f{stage}_"
                gains = g_both if stage == 0 else None if g is None else v(g, 0, KT)

                def low(m):
                    after(s["nx_hi"], m + 1)
                    stt(act_lo[:, m, :], xT[:, m, :], gains[:, m:m + 1], act_hi[:, m, :].bitcast(f32), MUL, SUB, f + "nx_lo")

                def add_square(m):
                    after(s["nx_sq"], m + 1)
                    tt(sumsq[:, :], sumsq[:, :], sq_buf[:, m, :], ADD, f + "nx_sum")

                for m in range(KT):
                    after(s["down_tile"], m + 1)
                    stt(xT[:, m, :], ps[:, m, :], mod(GT2, m) if scale is None else scale, xT[:, m, :], MUL, ADD, f + "x_new")
                    if gains is not None and m:
                        low(m - 1)
                    if gains is None and m > 1:
                        add_square(m - 1)
                if gains is None:
                    add_square(KT - 1)
                    inverse(s["sd"], f + "rstd")
                    return
                if gains is not None:
                    low(KT - 1)
                if stage == 0:
                    after(s["nx_sq"], 1)
                    tsc(mid_sq[:, :], sq_buf[:, 0, :], g_mid2[:, 0:1], None, MUL, ALU.bypass)
                    for m in range(1, KT):
                        after(s["nx_sq"], m + 1)
                        stt(mid_sq[:, :], sq_buf[:, m, :], g_mid2[:, m:m + 1], mid_sq[:, :], MUL, ADD, "mid_sum")
                    after(s["sd"], 1)
                    tsc(rstd[:, :], ps[:, 6, :], EPS / D, EPS * EPS, MUL, ADD)
                    after(sem("mid_stat"), 1)
                    stt(rstd[:, :], ps[:, 7, :], 1.0 / D, rstd[:, :], MUL, ADD, "mid_ms")
                    after(sem("mid_sd"), 1)
                    chain(nc.vector.reciprocal(rstd[:, :], rstd[:, :]))
                    return
                inverse(s["sd"])

            ffn(0, U_UP0)
            tt(g_mid2, v("g_mid", 0, KT), v("g_mid", 0, KT), MUL)
            tt(g_both, v("g_mid", 0, KT), v("g_ffn1", 0, KT), MUL, "g_both")
            next_x(0, None, None)
            ffn(1, U_UP1)
            next_x(1, 0.5, "g_in")

            chain(nc.vector.memset(pads[:, :, 0:1], 0.0))
            chain(nc.vector.memset(scan_mask[:, 0, :], 1.0))
            chain(nc.vector.memset(scan_mask[:, 0, 0:T:CH], 0.0))
            tsc(one_minus_ka, v("k_a", 0, PAIRS), -1.0, 1.0, MUL, ADD)

            def shifted(i, dst):
                after(unit_used, U_IN + i + 1)
                pad = pads[:, i % 2, :]
                tt(pad[:, 1:T + 1], ps[:, i % 4, :], rstd[:, :], MUL)
                tt(diff[:, :], pad[:, 0:T], pad[:, 1:T + 1], SUB)
                stt(dst, diff[:, :], v("mu", i), pad[:, 1:T + 1], MUL, ADD, "in_read")

            def pool_input(g):
                i = 2 + 3 * PAIRS + g
                after(unit_used, U_IN + i + 1)
                tt(pooled[:, g, :], ps[:, i % 4, :], rstd[:, :], MUL, "in_read")

            shifted(0, wa[:, 0, :])
            shifted(1, gx[:, 0, :])
            for p in range(PAIRS):
                i = 2 + 3 * p
                shifted(i, pk[:, 0, :])
                shifted(i + 1, rR[:, p, :])
                shifted(i + 2, rV[:, p, :])
                after(sem("za_read"), p + 1)
                chain(nc.vector.tensor_tensor_scan(cs[:, 0, :], scan_mask[:, 0, :], sg[:, 0, :], 0.0, MUL, ADD))
                tt(sg[:, 0, :], cs[:, 0, :], sg[:, 0, :], SUB, "cs_ready")
                after(sem("nr_ready"), p + 1)
                tsc(nr[:, 0, :], nr[:, 0, :], L2_EPS, None, MAX, ALU.bypass)
                chain(nc.vector.reciprocal(nr[:, 0, :], nr[:, 0, :]))
                stt(nr[:, 0, :], pk[:, 0, :], v("k_k", p), nr[:, 0, :], MUL, MUL)
                after(sem("exps"), p + 1)
                stt(rA[:, p, :], nr[:, 0, :], -1.0, sg[:, 0, :], MUL, MUL)
                tt(sq[:, 0, :], nr[:, 0, :], ag[:, 0, :], MUL)
                tt(rB[:, p, :], sq[:, 0, :], iv[:, 0, :], MUL)
                tsc(ag[:, 0, :], ag[:, 0, :], v("k_a", p), one_minus_ka[:, p:p + 1], MUL, ADD)
                tt(ag[:, 0, :], ag[:, 0, :], pk[:, 0, :], MUL)
                tt(rK[:, p, :], ag[:, 0, :], iv[:, 0, :], MUL)
                if p == PAIRS - 1:
                    pool_input(0)
                stt(pk[:, 0, :], rR[:, p, :], v("r_k", p), ag[:, 0, :], MUL, MUL, "rk_ready")
                chain(nc.vector.tensor_copy(pchunk[:, p, :], cs[:, 0, CH - 1:T:CH]))
                tt(rR[:, p, :], rR[:, p, :], cs[:, 0, :], MUL)
                if p == PAIRS - 1:
                    pool_input(1)
                after(sem("bonus_mm"), p + 1)
                tt(rBonus[:, p, :], ps[:, 6, :], rV[:, p, :], MUL, "prep")
            pool_input(2)
            pool_input(3)

            after(unit_used, U_OUT)
            ve.sem_inc(sem("in_done"), 1)
            after(sem("loaded_masks"), 32)
            n_step = [0, 0]

            def pair(p):
                pe_did, ve_did, ac_did, po_did = step_waits(ve, p)
                b = sets[p % 2]

                def did(name, ins):
                    n_step[p % 2] += 1
                    assert at(VE_STEPS, p, name) == n_step[p % 2], name
                    ins.then_inc(vector_step[p % 2], 1)

                def bank(k, n=1):
                    return ps[:, b.bank + k, :]

                def bank4(k):
                    return bank(k).rearrange("q (c h t) -> q c h t", c=2, h=2)

                halves = (("a", slice(0, 2)), ("b", slice(2, 4)))
                pe_did("tB")
                if p >= 2:
                    ve.wait_ge(vector_step[p % 2], at(VE_STEPS, p - 2, "out"))
                did("tB", nc.vector.tensor_copy(b.BT[:, :], bank(1)))
                yield
                for k, M in (("L", b.MB), ("K", b.MK)):
                    for i in range(NCP):
                        c0, h = i // 2 * 2, i % 2
                        pe_did(f"{k}{i}")
                        did(f"{k}{i}", nc.vector.tensor_tensor(M[:, c0:c0 + 2, h:4:2, :], bank4(i), mask2.unsqueeze(1).to_broadcast([P, 2, 2, P]), MUL))
                ve_did(f"L{NCP - 1}")
                for half, c in halves:
                    chain(nc.vector.tensor_tensor(b.TT[:, c, :, :], b.MB[:, c, 0:2, :], mask_lv[:, 0:1, :].unsqueeze(1).to_broadcast([P, 2, 2, P]), MUL))
                    did(f"D1{half}", nc.vector.tensor_tensor(b.TT[:, c, :, :], b.TT[:, c, :, :],
                                                            ident.unsqueeze(1).unsqueeze(1).to_broadcast([P, 2, 2, P]), ADD))
                yield
                pe_did("t1b")
                did("t1b", nc.vector.tensor_copy(b.T[:, 2:4, :, :], bank4(1)))
                yield
                for n in INVERT:
                    yield
                    for k, (half, c) in enumerate(halves):
                        pe_did(f"D{n}{half}")
                        did(f"D{n}{half}", nc.vector.tensor_tensor(b.TT[:, c, :, :], bank4(k), b.TT[:, c, :, :], ADD))
                    yield
                    if n < LAST:
                        pe_did(f"t{n}b")
                        did(f"t{n}b", nc.vector.tensor_copy(b.T[:, 2:4, :, :], bank4(3)))
                        yield
                yield
                pe_did("GHb")
                did("GHb", nc.vector.tensor_copy(b.GH[:, :, 4:8, :], bank(1).rearrange("q (s g k) -> q g s k", s=4, g=2)))
                yield
                pe_did("RP")
                did("RP", nc.vector.tensor_tensor(b.RP[:, :], bank(3), rR[:, p, :], ADD))
                yield
                for half, k, odd in (("a", 0, 0), ("b", 1, 1)):
                    pe_did(f"MT{half}")
                    m4 = b.MT[:, odd:NCH:2, :]
                    chain(nc.vector.tensor_tensor(m4, bank(k).rearrange("q (c t) -> q c t", c=4), ident.unsqueeze(1).to_broadcast([P, 4, P]), ADD))
                    did(f"MT{half}", nc.vector.tensor_tensor(m4, m4, mask_bd.unsqueeze(1).to_broadcast([P, 4, P]), MUL))
                for half, k, odd in (("a", 3, 0), ("b", 2, 1)):
                    pe_did(f"N{half}")
                    for c in range(odd, NCH, 2):
                        ins = nc.vector.scalar_tensor_tensor(b.S[:, c, :], bank(k)[:, (c // 2) * P:(c // 2 + 1) * P], pchunk[:, p, c:c + 1], mask_bd, MUL, MUL)
                        if c < NCH - 2 + odd:
                            ins.then_inc(sem("n_chain"), 1)
                    did(f"N{half}", ins)
                yield
                for c in range(1, NCH - 1):
                    pe_did(f"S{c}")
                    ve_did("Nb")
                    did(f"S{c}", nc.vector.scalar_tensor_tensor(b.S[:, c, :], bank((c + 1) % 2)[:, 0:P], pchunk[:, p, c:c + 1], b.S[:, c, :], MUL, ADD))
                    yield
                ac_did("OV")
                pe_did("Y")
                chain(nc.vector.tensor_copy(b.y[:, 0:CH], b.OV[:, 0:CH]))
                did("Y", nc.vector.tensor_tensor(b.y[:, CH:T], bank(3)[:, CH:T], b.OV[:, CH:T], ADD))
                yield
                pe_did("mean")
                ve_did("Y")
                did("yc", nc.vector.scalar_tensor_tensor(b.y[:, :], bank(0), -1.0 / HS, b.y[:, :], MUL, ADD))
                yield
                ac_did("sd")
                chain(nc.vector.reciprocal(b.sd[:, :], b.sd[:, :]))
                did("yn", nc.vector.tensor_tensor(b.y[:, :], b.y[:, :], b.sd[:, :], MUL))
                yield
                ac_did("affine")
                chain(nc.vector.tensor_tensor(b.y[:, :], b.y[:, :], rBonus[:, p, :], ADD))
                did("out", nc.vector.tensor_tensor(rG[:, p, :], b.y[:, :], rG[:, p, :], MUL))
                yield

            def mix_lo(p):
                after(sem("mix_hi"), p + 1)
                tt(act_lo[:, p, :], rG[:, p, :], act_hi[:, p, :].bitcast(f32), SUB, "mix_lo")

            def pool_lo(g):
                after(sem("pool_hi"), g + 1)
                stt(act_lo[:, PAIRS + g, :], ps[:, g, :], v("pool_scale", g), act_hi[:, PAIRS + g, :].bitcast(f32), MUL, SUB, "pool_lo")

            def closing():
                yield
                mix_lo(0)
                mix_lo(1)
                yield
                mix_lo(2)
                pool_lo(0)
                yield
                pool_lo(1)
                pool_lo(2)
                yield
                ve.wait_ge(tensor_step[1], at(PE_STEPS, PAIRS - 1, "Nb"))
                pool_lo(3)

            in_turns(pair, closing)
            mix_lo(PAIRS - 1)

            for m in range(KT):
                after(unit_used, U_OUT + m + 1)
                tt(xT[:, m, :], ps[:, m % 4, :], xT[:, m, :], ADD, "x2_new")
                if m:
                    after(sem("x2_sq"), m + 1)
                    tt(sumsq[:, :], sumsq[:, :], sq_buf[:, m, :], ADD, "x2_sum")
            for m in range(KT):
                after(sem("x2_hi"), m + 1)
                stt(act_lo[:, m, :], xT[:, m, :], v("g_ffn2", m), act_hi[:, m, :].bitcast(f32), MUL, SUB, "x2_lo")
            inverse(sem("x2_sd"))
            ffn(2, U_UP2)
            next_x(2, 0.5, None)
            after(sem("y_gained"), KT)
            for m in range(KT - Y_POOL):
                tt(act_out[:, m, :], act_out[:, m, :], rstd[:, :], MUL, "y_out")

        @block.tensor
        def _(pe):
            after = pe.wait_ge

            def three(o, wh, wl, xh, xl, start, stop):
                nc.tensor.matmul(o, wh, xh, start=start, stop=False)
                nc.tensor.matmul(o, wh, xl, start=False, stop=False)
                return nc.tensor.matmul(o, wl, xh, start=False, stop=stop)

            def blk(slot, b):
                return w_hi[:, slot, b * P:(b + 1) * P], w_lo[:, slot, b * P:(b + 1) * P]

            def mod_columns(vv):
                after(sem("wm_used"), KT * (vv + 1))
                if vv:
                    after(sem("mod_read"), vv)
                for m in range(KT):
                    last = nc.tensor.matmul(ps[:, 7, vv * KT + m:vv * KT + m + 1], acc_of(vv)[:, m * P:(m + 1) * P], ones[:, 0:1], start=True, stop=True)
                last.then_inc(sem("mod_mm"), 1)

            after(sem("cs_lo"), 1)
            for m in range(KT):
                b = 2 * (m % 3)
                if m >= 3:
                    after(sem("y_raw"), 2 * (m - 2))
                for bank, c0, n in ((b, 0, NCOS), (b + 1, NCOS, NSIN)):
                    for k in range(TT_):
                        after(sem("xn_lo"), k + 1)
                        w = slice(k * D + m * P, k * D + (m + 1) * P)
                        x = slice(k * NF + c0, k * NF + c0 + n)
                        last = three(ps[:, bank, 0:n], xn_hi[:, w], xn_lo[:, w], cs_hi[:, x], cs_lo[:, x], k == 0, k == TT_ - 1)
                last.then_inc(sem("seq_mm"), 1)
                if m == KT // 2:
                    after(sem("loaded_const"), 16)
                    mod_columns(SH1)
            mod_columns(SC1)
            after(lo_done, U_DFT + 1)
            for t in range(KT):
                g, mm = divmod(t, 2)
                b = 2 * (t % 3)
                after(sem("y_lo"), 2 * g + 2)
                if t >= 3:
                    after(sem("f_new"), t - 2)
                for f, c0, n in ((0, 0, NCOS), (1, NCOS, NSIN)):
                    for kk in range(2):
                        x = slice((2 * g + kk) * NF + c0, (2 * g + kk) * NF + c0 + n)
                        last = three(ps[:, b + f, 0:n], *blk(0, 4 * f + 2 * kk + mm), y_hi[:, x], y_lo[:, x], kk == 0, kk == 1)
                last.then_inc(sem("chan_mm"), 1)
            after(sem("chan_mm"), KT)
            pe.sem_inc(unit_used, 1)

            def unit_by_output(u, slot, bank, ready=None):
                after(lo_done, u + 1)
                for k in range(KT):
                    if ready is not None:
                        after(ready, k + 1)
                    last = three(ps[:, bank, :], *blk(slot, k), act_hi[:, k, :], act_lo[:, k, :], k == 0, k == KT - 1)
                last.then_inc(unit_used, 1)

            MOD_TILES = {1: GT1, 3: SH2, KT - 2: SC2}
            for m in range(KT):
                if m == KT - 1:
                    after(sem("x0_new"), 1)
                unit_by_output(U_FNET + m, (U_FNET + m) % RING, fnet_bank(m), sem("f_lo") if m == 0 else None)
                if m in MOD_TILES:
                    mod_columns(MOD_TILES[m])

            def stat(s_sum, n, s_stat, bank=6, sums=sumsq[:, :]):
                after(s_sum, n)
                nc.tensor.matmul(ps[:, bank, :], ones, sums, start=True, stop=True).then_inc(s_stat, 1)

            stat(sem("x0_sum"), KT - 1, sem("x0_stat"))

            def ffn(stage, u_up, u_dn, ready, mid):
                s = ffn_sems(stage)

                def up_pair(i, first):
                    for q in range(2):
                        j = 2 * i + q
                        for h in range(2):
                            off = u_up + 2 * q + h
                            if not first:
                                if stage == 0:
                                    pe.wait_ge(s["act_in"] if h == 0 else s["hid"], j - 1)
                                else:
                                    pe.wait_ge(s["act_in"] if h == 0 else s["val_read"], j - 1)
                            unit_by_output(4 * i + off, off % RING, 2 * q + h, ready if first and q == 0 and h == 0 else None)
                        if first and q == 0 and stage > 0:
                            mid()

                up_pair(0, True)
                if stage == 0:
                    for i in range(1, 4):
                        up_pair(i, False)
                    mid()
                with pe.Fori(4 if stage == 0 else 1, FT // 2) as i:
                    up_pair(i, False)

                def down(kt, u, slot, x, start, stop, signal=True):
                    after(lo_done, u + 1)
                    after(s["hid_lo"], kt + 1)
                    for m in range(KT):
                        last = three(ps[:, m, :], *blk(slot, m), hid_hi[:, x], hid_lo[:, x], start, stop)
                    last.then_inc(unit_used, 1)

                after(lo_done, u_dn + 1)
                for m in (4, 5, 6, 7, 0, 1, 2, 3):
                    if m == 0:
                        after(s["hid"], FT)
                    last = three(ps[:, m, :], *blk(u_dn % RING, m), hid_hi[:, 0:T], hid_lo[:, 0:T], True, False)
                last.then_inc(unit_used, 1)
                for kt in range(1, 4):
                    down(kt, u_dn + kt, (u_dn + kt) % RING, slice(kt * T, (kt + 1) * T), False, False)
                with pe.Fori(1, (FT - 2) // 4) as i:
                    for j in range(4):
                        down(4 * i + j, 4 * i + (u_dn + j), (u_dn + j) % RING, bass.ds((4 * i + j) * T, T), False, False)
                after(lo_done, u_dn + FT)
                after(s["hid_lo"], FT)
                for m in range(KT):
                    for kt in (FT - 2, FT - 1):
                        x = slice(kt * T, (kt + 1) * T)
                        last = three(ps[:, m, :], *blk((u_dn + kt) % RING, m), hid_hi[:, x], hid_lo[:, x], False, kt == FT - 1)
                    last.then_inc(s["down_tile"], 1)
                after(s["down_tile"], KT)
                pe.sem_inc(unit_used, 2)

            ffn(0, U_UP0, U_DN0, sem("a_lo"), lambda: mod_columns(GT2))
            s0, s1, s2 = (ffn_sems(i) for i in range(3))

            def mid_stats():
                after(s0["x_new"], KT)
                stat(s0["nx_sum"], KT - 1, s0["stat"])
                stat(sem("mid_sum"), KT - 1, sem("mid_stat"), 7, mid_sq[:, :])

            ffn(1, U_UP1, U_DN1, s0["nx_lo"], mid_stats)

            def small_products(i):
                if 2 <= i < 2 + 3 * PAIRS and (i - 2) % 3 == 1:
                    p = (i - 2) // 3
                    cols = slice(p * P, (p + 1) * P)
                    after(sem("wa_ready"), 1)
                    after(sem("loaded_lora"), 48)
                    if p:
                        after(sem("za_read"), p)
                    nc.tensor.matmul(ps[:, 4, :], lora[:, 0, cols], wa[:, 0, :], start=True, stop=True)
                    nc.tensor.matmul(ps[:, 5, :], lora[:, 1, cols], wa[:, 0, :], start=True, stop=True).then_inc(sem("za_mm"), 1)
                    after(sem("g_in"), 1)
                    if p:
                        after(sem("g_read"), p)
                    nc.tensor.matmul(ps[:, 7, :], g_lora[:, cols], gx[:, 0, :], start=True, stop=True).then_inc(sem("g_mm"), 1)
                if 2 <= i < 2 + 3 * PAIRS and (i - 2) % 3 == 2:
                    p = (i - 2) // 3
                    after(sem("sq_ready"), p + 1)
                    if p:
                        after(sem("prep"), p)
                    nc.tensor.matmul(ps[:, 6, :], bones, sq[:, 0, :], start=True, stop=True).then_inc(sem("ss_mm"), 1)
                if 5 <= i < 5 + 3 * PAIRS and (i - 5) % 3 == 1:
                    p = (i - 5) // 3
                    after(sem("rk_ready"), p + 1)
                    nc.tensor.matmul(ps[:, 6, :], bones, pk[:, 0, :], start=True, stop=True).then_inc(sem("bonus_mm"), 1)

            for i in range(len(IN_STARTS)):
                if i == 0:
                    after(s1["x_new"], KT)
                if i >= 4:
                    after(sem("in_read"), i - 3)
                unit_by_output(U_IN + i, (U_IN + i) % RING, i % 4, s1["nx_lo"] if i == 0 else None)
                if i == 0:
                    stat(s1["nx_sum"], KT - 1, s1["stat"])
                small_products(i)

            after(sem("in_done"), 1)
            n_step = [0, 0]

            def pair(p):
                _, ve_did, ac_did, po_did = step_waits(pe, p)
                b = sets[p % 2]

                def did(name, ins):
                    n_step[p % 2] += 1
                    assert at(PE_STEPS, p, name) == n_step[p % 2], name
                    ins.then_inc(tensor_step[p % 2], 1)

                def bank(k):
                    return ps[:, b.bank + k, :]

                for k, (name, src) in enumerate((("tA", rA), ("tB", rB), ("tK", rK), ("tV", rV))):
                    if p >= 2:
                        steps, names, read = ((vector_step, VE_STEPS, "yc"), (scalar_step, AC_STEPS, "sd"), (scalar_step, AC_STEPS, "OV"), (vector_step, VE_STEPS, "Y"))[k]
                        pe.wait_ge(steps[p % 2], at(names, p - 2, read))
                    for c in range(NCP):
                        cols = slice(c * P, (c + 1) * P)
                        last = nc.tensor.transpose(bank(k)[:, cols], src[:, p, cols], ident)
                    did(name, last)
                yield
                for k, src in (("L", rB), ("K", rK)):
                    for i in range(NCP):
                        c0, h = i // 2 * 2, i % 2
                        r = slice(h * HS, (h + 1) * HS)
                        if k == "K":
                            ve_did(f"L{i}")
                        elif i == 1:
                            ve_did("tB")
                        else:
                            ac_did({0: "tA", 2: "tK", 3: "tV"}[i])
                        for c in (c0, c0 + 1):
                            cols = slice(c * P, (c + 1) * P)
                            last = nc.tensor.matmul(bank(i)[:, (c - c0) * 2 * P:(c - c0 + 1) * 2 * P], src[r, p, cols], rAR[r, :, p, cols], start=True, stop=True)
                        did(f"{k}{i}", last)
                yield

                def systems(half):
                    c0 = 0 if half == "a" else 2
                    return [(c, h, slice(((c - c0) * 2 + h) * P, ((c - c0) * 2 + h + 1) * P)) for c in (c0, c0 + 1) for h in range(2)]

                def flip(n, k0):
                    for k, half in enumerate("ab"):
                        ve_did(f"D{n}{half}")
                        for c, h, o in systems(half):
                            last = nc.tensor.transpose(bank(k0 + k)[:, o], b.TT[:, c, h, :], ident)
                        did(f"t{n}{half}", last)

                flip(1, 0)
                yield
                for n in INVERT:
                    for k, half in enumerate("ab"):
                        po_did(f"X{n}")
                        (ac_did if half == "a" else ve_did)(f"t{n - 1}{half}")
                        for c, h, o in systems(half):
                            last = nc.tensor.matmul(bank(2 + k)[:, o], b.X[:, c, h, :], b.T[:, c, h, :], start=True, stop=True)
                        did(f"U{n}{half}", last)
                    yield
                    for k, half in enumerate("ab"):
                        ac_did(f"U{n}{half}")
                        for c, h, o in systems(half):
                            last = nc.tensor.matmul(bank(k)[:, o], b.U[:, c, h, :], b.TT[:, c, h, :], start=True, stop=True)
                        did(f"D{n}{half}", last)
                    yield
                    if n < LAST:
                        flip(n, 2)
                        yield
                for c in range(NCP):
                    for h in range(2):
                        last = nc.tensor.matmul(bank(2)[:, (2 * c + h) * HS:(2 * c + h + 1) * HS], b.MK[:, c, h, :], b.VT[:, c * P + h * HS:c * P + (h + 1) * HS], start=True, stop=True)
                did("AV", last)
                yield
                ac_did("AV")
                for k, half in enumerate("ab"):
                    ve_did(f"D{LAST}{half}")
                    for c, h, o in systems(half):
                        last = nc.tensor.matmul(bank(k)[:, o], b.TT[:, c, h, :], b.AA[:, c, h, :], start=True, stop=True)
                    did(f"GH{half}", last)
                yield
                ac_did("GHa")
                ve_did("GHb")
                for c in range(NCP):
                    for h in range(2):
                        r = slice(h * HS, (h + 1) * HS)
                        last = nc.tensor.matmul(ps[r, b.bank + 3, c * P:(c + 1) * P], b.GH[:, 0, 2 * c + h, :], b.MB[:, c, 2 + h, :], start=True, stop=True)
                did("RP", last)
                for c in range(NCP):
                    for h in range(2):
                        r, o = slice(h * HS, (h + 1) * HS), slice(c * P, (c + 1) * P)
                        nc.tensor.matmul(ps[r, b.bank + 2, o], b.GH[:, 1, 2 * c + h, :], b.MB[:, c, 2 + h, :], start=True, stop=False)
                        last = nc.tensor.matmul(ps[r, b.bank + 2, o], b.VT[:, c * P + h * HS:c * P + (h + 1) * HS], b.MK[:, c, 2 + h, :], start=False, stop=True)
                did("OV", last)
                yield
                for half, k, odd in (("a", 0, 0), ("b", 1, 1)):
                    for c in range(odd, NCH, 2):
                        cp, r = c // 2, slice(odd * CH, (odd + 1) * CH)
                        last = nc.tensor.matmul(bank(k)[:, cp * P:(cp + 1) * P], b.GH[r, 0, 2 * cp:2 * cp + 2, :].rearrange("q s k -> q (s k)"), b.BT[r, cp * P:(cp + 1) * P], start=True, stop=True)
                    did(f"MT{half}", last)
                for half, k, odd in (("a", 3, 0), ("b", 2, 1)):
                    if odd:
                        ac_did("OV")
                    else:
                        ve_did("RP")
                    for c in range(odd, NCH, 2):
                        cp, r = c // 2, slice(odd * CH, (odd + 1) * CH)
                        o = bank(k)[:, cp * P:(cp + 1) * P]
                        nc.tensor.matmul(o, b.BT[r, cp * P:(cp + 1) * P], b.GH[r, 1, 2 * cp:2 * cp + 2, :].rearrange("q s k -> q (s k)"), start=True, stop=False)
                        last = nc.tensor.matmul(o, b.KT[r, cp * P:(cp + 1) * P], b.VT[r, cp * P:(cp + 1) * P], start=False, stop=True)
                    did(f"N{half}", last)
                yield
                ve_did("Nb")
                for c in range(1, NCH - 1):
                    if c > 1:
                        ve_did(f"S{c - 1}")
                    did(f"S{c}", nc.tensor.matmul(bank((c + 1) % 2)[:, 0:P], b.MT[:, c, :], b.S[:, c - 1, :], start=True, stop=True))
                    yield
                ve_did(f"S{NCH - 2}")
                for c in range(1, NCH):
                    last = nc.tensor.matmul(bank(3)[:, c * CH:(c + 1) * CH], b.S[:, c - 1, :], b.RP[:, c * CH:(c + 1) * CH], start=True, stop=True)
                did("Y", last)
                yield
                ve_did("Y")
                did("mean", nc.tensor.matmul(bank(0), bones, b.y[:, :], start=True, stop=True))
                yield
                ac_did("sq")
                did("var", nc.tensor.matmul(bank(1), bones, b.ysq[:, :], start=True, stop=True))
                yield
                yield

            def out_block(m, k, start, stop):
                u = U_OUT + m
                if start:
                    after(lo_done, u + 1)
                    if m < RING:
                        after(sem("pool_lo"), m + 1)
                    else:
                        after(sem("x2_new"), m - 3)
                if m == 0:
                    after(*((sem("mix_lo"), k + 1) if k < PAIRS else (sem("pool_lo"), k - PAIRS + 1)))
                last = three(ps[:, m % 4, :], *blk(u % RING, k), act_hi[:, k, :], act_lo[:, k, :], start, stop)
                if stop:
                    last.then_inc(unit_used, 1)

            others = [k for k in range(KT) if k != PAIRS - 1]

            def closing():
                after(sem("pooled"), len(WINDOWS))
                pe.wait_ge(vector_step[0], at(VE_STEPS, PAIRS - 2, "out"))
                for g in range(len(WINDOWS)):
                    nc.tensor.matmul(ps[:, g, :], w_pool[:, g, :], pooled[:, g, :], start=True, stop=True).then_inc(sem("pool_mm"), 1)
                for _ in range(4):
                    yield
                n = 0
                for m in range(RING):
                    for k in others:
                        out_block(m, k, k == 0, False)
                        n += 1
                        if n < NCH - 1 or n % 5 == 0:
                            yield

            in_turns(pair, closing)

            for m in range(KT):
                if m >= RING:
                    for k in others:
                        out_block(m, k, k == 0, False)
                out_block(m, PAIRS - 1, False, True)
            after(sem("x2_new"), KT)
            ffn(2, U_UP2, U_DN2, sem("x2_lo"), lambda: stat(sem("x2_sum"), KT - 1, sem("x2_stat")))
            after(s2["x_new"], KT)
            stat(s2["nx_sum"], KT - 1, s2["stat"])


def _columns(a):
    return np.asarray(a).reshape(-1, P).T


def _by_output(w):
    return w.reshape(KT, P, -1, P).transpose(2, 1, 0, 3).reshape(-1, P, D)


def _tables():
    l = np.arange(T)
    cos_k, sin_k = np.arange(NCOS), np.arange(NSIN)
    cs = np.concatenate([np.cos(2 * np.pi * (np.outer(l, cos_k) % T) / T), np.sin(2 * np.pi * (np.outer(l, sin_k) % T) / T)], 1)
    cs[:, NCOS] = 0.0
    cs = cs.reshape(TT_, P, NF).transpose(1, 0, 2)
    c = np.arange(FG)
    ang = 2 * np.pi * (np.outer(c, c) % FG) / FG
    norm = 1.0 / np.sqrt(T * FG)
    chan = np.stack([np.cos(ang) * norm, np.sin(ang) * norm]).reshape(2, 2, P, 2, P).transpose(2, 0, 1, 3, 4).reshape(P, D)
    i = np.arange(P)
    inv = np.stack([1.0 / np.minimum(np.arange(PADW) + 1, w) for w in WINDOWS]).reshape(1, -1).repeat(P, 0)
    const = np.concatenate([np.eye(P), np.ones((P, P)), (i[:, None] // HS == i // HS) * 1.0, inv], 1)
    s, t = i[:, None], i[None, :]
    same = s // CH == t // CH
    strict, incl = same & (s < t), same & (s <= t)
    levels = [(t // b % 2 == 1) & (s // b == t // b - 1) for b in LEVELS]
    mask = np.concatenate([strict, strict, incl, incl] + levels + [s // HS == t // HS], 1)
    return [np.ascontiguousarray(a, dtype=np.float32) for a in (cs, chan, const, mask)]


def kernel(**inputs):
    import concourse.bacc as bacc
    from concourse.bass_utils import run_bass_kernel_spmd

    g = {k: np.asarray(a) for k, a in inputs.items()}
    cs, chan, const, mask = _tables()
    w_in = g["w_in_2"][0]
    mu = np.zeros(1600 + P, np.float32)
    mu[:g["mu_shift_2"].shape[1]] = g["mu_shift_2"][0]
    eps = np.full((P, 1), EPS, np.float32)
    vec = np.concatenate(
        [_columns(g["c"][0]), _columns(g["b_mod"][0]), _columns(g["g_norm_mix"][0]), _columns(g["g_norm_ffn"][0]),
         _columns(g["w_ffn_conv"][0]), _columns(g["b_ffn_conv"][0]), _columns(g["ffn1_norm_2"][0]), _columns(g["mix_norm_2"][0])]
        + [_columns(mu[s:s + P]) for s in IN_STARTS_RW]
        + [_columns(g[n][0]) for n in ("w0_2", "a0_2", "k_k_2", "k_a_2", "r_k_2", "ln_w_2", "ln_b_2", "pool_scale_2", "ffn2_norm_2")]
        + [_columns(g["g_final"]), _columns(g["final_norm_2"]), eps, np.full((P, 1), GN_EPS, np.float32)], 1)

    def gated(a, b):
        return np.stack([_by_output(a), _by_output(b)], 1).reshape(-1, P, D)

    up = g["w_ffn_up"][0]
    units = np.concatenate(
        [chan[None], _by_output(g["w_fnet_out"][0]), gated(up[:, :F], up[:, F:]), g["w_ffn_down"][0].reshape(FT, P, D),
         gated(g["ffn1_w_gate_2"][0], g["ffn1_w_up_2"][0]), g["ffn1_w_down_2"][0].reshape(FT, P, D)]
        + [_by_output(w_in[:, s:s + P]) for s in IN_STARTS]
        + [_by_output(g["w_out_2"][0]), gated(g["ffn2_w_gate_2"][0], g["ffn2_w_up_2"][0]), g["ffn2_w_down_2"][0].reshape(FT, P, D)])
    w_mod = g["w_mod"][0].reshape(KT, P, 6, D).transpose(2, 0, 1, 3).reshape(6 * KT, P, D)
    lora = np.zeros((P, 3, RW), np.float32)
    lora[0:32, 0] = g["w_lora_up_2"][0]
    lora[32:64, 1] = g["a_lora_up_2"][0]
    lora[0:96, 2] = g["g_lora_up_2"][0]
    x = g["x"][0]
    arrays = {
        "vectors": vec, "constants": const, "masks": mask, "tokens": x, "tokens_by_channel": x.T.reshape(KT, P, T).transpose(1, 0, 2),
        "seq_transform": cs, "mod_units": w_mod, "weight_units": units, "low_rank": lora,
        "pool_weights": g["w_pool_2"][0].transpose(1, 0, 2),
    }
    arrays = {k: np.ascontiguousarray(a) for k, a in arrays.items()}
    nc = bacc.Bacc("TRN2", target_bir_lowering=False, num_devices=1)
    args = [nc.dram_tensor(k, a.shape, mybir.dt.from_np(a.dtype), kind="ExternalInput").ap() for k, a in arrays.items()]
    result = nc.dram_tensor("result", (D, T), mybir.dt.float32, kind="ExternalOutput").ap()
    build(nc, *args, result)
    r = run_bass_kernel_spmd(nc, [arrays], core_ids=[0])
    return np.ascontiguousarray(r.results[0]["result"].T).reshape(1, T, D)
```
